# Optimizing a Trainium2 kernel written in Bass

```python
import math
import jax
import jax.numpy as jnp
from jax import lax
import numpy as np
import jax, jax.numpy as jnp

D_MODEL = 1024
BATCH = 1
SEQ = 256
DEPTH = 1

F32 = jnp.float32
EPS = 1e-6
PLE_DIM = 256

A_HEADS = 8
A_HEAD_DIM = 64
A_WIDTH = A_HEADS * A_HEAD_DIM
MOBA_BLOCK = 256
MOBA_TOPK = 3
MOBA_QCHUNK = 16

SSD_D_INNER = D_MODEL
SSD_HEAD_DIM = 64
SSD_HEADS = SSD_D_INNER // SSD_HEAD_DIM
SSD_GROUPS = 2
SSD_D_STATE = 128
SSD_CONV = 4
SSD_CHUNK = 256
SSD_CONV_DIM = SSD_D_INNER + 2 * SSD_GROUPS * SSD_D_STATE

MOE_GROUPS = 4
MOE_EXPERTS_PER_GROUP = 4
MOE_EXPERTS = MOE_GROUPS * MOE_EXPERTS_PER_GROUP
MOE_TOPK = 2
MOE_D_FF = 512

OFF_Q = 0
OFF_K = OFF_Q + A_WIDTH
OFF_V = OFF_K + A_WIDTH
OFF_Z = OFF_V + A_WIDTH
OFF_XBC = OFF_Z + SSD_D_INNER
OFF_DT = OFF_XBC + SSD_CONV_DIM
OFF_GA = OFF_DT + SSD_HEADS
OFF_GB = OFF_GA + D_MODEL
IN_DIM = OFF_GB + D_MODEL


def rms_norm(x, g):
    xf = x.astype(F32)
    y = xf * lax.rsqrt(jnp.mean(xf * xf, axis=-1, keepdims=True) + EPS)
    return (y * g.astype(F32)).astype(x.dtype)

def alibi_slopes(n):
    return 2.0 ** (-8.0 * jnp.arange(1, n + 1, dtype=F32) / n)

def moba_attention(q, k, v):
    bsz, s, nh, hd = q.shape
    nb = -(-s // MOBA_BLOCK)
    s_pad = nb * MOBA_BLOCK
    pad = ((0, 0), (0, s_pad - s), (0, 0), (0, 0))
    q, k, v = [jnp.pad(t, pad).transpose(0, 2, 1, 3) for t in (q, k, v)]
    scale = hd ** -0.5
    kb = k.reshape(bsz, nh, nb, MOBA_BLOCK, hd)
    vb = v.reshape(bsz, nh, nb, MOBA_BLOCK, hd)
    k_mean = jnp.mean(kb.astype(F32), axis=3)
    gate = jnp.einsum('bhtd,bhnd->bhtn', q.astype(F32), k_mean)
    q_blk = jnp.arange(s_pad) // MOBA_BLOCK
    past = jnp.arange(nb)[None, :] < q_blk[:, None]
    gate = jnp.where(past[None, None], gate, -jnp.inf)
    topk = min(MOBA_TOPK, nb)
    _, top_idx = lax.top_k(gate, topk)
    sel_valid = jnp.arange(topk)[None, :] < q_blk[:, None]
    slopes = alibi_slopes(nh)[None, :, None, None]
    bi = jnp.arange(bsz)[:, None, None, None]
    hi = jnp.arange(nh)[None, :, None, None]
    offs = jnp.arange(MOBA_BLOCK)
    n_chunks = s_pad // MOBA_QCHUNK

    def chunk(c):
        t0 = c * MOBA_QCHUNK
        qc = lax.dynamic_slice_in_dim(q, t0, MOBA_QCHUNK, axis=2)
        idx = lax.dynamic_slice_in_dim(top_idx, t0, MOBA_QCHUNK, axis=2)
        valid = lax.dynamic_slice_in_dim(sel_valid, t0, MOBA_QCHUNK, axis=0)
        t = t0 + jnp.arange(MOBA_QCHUNK)
        kg = kb[bi, hi, idx]
        vg = vb[bi, hi, idx]
        s_sel = jnp.einsum('bhqd,bhqkld->bhqkl', qc, kg, preferred_element_type=F32) * scale
        kpos = idx[..., None] * MOBA_BLOCK + offs
        s_sel = s_sel - slopes[..., None] * (t[:, None, None] - kpos).astype(F32)
        s_sel = jnp.where(valid[:, :, None], s_sel, -jnp.inf)
        blk0 = (t0 // MOBA_BLOCK) * MOBA_BLOCK
        ko = lax.dynamic_slice_in_dim(k, blk0, MOBA_BLOCK, axis=2)
        vo = lax.dynamic_slice_in_dim(v, blk0, MOBA_BLOCK, axis=2)
        s_own = jnp.einsum('bhqd,bhld->bhql', qc, ko, preferred_element_type=F32) * scale
        dist = t[:, None] - (blk0 + offs)[None, :]
        s_own = jnp.where(dist >= 0, s_own - slopes * dist.astype(F32), -jnp.inf)
        sc = jnp.concatenate([s_sel.reshape(bsz, nh, MOBA_QCHUNK, topk * MOBA_BLOCK), s_own], axis=-1)
        pr = jax.nn.softmax(sc, axis=-1).astype(v.dtype)
        p_sel = pr[..., :topk * MOBA_BLOCK].reshape(bsz, nh, MOBA_QCHUNK, topk, MOBA_BLOCK)
        p_own = pr[..., topk * MOBA_BLOCK:]
        return (jnp.einsum('bhqkl,bhqkld->bhqd', p_sel, vg)
                + jnp.einsum('bhql,bhld->bhqd', p_own, vo))

    out = lax.map(chunk, jnp.arange(n_chunks))
    out = out.transpose(1, 2, 0, 3, 4).reshape(bsz, nh, s_pad, hd)[:, :, :s]
    return out.transpose(0, 2, 1, 3)

def causal_depthwise_conv(u, w, b):
    c = u.shape[-1]
    out = lax.conv_general_dilated(u, w[:, None, :].astype(u.dtype), window_strides=(1,),
                                   padding=[(SSD_CONV - 1, 0)],
                                   dimension_numbers=('NWC', 'WIO', 'NWC'),
                                   feature_group_count=c)
    return out + b

def segsum(a):
    tlen = a.shape[-1]
    cs = jnp.cumsum(a, axis=-1)
    diff = cs[..., :, None] - cs[..., None, :]
    mask = jnp.tril(jnp.ones((tlen, tlen), dtype=bool))
    return jnp.where(mask, diff, -jnp.inf)

def ssd_chunked_scan(x, dt, a, b_in, c_in):
    bsz, s, nh, hp = x.shape
    ng, ns = b_in.shape[2], b_in.shape[3]
    hpg = nh // ng
    nc = -(-s // SSD_CHUNK)
    sp = nc * SSD_CHUNK

    def padt(t):
        return jnp.pad(t.astype(F32), [(0, 0), (0, sp - s)] + [(0, 0)] * (t.ndim - 2))

    x, dt, b_in, c_in = padt(x), padt(dt), padt(b_in), padt(c_in)
    xdt = (x * dt[..., None]).reshape(bsz, nc, SSD_CHUNK, ng, hpg, hp)
    da = (dt * a.astype(F32)).reshape(bsz, nc, SSD_CHUNK, ng, hpg).transpose(0, 3, 4, 1, 2)
    bc = b_in.reshape(bsz, nc, SSD_CHUNK, ng, ns)
    cc = c_in.reshape(bsz, nc, SSD_CHUNK, ng, ns)
    da_cs = jnp.cumsum(da, axis=-1)
    decay_in = jnp.exp(segsum(da))
    cb = jnp.einsum('bclgn,bcsgn->bgcls', cc, bc)
    y_diag = jnp.einsum('bgcls,bgjcls,bcsgjp->bclgjp', cb, decay_in, xdt)
    decay_to_end = jnp.exp(da_cs[..., -1:] - da_cs)
    chunk_states = jnp.einsum('bclgn,bgjcl,bclgjp->cbgjpn', bc, decay_to_end, xdt)
    chunk_decay = jnp.exp(da_cs[..., -1]).transpose(3, 0, 1, 2)

    def carry_state(h, inp):
        st, dec = inp
        return h * dec[..., None, None] + st, h

    h0 = jnp.zeros(chunk_states.shape[1:], F32)
    _, h_in = lax.scan(carry_state, h0, (chunk_states, chunk_decay))
    y_off = jnp.einsum('bclgn,cbgjpn,bgjcl->bclgjp', cc, h_in, jnp.exp(da_cs))
    return (y_diag + y_off).reshape(bsz, sp, nh, hp)[:, :s]

def ssd_mixer(z, xbc, dt_raw, conv_w, conv_b, dt_bias, a_log, d_skip, norm_g):
    bsz, s, _ = z.shape
    xbc = jax.nn.silu(causal_depthwise_conv(xbc, conv_w, conv_b))
    xs = xbc[..., :SSD_D_INNER].reshape(bsz, s, SSD_HEADS, SSD_HEAD_DIM)
    gs = SSD_GROUPS * SSD_D_STATE
    b_in = xbc[..., SSD_D_INNER:SSD_D_INNER + gs].reshape(bsz, s, SSD_GROUPS, SSD_D_STATE)
    c_in = xbc[..., SSD_D_INNER + gs:].reshape(bsz, s, SSD_GROUPS, SSD_D_STATE)
    dt = jax.nn.softplus(dt_raw.astype(F32) + dt_bias.astype(F32))
    a = -jnp.exp(a_log.astype(F32))
    y = ssd_chunked_scan(xs, dt, a, b_in, c_in)
    y = y + d_skip.astype(F32)[:, None] * xs.astype(F32)
    u = (y.reshape(bsz, s, SSD_D_INNER) * jax.nn.silu(z.astype(F32)))
    u = u.reshape(bsz, s, SSD_GROUPS, SSD_D_INNER // SSD_GROUPS)
    u = u * lax.rsqrt(jnp.mean(u * u, axis=-1, keepdims=True) + EPS)
    return (u.reshape(bsz, s, SSD_D_INNER) * norm_g.astype(F32)).astype(z.dtype)

def hier_moe(h, w_rg, b_rg, w_re, b_re, w_gate, w_up, w_down):
    bsz, s, _ = h.shape
    hf = h.astype(F32)
    g_logits = hf @ w_rg.astype(F32) + b_rg.astype(F32)
    g_prob = jax.nn.softmax(g_logits, axis=-1)
    g_pw, g_sel = lax.top_k(g_prob, 1)
    e_logits = (hf @ w_re.astype(F32) + b_re.astype(F32)).reshape(bsz, s, MOE_GROUPS, MOE_EXPERTS_PER_GROUP)
    e_in_group = jnp.take_along_axis(e_logits, g_sel[..., None], axis=2)[:, :, 0]
    e_val, e_idx = lax.top_k(e_in_group, MOE_TOPK)
    e_w = jax.nn.softmax(e_val, axis=-1) * g_pw
    expert_id = g_sel * MOE_EXPERTS_PER_GROUP + e_idx
    combine = jnp.sum(jax.nn.one_hot(expert_id, MOE_EXPERTS, dtype=F32) * e_w[..., None], axis=-2)
    out = jnp.zeros_like(h)
    for e in range(MOE_EXPERTS):
        he = jax.nn.silu(h @ w_gate[e]) * (h @ w_up[e])
        out = out + combine[..., e:e + 1].astype(h.dtype) * (he @ w_down[e])
    return out

def first_inputs(seed: int = 0) -> dict:
    key = jax.random.key(seed)
    ks = jax.random.split(key, 24)
    nrm = jax.random.normal

    def gain(k, n):
        return 1.0 + 0.02 * nrm(k, (DEPTH, n), F32)

    dt0 = jnp.exp(jax.random.uniform(ks[6], (DEPTH, SSD_HEADS), F32)
                  * (math.log(0.1) - math.log(1e-3)) + math.log(1e-3))
    return {
        'x': nrm(ks[0], (BATCH, SEQ, D_MODEL), F32),
        'p': nrm(ks[1], (DEPTH, BATCH, SEQ, PLE_DIM), F32),
        'mix_norm_g': gain(ks[2], D_MODEL),
        'w_in': nrm(ks[3], (DEPTH, D_MODEL, IN_DIM), F32) * D_MODEL ** -0.5,
        'conv_w': nrm(ks[4], (DEPTH, SSD_CONV, SSD_CONV_DIM), F32) * SSD_CONV ** -0.5,
        'conv_b': 0.02 * nrm(ks[5], (DEPTH, SSD_CONV_DIM), F32),
        'dt_bias': dt0 + jnp.log(-jnp.expm1(-dt0)),
        'a_log': jnp.log(jax.random.uniform(ks[7], (DEPTH, SSD_HEADS), F32, minval=1.0, maxval=16.0)),
        'd_skip': gain(ks[8], SSD_HEADS),
        'ssd_norm_g': gain(ks[9], SSD_D_INNER),
        'w_out_a': nrm(ks[10], (DEPTH, A_WIDTH, D_MODEL), F32) * A_WIDTH ** -0.5,
        'w_out_b': nrm(ks[11], (DEPTH, SSD_D_INNER, D_MODEL), F32) * SSD_D_INNER ** -0.5,
        'w_out': nrm(ks[12], (DEPTH, D_MODEL, D_MODEL), F32) * D_MODEL ** -0.5,
        'ffn_norm_g': gain(ks[13], D_MODEL),
        'w_rg': nrm(ks[14], (DEPTH, D_MODEL, MOE_GROUPS), F32) * D_MODEL ** -0.5,
        'b_rg': 0.01 * nrm(ks[15], (DEPTH, MOE_GROUPS), F32),
        'w_re': nrm(ks[16], (DEPTH, D_MODEL, MOE_EXPERTS), F32) * D_MODEL ** -0.5,
        'b_re': 0.01 * nrm(ks[17], (DEPTH, MOE_EXPERTS), F32),
        'w_gate': nrm(ks[18], (DEPTH, MOE_EXPERTS, D_MODEL, MOE_D_FF), F32) * D_MODEL ** -0.5,
        'w_up': nrm(ks[19], (DEPTH, MOE_EXPERTS, D_MODEL, MOE_D_FF), F32) * D_MODEL ** -0.5,
        'w_down': nrm(ks[20], (DEPTH, MOE_EXPERTS, MOE_D_FF, D_MODEL), F32) * MOE_D_FF ** -0.5,
        'w_ple_proj': nrm(ks[21], (DEPTH, PLE_DIM, D_MODEL), F32) * PLE_DIM ** -0.5,
        'w_ple_gate': nrm(ks[22], (DEPTH, D_MODEL, D_MODEL), F32) * D_MODEL ** -0.5,
        'final_norm_g': 1.0 + 0.02 * nrm(ks[23], (D_MODEL,), F32),
    }

def first_block(x, p, mix_norm_g, w_in, conv_w, conv_b, dt_bias, a_log, d_skip, ssd_norm_g,
              w_out_a, w_out_b, w_out, ffn_norm_g, w_rg, b_rg, w_re, b_re, w_gate, w_up,
              w_down, w_ple_proj, w_ple_gate, final_norm_g):
    bsz, s, _ = x.shape
    for i in range(DEPTH):
        h = rms_norm(x, mix_norm_g[i])
        proj = h @ w_in[i]
        q = proj[..., OFF_Q:OFF_K].reshape(bsz, s, A_HEADS, A_HEAD_DIM)
        k = proj[..., OFF_K:OFF_V].reshape(bsz, s, A_HEADS, A_HEAD_DIM)
        v = proj[..., OFF_V:OFF_Z].reshape(bsz, s, A_HEADS, A_HEAD_DIM)
        z = proj[..., OFF_Z:OFF_XBC]
        xbc = proj[..., OFF_XBC:OFF_DT]
        dt_raw = proj[..., OFF_DT:OFF_GA]
        gate_a = jax.nn.sigmoid(proj[..., OFF_GA:OFF_GB])
        gate_b = jax.nn.sigmoid(proj[..., OFF_GB:IN_DIM])
        y_a = moba_attention(q, k, v).reshape(bsz, s, A_WIDTH) @ w_out_a[i]
        y_b = ssd_mixer(z, xbc, dt_raw, conv_w[i], conv_b[i], dt_bias[i], a_log[i],
                        d_skip[i], ssd_norm_g[i]) @ w_out_b[i]
        x = x + (gate_a * y_a + gate_b * y_b) @ w_out[i]
        h2 = rms_norm(x, ffn_norm_g[i])
        x = x + hier_moe(h2, w_rg[i], b_rg[i], w_re[i], b_re[i], w_gate[i], w_up[i], w_down[i])
        x = x + jax.nn.sigmoid(x @ w_ple_gate[i]) * (p[i] @ w_ple_proj[i])
    return rms_norm(x, final_norm_g)


HEAD_DIM = 64
QBLOCK = 128
EPS_2 = 1e-5
SWA_HEADS = 8
SWA_KV_HEADS = 2
SWA_WINDOW = 128
DIFF_HEADS = 4
NSA_HEADS = 8
NSA_KV_HEADS = 2
CMP_BLOCK = 32
CMP_STRIDE = 16
CMP_HIDDEN = 256
SEL_BLOCK = 64
SEL_TOPN = 16
SEL_QCHUNK = 32
NSA_WINDOW = 512
BRANCH_WIDTH = 512
N_BRANCHES = 3
N_EXPERTS = 32
TOP_K = 4
D_EXPERT = D_MODEL
SWIGLU_LIMIT = 7.0
SWIGLU_ALPHA = 1.702
MOE_BLOCK = 128
A_Q = SWA_HEADS * HEAD_DIM
A_KV = SWA_KV_HEADS * HEAD_DIM
B_QK = DIFF_HEADS * 2 * HEAD_DIM
B_V = DIFF_HEADS * 2 * HEAD_DIM
C_Q = NSA_HEADS * HEAD_DIM
C_KV = NSA_KV_HEADS * HEAD_DIM
NSA_GATES = NSA_HEADS * 3
MERGE_GATES = N_BRANCHES * D_MODEL
IN_SPLITS = (A_Q, A_KV, A_KV, B_QK, B_QK, B_V, C_Q, C_KV, C_KV, C_KV, C_KV, C_KV, C_KV, NSA_GATES, MERGE_GATES)
IN_WIDTH = sum(IN_SPLITS)


def rms_norm_2(x, g):
    xf = x.astype(jnp.float32)
    y = xf * lax.rsqrt(jnp.mean(xf * xf, axis=-1, keepdims=True) + EPS_2)
    return (y * g.astype(jnp.float32)).astype(x.dtype)

def alibi_slopes_2(n):
    return 2.0 ** (-8.0 * jnp.arange(1, n + 1, dtype=jnp.float32) / n)

def banded_attention(q, k, v, window, slopes, sinks=None):
    B, S, Hkv, G, d = q.shape
    nb = S // QBLOCK
    n_prev = -(-(window - 1) // QBLOCK)
    ctx = (n_prev + 1) * QBLOCK
    pad = ((0, 0), (n_prev * QBLOCK, 0), (0, 0), (0, 0))
    kp = jnp.pad(k, pad)
    vp = jnp.pad(v, pad)
    qb = q.reshape(B, nb, QBLOCK, Hkv, G, d).swapaxes(0, 1)
    scale = d ** -0.5

    def block(args):
        qi, i = args
        start = i * QBLOCK
        kc = lax.dynamic_slice_in_dim(kp, start, ctx, axis=1)
        vc = lax.dynamic_slice_in_dim(vp, start, ctx, axis=1)
        s = jnp.einsum('bqhgd,bkhd->bhgqk', qi, kc).astype(jnp.float32) * scale
        t = start + jnp.arange(QBLOCK)
        pos = start - n_prev * QBLOCK + jnp.arange(ctx)
        dist = t[:, None] - pos[None, :]
        valid = (dist >= 0) & (dist < window) & (pos[None, :] >= 0)
        s = s - slopes[:, :, None, None] * dist.astype(jnp.float32)
        s = jnp.where(valid, s, -jnp.inf)
        if sinks is None:
            p = jax.nn.softmax(s, axis=-1)
        else:
            lse = jnp.logaddexp(jax.nn.logsumexp(s, axis=-1, keepdims=True), sinks[:, :, None, None])
            p = jnp.exp(s - lse)
        return jnp.einsum('bhgqk,bkhd->bqhgd', p.astype(vc.dtype), vc)

    o = lax.map(block, (qb, jnp.arange(nb)))
    return o.swapaxes(0, 1).reshape(B, S, Hkv, G, d)

def diff_attention(q, k, v, lam_params, subln_g, slopes, lam_init):
    B, S, H, _, d = q.shape
    nb = S // QBLOCK
    lp = lam_params.astype(jnp.float32)
    lam = jnp.exp(jnp.sum(lp[0] * lp[1])) - jnp.exp(jnp.sum(lp[2] * lp[3])) + lam_init
    qb = q.reshape(B, nb, QBLOCK, H, 2, d).swapaxes(0, 1)
    kpos = jnp.arange(S)
    scale = d ** -0.5

    def block(args):
        qi, i = args
        s = jnp.einsum('bqhcd,bkhcd->bhcqk', qi, k).astype(jnp.float32) * scale
        t = i * QBLOCK + jnp.arange(QBLOCK)
        dist = t[:, None] - kpos[None, :]
        s = s - slopes[:, None, None, None] * dist.astype(jnp.float32)
        s = jnp.where(dist >= 0, s, -jnp.inf)
        p = jax.nn.softmax(s, axis=-1)
        w = p[:, :, 0] - lam * p[:, :, 1]
        return jnp.einsum('bhqk,bkhe->bqhe', w.astype(v.dtype), v)

    o = lax.map(block, (qb, jnp.arange(nb)))
    o = o.swapaxes(0, 1).reshape(B, S, H, 2 * d)
    return rms_norm_2(o, subln_g) * (1.0 - lam_init)

def compress_blocks(x, pos, w1, b1, w2, b2):
    B, S, Hkv, d = x.shape
    nc = (S - CMP_BLOCK) // CMP_STRIDE + 1
    idx = jnp.arange(nc)[:, None] * CMP_STRIDE + jnp.arange(CMP_BLOCK)[None, :]
    blk = x[:, idx] + pos[:, None, :]
    blk = blk.transpose(0, 1, 3, 2, 4).reshape(B, nc, Hkv, CMP_BLOCK * d)
    hid = jax.nn.gelu(blk @ w1 + b1)
    return hid @ w2 + b2

def nsa_attention(q, k_cmp, v_cmp, k_slc, v_slc, k_win, v_win, gates, cmp_pos, cmp_w1, cmp_b1, cmp_w2, cmp_b2, slopes):
    B, S, Hkv, G, d = q.shape
    scale = d ** -0.5
    t = jnp.arange(S)
    kc = compress_blocks(k_cmp, cmp_pos[0], cmp_w1[0], cmp_b1[0], cmp_w2[0], cmp_b2[0])
    vc = compress_blocks(v_cmp, cmp_pos[1], cmp_w1[1], cmp_b1[1], cmp_w2[1], cmp_b2[1])
    nc = kc.shape[1]
    cstart = jnp.arange(nc) * CMP_STRIDE
    cvalid = (cstart[None, :] + CMP_BLOCK - 1) <= t[:, None]
    s = jnp.einsum('bqhgd,bchd->bhgqc', q, kc).astype(jnp.float32) * scale
    p_cmp = jax.nn.softmax(jnp.where(cvalid, s, -1e30), axis=-1) * cvalid
    o_cmp = jnp.einsum('bhgqc,bchd->bqhgd', p_cmp.astype(vc.dtype), vc)
    nsb = S // SEL_BLOCK
    sstart = jnp.arange(nsb) * SEL_BLOCK
    overlap = jnp.clip(jnp.minimum(cstart[:, None] + CMP_BLOCK, sstart[None, :] + SEL_BLOCK)
                       - jnp.maximum(cstart[:, None], sstart[None, :]), 0).astype(jnp.float32) / CMP_BLOCK
    imp = jnp.einsum('bhgqc,cn->bhqn', p_cmp, overlap)
    cur = t // SEL_BLOCK
    blk = jnp.arange(nsb)
    causal_blk = blk[None, :] <= cur[:, None]
    forced = (blk[None, :] == 0) | (blk[None, :] == cur[:, None]) | (blk[None, :] == cur[:, None] - 1)
    score = jnp.where(forced, jnp.inf, jnp.where(causal_blk, imp, -jnp.inf))
    n_sel = min(SEL_TOPN, nsb)
    top_s, top_i = lax.top_k(score, n_sel)
    sel_ok = top_s > -jnp.inf
    kb = k_slc.reshape(B, nsb, SEL_BLOCK, Hkv, d).transpose(0, 3, 1, 2, 4)
    vb = v_slc.reshape(B, nsb, SEL_BLOCK, Hkv, d).transpose(0, 3, 1, 2, 4)
    nq = S // SEL_QCHUNK
    qch = q.reshape(B, nq, SEL_QCHUNK, Hkv, G, d).swapaxes(0, 1)
    ich = top_i.reshape(B, Hkv, nq, SEL_QCHUNK, n_sel).transpose(2, 0, 1, 3, 4)
    och = sel_ok.reshape(B, Hkv, nq, SEL_QCHUNK, n_sel).transpose(2, 0, 1, 3, 4)
    bidx = jnp.arange(B)[:, None, None, None]
    hidx = jnp.arange(Hkv)[None, :, None, None]

    def chunk(args):
        qi, ii, oki, cidx = args
        kg = kb[bidx, hidx, ii]
        vg = vb[bidx, hidx, ii]
        sc = jnp.einsum('bqhgd,bhqnld->bhgqnl', qi, kg).astype(jnp.float32) * scale
        tq = cidx * SEL_QCHUNK + jnp.arange(SEL_QCHUNK)
        kpos = ii[..., None] * SEL_BLOCK + jnp.arange(SEL_BLOCK)
        dist = tq[None, None, :, None, None] - kpos
        ok = (dist >= 0) & oki[..., None]
        sc = sc - slopes[None, :, :, None, None, None] * dist[:, :, None].astype(jnp.float32)
        sc = jnp.where(ok[:, :, None], sc, -jnp.inf)
        shp = sc.shape
        pr = jax.nn.softmax(sc.reshape(shp[:4] + (shp[4] * shp[5],)), axis=-1).reshape(shp)
        return jnp.einsum('bhgqnl,bhqnld->bqhgd', pr.astype(vg.dtype), vg)

    o_slc = lax.map(chunk, (qch, ich, och, jnp.arange(nq)))
    o_slc = o_slc.swapaxes(0, 1).reshape(B, S, Hkv, G, d)
    o_win = banded_attention(q, k_win, v_win, NSA_WINDOW, slopes)
    g = jax.nn.sigmoid(gates)
    return g[..., 0:1] * o_cmp + g[..., 1:2] * o_slc + g[..., 2:3] * o_win

def hybrid_mixer(h, w_in, b_in, sinks, diff_lambda, diff_subln_g, cmp_pos, cmp_w1, cmp_b1, cmp_w2, cmp_b2, w_branch, w_out, lam_init):
    B, S, _ = h.shape
    z = h @ w_in + b_in
    offs = np.cumsum(IN_SPLITS)[:-1].tolist()
    (qa, ka, va, qb, kb, vb, qc, kcm, vcm, ksl, vsl, kwn, vwn, g_nsa, g_merge) = jnp.split(z, offs, axis=-1)
    ga = SWA_HEADS // SWA_KV_HEADS
    o_a = banded_attention(qa.reshape(B, S, SWA_KV_HEADS, ga, HEAD_DIM),
                           ka.reshape(B, S, SWA_KV_HEADS, HEAD_DIM), va.reshape(B, S, SWA_KV_HEADS, HEAD_DIM),
                           SWA_WINDOW, alibi_slopes_2(SWA_HEADS).reshape(SWA_KV_HEADS, ga),
                           sinks.astype(jnp.float32).reshape(SWA_KV_HEADS, ga)).reshape(B, S, BRANCH_WIDTH)
    o_b = diff_attention(qb.reshape(B, S, DIFF_HEADS, 2, HEAD_DIM), kb.reshape(B, S, DIFF_HEADS, 2, HEAD_DIM),
                         vb.reshape(B, S, DIFF_HEADS, 2 * HEAD_DIM), diff_lambda, diff_subln_g,
                         alibi_slopes_2(DIFF_HEADS), lam_init).reshape(B, S, BRANCH_WIDTH)
    gc = NSA_HEADS // NSA_KV_HEADS
    kv = lambda a: a.reshape(B, S, NSA_KV_HEADS, HEAD_DIM)
    o_c = nsa_attention(qc.reshape(B, S, NSA_KV_HEADS, gc, HEAD_DIM), kv(kcm), kv(vcm), kv(ksl), kv(vsl), kv(kwn), kv(vwn),
                        g_nsa.reshape(B, S, NSA_KV_HEADS, gc, 3), cmp_pos, cmp_w1, cmp_b1, cmp_w2, cmp_b2,
                        alibi_slopes_2(NSA_HEADS).reshape(NSA_KV_HEADS, gc)).reshape(B, S, BRANCH_WIDTH)
    gm = jax.nn.sigmoid(g_merge.reshape(B, S, N_BRANCHES, D_MODEL))
    merged = gm[:, :, 0] * (o_a @ w_branch[0]) + gm[:, :, 1] * (o_b @ w_branch[1]) + gm[:, :, 2] * (o_c @ w_branch[2])
    return merged @ w_out

def moe_ffn(h, router_w, router_b, w1, b1, w2, b2):
    B, S, D = h.shape
    N = B * S
    xt = h.reshape(N, D)
    logits = (xt @ router_w + router_b).astype(jnp.float32)
    top_v, top_e = lax.top_k(logits, TOP_K)
    gate = jax.nn.softmax(top_v, axis=-1)
    A = N * TOP_K
    e_flat = top_e.reshape(A)
    order = jnp.argsort(e_flat)
    e_sorted = e_flat[order]
    tok_sorted = order // TOP_K
    g_sorted = gate.reshape(A)[order]
    counts = jnp.bincount(e_flat, length=N_EXPERTS)
    group_start = jnp.cumsum(counts) - counts
    padded = (counts + MOE_BLOCK - 1) // MOE_BLOCK * MOE_BLOCK
    pad_end = jnp.cumsum(padded)
    pad_start = pad_end - padded
    dest = pad_start[e_sorted] + (jnp.arange(A) - group_start[e_sorted])
    n_blocks = -(-A // MOE_BLOCK) + N_EXPERTS
    P = n_blocks * MOE_BLOCK
    row_tok = jnp.zeros((P,), jnp.int32).at[dest].set(tok_sorted.astype(jnp.int32))
    row_w = jnp.zeros((P,), jnp.float32).at[dest].set(g_sorted)
    block_expert = jnp.clip(jnp.searchsorted(pad_end, jnp.arange(n_blocks) * MOE_BLOCK, side='right'), 0, N_EXPERTS - 1)

    def expert_block(args):
        rows, e = args
        xb = xt[rows]
        hb = xb @ w1[e] + b1[e]
        g, u = hb[:, :D_EXPERT], hb[:, D_EXPERT:]
        g = jnp.minimum(g, SWIGLU_LIMIT)
        u = jnp.clip(u, -SWIGLU_LIMIT, SWIGLU_LIMIT)
        glu = g * jax.nn.sigmoid(g * SWIGLU_ALPHA)
        return ((u + 1.0) * glu) @ w2[e] + b2[e]

    y = lax.map(expert_block, (row_tok.reshape(n_blocks, MOE_BLOCK), block_expert)).reshape(P, D)
    out = jnp.zeros((N, D), y.dtype).at[row_tok].add(y * row_w[:, None].astype(y.dtype))
    return out.reshape(B, S, D)

def second_inputs(seed: int = 0) -> dict:
    key = jax.random.key(seed)
    ks = jax.random.split(key, 32)
    L, D, E, F = DEPTH, D_MODEL, N_EXPERTS, D_EXPERT
    nrm = lambda k, shape, s: jax.random.normal(k, shape, jnp.float32) * s
    return {
        'x': nrm(ks[0], (BATCH, SEQ, D), 1.0),
        'c': nrm(ks[1], (BATCH, D), 1.0),
        'mod_w': nrm(ks[2], (L, D, 6 * D), 0.5 * D ** -0.5),
        'mod_b': nrm(ks[3], (L, 6 * D), 0.02),
        'norm1_g': 1.0 + nrm(ks[4], (L, D), 0.1),
        'norm2_g': 1.0 + nrm(ks[5], (L, D), 0.1),
        'w_in': nrm(ks[6], (L, D, IN_WIDTH), D ** -0.5),
        'b_in': nrm(ks[7], (L, IN_WIDTH), 0.02),
        'sinks': nrm(ks[8], (L, SWA_HEADS), 0.5),
        'diff_lambda': nrm(ks[9], (L, 4, HEAD_DIM), 0.1),
        'diff_subln_g': 1.0 + nrm(ks[10], (L, 2 * HEAD_DIM), 0.1),
        'cmp_pos': nrm(ks[11], (L, 2, CMP_BLOCK, HEAD_DIM), 0.1),
        'cmp_w1': nrm(ks[12], (L, 2, CMP_BLOCK * HEAD_DIM, CMP_HIDDEN), (CMP_BLOCK * HEAD_DIM) ** -0.5),
        'cmp_b1': nrm(ks[13], (L, 2, CMP_HIDDEN), 0.02),
        'cmp_w2': nrm(ks[14], (L, 2, CMP_HIDDEN, HEAD_DIM), CMP_HIDDEN ** -0.5),
        'cmp_b2': nrm(ks[15], (L, 2, HEAD_DIM), 0.02),
        'w_branch': nrm(ks[16], (L, N_BRANCHES, BRANCH_WIDTH, D), BRANCH_WIDTH ** -0.5),
        'w_out': nrm(ks[17], (L, D, D), D ** -0.5),
        'router_w': nrm(ks[18], (L, D, E), D ** -0.5),
        'router_b': nrm(ks[19], (L, E), 0.01),
        'exp_w1': nrm(ks[20], (L, E, D, 2 * F), D ** -0.5),
        'exp_b1': nrm(ks[21], (L, E, 2 * F), 0.02),
        'exp_w2': nrm(ks[22], (L, E, F, D), F ** -0.5),
        'exp_b2': nrm(ks[23], (L, E, D), 0.02),
        'final_g': 1.0 + nrm(ks[24], (D,), 0.1),
    }

def second_block(x, c, mod_w, mod_b, norm1_g, norm2_g, w_in, b_in, sinks, diff_lambda, diff_subln_g, cmp_pos, cmp_w1, cmp_b1, cmp_w2, cmp_b2, w_branch, w_out, router_w, router_b, exp_w1, exp_b1, exp_w2, exp_b2, final_g):
    cs = jax.nn.silu(c)
    for l in range(DEPTH):
        mod = cs @ mod_w[l] + mod_b[l]
        sh1, sc1, g1, sh2, sc2, g2 = [m[:, None, :] for m in jnp.split(mod, 6, axis=-1)]
        lam_init = 0.8 - 0.6 * math.exp(-0.3 * l)
        h = rms_norm_2(x, norm1_g[l]) * (1.0 + sc1) + sh1
        x = x + g1 * hybrid_mixer(h, w_in[l], b_in[l], sinks[l], diff_lambda[l], diff_subln_g[l], cmp_pos[l], cmp_w1[l],
                                  cmp_b1[l], cmp_w2[l], cmp_b2[l], w_branch[l], w_out[l], lam_init)
        h = rms_norm_2(x, norm2_g[l]) * (1.0 + sc2) + sh2
        x = x + g2 * moe_ffn(h, router_w[l], router_b[l], exp_w1[l], exp_b1[l], exp_w2[l], exp_b2[l])
    return rms_norm_2(x, final_g)


def setup_inputs(seed=0):
    out = dict(first_inputs(seed))
    for name, value in second_inputs(seed + 1).items():
        if name != "x":
            out[name + "_2"] = value
    return out


def reference(
    x, p, mix_norm_g, w_in, conv_w, conv_b, dt_bias, a_log, d_skip, ssd_norm_g, w_out_a,
    w_out_b, w_out, ffn_norm_g, w_rg, b_rg, w_re, b_re, w_gate, w_up, w_down, w_ple_proj,
    w_ple_gate, final_norm_g, c_2, mod_w_2, mod_b_2, norm1_g_2, norm2_g_2, w_in_2, b_in_2,
    sinks_2, diff_lambda_2, diff_subln_g_2, cmp_pos_2, cmp_w1_2, cmp_b1_2, cmp_w2_2, cmp_b2_2,
    w_branch_2, w_out_2, router_w_2, router_b_2, exp_w1_2, exp_b1_2, exp_w2_2, exp_b2_2,
    final_g_2,
):
    x = first_block(
        x, p, mix_norm_g, w_in, conv_w, conv_b, dt_bias, a_log, d_skip, ssd_norm_g, w_out_a,
        w_out_b, w_out, ffn_norm_g, w_rg, b_rg, w_re, b_re, w_gate, w_up, w_down, w_ple_proj,
        w_ple_gate, final_norm_g,
    )
    return second_block(
        x, c_2, mod_w_2, mod_b_2, norm1_g_2, norm2_g_2, w_in_2, b_in_2, sinks_2, diff_lambda_2,
        diff_subln_g_2, cmp_pos_2, cmp_w1_2, cmp_b1_2, cmp_w2_2, cmp_b2_2, w_branch_2, w_out_2,
        router_w_2, router_b_2, exp_w1_2, exp_b1_2, exp_w2_2, exp_b2_2, final_g_2,
    )


_drawn_inputs = setup_inputs


def setup_inputs(seed=0):
    import zlib

    import numpy as np

    out = dict(_drawn_inputs(seed))
    spreads = {}
    factors = {'d_skip': 3.87,
     'ssd_norm_g': 2.725,
     'b_rg': 64.0,
     'b_re': 7.096,
     'b_in_2': 4.597,
     'sinks_2': 6.363,
     'diff_lambda_2': 5.271,
     'diff_subln_g_2': 2.838,
     'cmp_pos_2': 8.0,
     'cmp_b1_2': 40.077,
     'cmp_b2_2': 31.769,
     'router_b_2': 5.079,
     'exp_b1_2': 8.0,
     'exp_b2_2': 8.0,
     'ffn_norm_g': 3.987}
    for name, (base, spread) in spreads.items():
        noise = np.random.default_rng([zlib.crc32(name.encode()), seed]).standard_normal(out[name].shape)
        drawn = base * np.exp(spread * noise) if base else spread * noise
        out[name] = jnp.asarray(drawn.astype(out[name].dtype))
    for name, factor in factors.items():
        out[name] = (out[name] * factor).astype(out[name].dtype)
    return out
```

```python
from contextlib import ExitStack

import numpy as np

P = 128
T = 256
NT = T // P
D = 1024
KD = D // P
RING = 6
SLOT = 4096
BIG = 1e30
R_BIG = 12580


def layouts():
    w1 = dict(q=0, k=512, v=1024, z=1536, xbc=2560, dt=4096, ga=4112, gb=5136)
    w2 = dict(qa=0, kva=512, qb=768, kb=1280, vb=1792, qc=2304, kvc=2816, kvw=3328, gn=3584, gm=3608)
    return w1, w2


def build(nc, a):
    import concourse.bass as bass
    from concourse import mybir
    from concourse.alu_op_type import AluOpType as ALU

    F32 = mybir.dt.float32
    U32 = mybir.dt.uint32
    ACT = mybir.ActivationFunctionType
    AX = mybir.AxisListType
    W1, W2 = layouts()
    NE1, NE2 = 16, 32
    ctx = ExitStack()
    with ctx:
        sems = {}

        def sem(name):
            if name not in sems:
                sems[name] = ctx.enter_context(nc.semaphore(name))
            return sems[name]

        def sb(name, cols, dt=F32, parts=P):
            return ctx.enter_context(nc.sbuf_tensor(name, [parts, cols], dt))[:, :]

        ring = sb("ring", RING * SLOT)
        X = sb("x_resid", NT * D).rearrange("p (t n) -> p t n", t=NT)
        XT = sb("x_T", KD * T).rearrange("p (k t) -> p k t", k=KD)
        r_mix = sb("r_mix", 2048)
        XN = r_mix.rearrange("p (t n) -> p t n", t=NT)
        SC = r_mix.rearrange("p (b h k) -> p b h k", b=2, h=4)
        MRG = XN
        r_at = sb("r_at", 2048)
        PT = r_at.rearrange("p (b m q) -> p b m q", b=2, m=8)
        AT = r_at.rearrange("p (k t) -> p k t", k=KD)
        ident = sb("ident", P)
        DM = sb("dist_causal", 512).rearrange("p (t k) -> p t k", t=2)
        DMW = sb("dist_window", 512).rearrange("p (t k) -> p t k", t=2)
        r_u = sb("r_u", 2048)
        U = r_u[:, 0:512].rearrange("p (t k) -> p t k", t=2)
        MK = r_u[:, 512:1024].rearrange("p (t k) -> p t k", t=2)
        GT = r_u[:, 1024:2048].rearrange("p (g s t) -> p g s t", g=2, s=2)
        brow = r_u
        CV = sb("cmp_valid", 30).rearrange("p (t k) -> p t k", t=2)
        CM = sb("cmp_mask", 30).rearrange("p (t k) -> p t k", t=2)
        io32 = sb("iota32", 32)
        ones = sb("ones", 256)
        VT = sb("vec_T", P)
        VT2 = sb("vec_T2", 40)
        modT = sb("mod_T", 32)
        eps = sb("eps", 2)
        dtb, alog, dsk = sb("dt_bias_b", 16), sb("a_log_b", 16), sb("d_skip_b", 16)
        rb1, rb2 = sb("router_bias1", 20), sb("router_bias2", 32)
        snk, nsnk = sb("sinks_b", 8), sb("neg_sinks_b", 8)
        lamv = sb("lambda_b", 256)
        sub_g = sb("subln_b", P)
        cb2 = sb("cmp_b2_b", 2 * 64)
        cb2T = sb("cmp_b2_T", 1)
        cw2 = sb("cmp_w2", 4 * 64).rearrange("p (j k n) -> p j k n", j=2, k=2)
        wr1 = sb("router_w1", KD * 20).rearrange("p (k n) -> p k n", k=KD)
        wr2 = sb("router_w2", KD * 32).rearrange("p (k n) -> p k n", k=KD)
        wdt = sb("w_dt", KD * 16).rearrange("p (k n) -> p k n", k=KD)
        wgn = sb("w_gn", KD * 24).rearrange("p (k n) -> p k n", k=KD)
        st = sb("stats", 84)
        rt_s = sb("route", 256)
        comb = sb("combine", NT * 32).rearrange("p (t e) -> p t e", t=NT)
        r_big = sb("r_big", R_BIG)
        used = [0]

        def take(n):
            used[0] += n
            assert used[0] <= R_BIG, used[0]
            return r_big[:, used[0] - n:used[0]]

        qT = take(1024).rearrange("p (c t) -> p c t", c=4)
        kT = take(1024).rearrange("p (c t) -> p c t", c=4)
        v1 = take(1024).rearrange("p (t n) -> p t n", t=2)
        O1 = take(1024).rearrange("p (t n) -> p t n", t=2)
        silz = take(2048).rearrange("p (t n) -> p t n", t=2)
        xbcP = take(12 * 259).rearrange("p (c t) -> p c t", c=12)
        cvT = take(3072).rearrange("p (c t) -> p c t", c=12)
        ssd_small = take(8 * 32)
        xs = r_big[:, 0:2048].rearrange("p (t n) -> p t n", t=2)
        xdt = XN
        Y = xbcP.rearrange("p c t -> p (c t)")[:, 0:2048].rearrange("p (t n) -> p t n", t=2)
        Mt = cvT.rearrange("p c t -> p (c t)").rearrange("p (b h n) -> p b h n", b=2, h=4)
        OT = r_big[:, 2048:3072].rearrange("p (c t) -> p c t", c=4)
        sg = r_big[:, 3072:4096].rearrange("p (t n) -> p t n", t=2)
        pin = r_big[:, 0:512].rearrange("p (t n) -> p t n", t=2)
        pT = r_big[:, 512:1024].rearrange("p (c t) -> p c t", c=2)
        growB = r_big[:, 4096:5120]
        used1 = used[0]
        used[0] = 5120
        Hb = take(2048).rearrange("p (b f t) -> p b f t", b=2, f=4)
        GS = take(1024)
        US = take(1024)
        SG = take(1024)
        ACC = take(2048).rearrange("p (t n) -> p t n", t=2)
        b1T = r_big[:, 0:512].rearrange("p (e f) -> p e f", e=32)
        b1R = r_big[:, 512:1024].rearrange("p (c n) -> p c n", c=4)
        b2R = r_big[:, 1024:2048]
        combT = r_big[:, 2048:2304]
        used[0] = 0
        qa = take(1024).rearrange("p (c t) -> p c t", c=4)
        qb = take(1024).rearrange("p (c t) -> p c t", c=4)
        kb = take(1024).rearrange("p (c t) -> p c t", c=4)
        vb = take(1024).rearrange("p (t n) -> p t n", t=2)
        qc = take(1024).rearrange("p (c t) -> p c t", c=4)
        ka = take(512).rearrange("p (h t) -> p h t", h=2)
        ksl = take(512).rearrange("p (h t) -> p h t", h=2)
        kwn = take(512).rearrange("p (h t) -> p h t", h=2)
        va = take(256).rearrange("p (t n) -> p t n", t=2)
        vsl = take(256).rearrange("p (t n) -> p t n", t=2)
        vwn = take(256).rearrange("p (t n) -> p t n", t=2)
        kraw = take(512).rearrange("p (j t) -> p j t", j=2)
        kexp = take(960).rearrange("p (j l h c) -> p j l h c", j=2, l=16, h=2)
        hid = take(120).rearrange("p (j m c) -> p j m c", j=2, m=2)
        kcmp = take(30).rearrange("p (h c) -> p h c", h=2)
        vcmp = take(128).rearrange("p (h n) -> p h n", h=2)
        gts = take(48).rearrange("p (t n) -> p t n", t=2)
        Oa = take(1024).rearrange("p (t n) -> p t n", t=2)
        Ob = take(1024).rearrange("p (t n) -> p t n", t=2)
        Oc = take(1024).rearrange("p (t n) -> p t n", t=2)
        tmpO = kraw.rearrange("p j t -> p (j t)")
        hT3 = [x for x in (qb, kb, qc)]
        sg2 = qa.rearrange("p c t -> p (c t)").rearrange("p (t n) -> p t n", t=2)
        G12 = sb("mod_gates", 2048).rearrange("p (g n) -> p g n", g=2)

        growA = G12[:, 0]
        growF = r_u[:, 0:1024]

        ps = [ctx.enter_context(nc.psum_tensor(f"pair{i}", [P, 1024], F32))[:, :] for i in range(4)]

        def blk(w, r0, nk, c0, n):
            return w[r0:r0 + nk * P, c0:c0 + n].rearrange("(t p) n -> p t n", p=P)

        items, item_at = [], {}

        def item(name, w, r0, nk, c0, n):
            item_at[name] = len(items)
            items.append((blk(w, r0, nk, c0, n), nk, n))

        w_in, w_in2 = a["w_in"][0], a["w_in_2"][0]
        for nm, c0 in (("q", W1["q"]), ("k", W1["k"]), ("v", W1["v"]), ("z0", W1["z"]), ("z1", W1["z"] + 512),
                       ("x0", W1["xbc"]), ("x1", W1["xbc"] + 512), ("x2", W1["xbc"] + 1024)):
            item(nm, w_in, 0, KD, c0, 512)
        item("woa", a["w_out_a"][0], 0, 4, 0, 1024)
        item("ga0", w_in, 0, KD, W1["ga"], 512)
        item("ga1", w_in, 0, KD, W1["ga"] + 512, 512)
        for h in range(2):
            item(f"wob{h}", a["w_out_b"][0], 0, KD, 512 * h, 512)
            item(f"gb{h}", w_in, 0, KD, W1["gb"] + 512 * h, 512)
        for h in range(2):
            item(f"wo{h}", a["w_out"][0], 0, KD, 512 * h, 512)
        n_front1 = len(items)
        moe1_slot = n_front1 % RING
        front1 = list(items)
        items.clear()
        after1 = {}

        def item2(name, w, r0, nk, c0, n):
            after1[name] = len(items)
            items.append((blk(w, r0, nk, c0, n), nk, n))

        for h in range(2):
            item2(f"pg{h}", a["w_ple_gate"][0], 0, KD, 512 * h, 512)
        item2("pp", a["w_ple_proj"][0], 0, 2, 0, 1024)
        for i in range(12):
            item2(f"mod{i}", a["mod_w_2"][0], 0, KD, 512 * i, 512)
        for nm, c0, n in (("qa", W2["qa"], 512), ("kva", W2["kva"], 256), ("qb", W2["qb"], 512), ("kb", W2["kb"], 512),
                          ("vb", W2["vb"], 512), ("qc", W2["qc"], 512), ("kvc", W2["kvc"], 512),
                          ("kvw", W2["kvw"], 256)):
            item2(nm, w_in2, 0, KD, c0, n)
        for j in range(2):
            item2(f"cw{j}", a["cmp_w1_2"][0, j], 0, 16, 0, 256)
        for b in range(3):
            item2(f"wb{b}", a["w_branch_2"][0, b], 0, 4, 0, 1024)
            for h in range(2):
                item2(f"gm{b}{h}", w_in2, 0, KD, W2["gm"] + 1024 * b + 512 * h, 512)
        for h in range(2):
            item2(f"w2o{h}", a["w_out_2"][0], 0, KD, 512 * h, 512)
        front2 = list(items)
        n1_exp, n2_exp = NE1, 2 * NE2
        base_mid = n_front1 + 3 * n1_exp
        base_exp2 = base_mid + len(front2)

        steps = {}
        seq = []

        def step(name, *names):
            for nm in (name,) + names:
                steps[nm] = len(seq)
                seq.append(nm)

        step("vec", "xt0", "xt1", "q", "k", "v", "z0", "z1", "x0", "x1", "x2", "dt")
        step("G", "xsT0", "xsT1", "xsT2", "xsT3", "cs", "cb0", "cb1", "cb2", "cb3")
        step("ot1", "a0", "ga0", "a1", "ga1", "yt0", "yt1", "b0", "gb0", "b1", "gb1")
        step("mt0", "mt1", "wo0", "wo1", "ht0", "ht1", "rt1")
        n_s1 = len(seq)
        step("p0", "p1", "ptr", "pg0", "pp0", "pg1", "pp1")
        step("md0", "md1", "md2", "md3", "md4", "md5", "md6", "md7", "md8", "md9", "md10", "md11")
        step("nt0", "nt1", "qa", "ka", "va", "qb", "kb", "vb", "qc", "kc", "ksl", "vsl", "kwn", "vwn", "gn")
        step("c0", "c1", "cc")
        for b in range(3):
            step(f"bt{b}", f"y{b}0", f"g{b}0", f"y{b}1", f"g{b}1")
        step("nt2", "nt3", "no0", "no1", "h20", "h21", "rt2", "b1t", "ct", "cb")
        last_step_of_item = dict(q="q", k="k", v="v", z0="z0", z1="z1", x0="x0", x1="x1", x2="x2", woa="a1", ga0="ga0",
                                 ga1="ga1", wob0="b0", gb0="gb0", wob1="b1", gb1="gb1", wo0="wo0", wo1="wo1",
                                 pg0="pg0", pg1="pg1", pp="pp1", qa="qa", kva="va", qb="qb", kb="kb", vb="vb",
                                 qc="qc", kvc="vsl", kvw="vwn", cw0="c0", cw1="c1", w2o0="no0", w2o1="no1")
        for i in range(12):
            last_step_of_item[f"mod{i}"] = f"md{i}"
        for b in range(3):
            last_step_of_item[f"wb{b}"] = f"y{b}1"
            for h in range(2):
                last_step_of_item[f"gm{b}{h}"] = f"g{b}{h}"

        def done_value(name):
            n = steps[name] + 1
            return n if steps[name] < n_s1 else n + 3 * n1_exp

        PD = sem("products_done")
        pair_free = [sem("pair0_free"), sem("pair1_free")]
        gate_free, up_free, down_free = sem("gate_psum_free"), sem("up_psum_free"), sem("down_psum_free")
        slot_loaded = [sem(f"slot{i}_loaded") for i in range(RING)]

        def pair(name):
            return ps[steps[name] % 2]

        def uses_before(j):
            return 16 * (j // RING + 1)

        def slopes(n):
            return [2.0 ** (-8.0 * (i + 1) / n) for i in range(n)]

        chunks = []

        def add_maps(kind, tag, w=64):
            for qt in range(NT):
                for hc in range(2):
                    chunks.append((kind, tag, qt, hc, w))

        add_maps("moba", 0)
        n_att1 = len(chunks)
        add_maps("swa", 0)
        add_maps("diff", 0, 128)
        add_maps("cmp", 0)
        add_maps("slc", 0)
        add_maps("win", 0)

        def map_operands(kind, h):
            lo = 64 * (h % 2)
            r = slice(lo, lo + 64)
            if kind == "moba":
                return qT[r, h // 2], kT[r, h // 2]
            if kind == "swa":
                return qa[r, h // 2], ka[r, h // 4]
            if kind == "diff":
                return qb[r, h // 2], kb[r, h // 2]
            k = {"cmp": kcmp, "slc": ksl, "win": kwn}[kind]
            return qc[r, h // 2], k[r, h // 4]

        def map_values(kind, h, kt):
            if kind == "moba":
                return v1[:, kt, 64 * h:64 * h + 64]
            if kind == "diff":
                return vb[:, kt, 128 * (h // 2):128 * (h // 2) + 128]
            if kind == "cmp":
                return vcmp[0:15, h // 4, :]
            vv = {"swa": va, "slc": vsl, "win": vwn}[kind]
            return vv[:, kt, 64 * (h // 4):64 * (h // 4) + 64]

        def score_col(h):
            return 512 * (h % 2) + 256 * (h // 2)

        def map_slope(kind, h):
            return slopes(4)[h // 2] if kind == "diff" else slopes(8)[h]

        nm_s = st[:, 0:8].rearrange("p (b h) -> p b h", b=2)
        rs_s = st[:, 8:16].rearrange("p (b h) -> p b h", b=2)
        es_s = st[:, 16:24].rearrange("p (b h) -> p b h", b=2)
        rv_s = st[:, 24:28]
        lam_s = st[:, 28:36]
        ss_s = st[:, 36:52]
        g8 = st[:, 52:60]
        m8 = st[:, 60:68]
        i8 = sb("top_index", 8, U32)
        f8 = st[:, 68:76]
        w8 = st[:, 76:84]

        n_vec, n_small, n_p = 11, 20, 19

        block = ctx.enter_context(nc.Block())

        @block.sync
        def _(sp):
            loads = {}

            def load(dst, src, s="vectors_loaded"):
                loads[s] = loads.get(s, 0) + 1
                sp.dma_start(dst, src).then_inc(sem(s), 16)

            def ring_load(j, ap, nk, n, wait):
                if wait is not None:
                    sp.wait_ge(PD, wait)
                s = j % RING
                dst = ring[:, s * SLOT:s * SLOT + nk * n].rearrange("p (t n) -> p t n", t=nk)
                sp.dma_start(dst, ap).then_inc(slot_loaded[s], 16)

            read_at = []
            for nm, idx in item_at.items():
                read_at.append(done_value(last_step_of_item[nm]))
            for k in range(3 * n1_exp):
                read_at.append(n_s1 + k + 1)
            for nm, idx in after1.items():
                read_at.append(done_value(last_step_of_item[nm]))

            load(X[:, :, :], a["x"][0].rearrange("(t p) n -> p t n", p=P), "x_loaded")
            r0 = 0
            vr = XT.rearrange("p k t -> p (k t)")[:, 0:P]
            vr2 = XT.rearrange("p k t -> p (k t)")[:, P:2 * P]
            for src, n in ((a["mix_norm_g"][0], 8), (a["ffn_norm_g"][0], 8), (a["norm1_g_2"][0], 8),
                           (a["norm2_g_2"][0], 8), (a["conv_b"][0], 12)):
                load(vr[r0:r0 + n, :], src.rearrange("(r n) -> r n", n=P))
                r0 += n
            load(vr[r0:r0 + 48, :], a["conv_w"][0].rearrange("k (r n) -> (k r) n", n=P))
            load(vr[92:108, :], a["mod_b_2"][0, 0:2048].rearrange("(r n) -> r n", n=P))
            load(vr[108:124, :], a["mod_b_2"][0, 3072:5120].rearrange("(r n) -> r n", n=P))
            load(vr[124:128, :], a["cmp_b1_2"][0].rearrange("j (r n) -> (j r) n", n=P))
            load(vr2[0:32, :], a["cmp_pos_2"][0].rearrange("j (l r) d -> (j l) (r d)", r=2))
            load(vr2[32:40, :], a["c_2"][0].rearrange("(r n) -> r n", n=P))
            for j in range(RING):
                ap, nk, n = front1[j]
                ring_load(j, ap, nk, n, None)
            load(wdt[:, :, :], blk(w_in, 0, KD, W1["dt"], 16), "small_loaded")
            load(wr1[:, :, 0:4], blk(a["w_rg"][0], 0, KD, 0, 4), "small_loaded")
            load(wr1[:, :, 4:20], blk(a["w_re"][0], 0, KD, 0, 16), "small_loaded")
            load(wr2[:, :, :], blk(a["router_w_2"][0], 0, KD, 0, 32), "small_loaded")
            load(wgn[:, :, :], blk(w_in2, 0, KD, W2["gn"], 24), "small_loaded")
            for j in range(2):
                load(cw2[:, j], blk(a["cmp_w2_2"][0, j], 0, 2, 0, 64), "small_loaded")
            for half in range(2):
                load(cb2T[64 * half:64 * half + 64, :], a["cmp_b2_2"][0, 0].rearrange("(n o) -> n o", o=1), "small_loaded")
            for dst, src in ((dtb, a["dt_bias"][0]), (alog, a["a_log"][0]), (dsk, a["d_skip"][0]),
                             (rb1[:, 0:4], a["b_rg"][0]), (rb1[:, 4:20], a["b_re"][0]), (rb2, a["router_b_2"][0]),
                             (snk, a["sinks_2"][0]), (lamv, a["diff_lambda_2"][0].rearrange("a b -> (a b)")),
                             (sub_g, a["diff_subln_g_2"][0]),
                             (cb2, a["cmp_b2_2"][0].rearrange("a b -> (a b)")),
                             (growA, a["ssd_norm_g"][0])):
                load(dst, src.rearrange("(o n) -> o n", o=1).broadcast_to([P, src.shape[0]]), "small_loaded")
            assert loads["vectors_loaded"] == n_vec and loads["small_loaded"] == n_small
            starts = [(W2["qa"], 512), (W2["kva"], 256), (W2["qb"], 512), (W2["kb"], 512), (W2["vb"], 512),
                      (W2["qc"], 512), (W2["kvc"], 512), (W2["kvw"], 256), (W2["gn"], 24)] + \
                     [(W2["gm"] + 512 * i, 512) for i in range(6)]
            for j in range(RING, n_front1):
                ap, nk, n = front1[j]
                ring_load(j, ap, nk, n, read_at[j - RING])
            wg = a["w_gate"][0].rearrange("e d f -> (e d) f")
            wu = a["w_up"][0].rearrange("e d f -> (e d) f")
            wd = a["w_down"][0].rearrange("e f d -> (e f) d")

            def expert1(slot, kind, e, wait):
                w, nk, n = ((wg, KD, 512), (wu, KD, 512), (wd, 4, 1024))[kind]
                sp.wait_ge(PD, wait)
                src = w[bass.ds(e * (nk * P), nk * P), :].rearrange("(t p) n -> p t n", p=P)
                dst = ring[:, slot * SLOT:(slot + 1) * SLOT].rearrange("p (t n) -> p t n", t=nk)
                sp.dma_start(dst, src).then_inc(slot_loaded[slot], 16)

            j = n_front1
            for kind in (0, 1):
                expert1(j % RING, kind, 0, read_at[j - RING])
                j += 1
            def body1(i, jj, wait_of):
                for k, (kind, de) in enumerate(((0, 1), (1, 1), (2, 0), (0, 2), (1, 2), (2, 1))):
                    expert1((jj + k) % RING, kind, 2 * i + de, wait_of(k))

            body1(0, j, lambda k: read_at[j + k - RING])
            with sp.Fori(1, (n1_exp - 2) // 2) as i:
                body1(i, j, lambda k: 6 * i + (n_s1 + 2 + k - RING + 1))
            j += 3 * (n1_exp - 2)
            for kind, e in ((0, n1_exp - 1), (1, n1_exp - 1), (2, n1_exp - 2), (2, n1_exp - 1)):
                expert1(j % RING, kind, e, read_at[j - RING])
                j += 1
            assert j == base_mid
            sp.wait_ge(sem("ssd_gated"), 1)
            sp.wait_ge(sem("h2_ready"), 1)
            for s, (c0, n) in enumerate(starts):
                load(brow[32 * (s % 4):32 * (s % 4) + 1, 512 * (s // 4):512 * (s // 4) + n],
                     a["b_in_2"][0:1, c0:c0 + n], "p_loaded")
            load(pin[:, :, :], a["p"][0, 0].rearrange("(t p) n -> p t n", p=P), "p_loaded")
            for dst, src in ((growB, a["final_norm_g"]), (G12[:, 0], a["mod_b_2"][0, 2048:3072]),
                             (G12[:, 1], a["mod_b_2"][0, 5120:6144])):
                load(dst, src.rearrange("(o n) -> o n", o=1).broadcast_to([P, D]), "p_loaded")
            assert loads["p_loaded"] == n_p
            for k, (ap, nk, n) in enumerate(front2):
                ring_load(base_mid + k, ap, nk, n, read_at[base_mid + k - RING])
            w1e = a["exp_w1_2"][0].rearrange("e d f -> (e d) f")
            w2e = a["exp_w2_2"][0].rearrange("e f d -> (e f) d")

            def expert2(slot, kind, e, half, wait):
                sp.wait_ge(PD, wait)
                if kind < 2:
                    src = w1e[bass.ds(e * D, D), 1024 * kind + 512 * half:1024 * kind + 512 * half + 512]
                    nk = KD
                else:
                    src = w2e[bass.ds(e * D + 512 * half, 512), :]
                    nk = 4
                dst = ring[:, slot * SLOT:(slot + 1) * SLOT].rearrange("p (t n) -> p t n", t=nk)
                sp.dma_start(dst, src.rearrange("(t p) n -> p t n", p=P)).then_inc(slot_loaded[slot], 16)

            base_pd2 = len(seq) + 3 * n1_exp
            j = base_exp2
            for kind in (0, 1):
                expert2(j % RING, kind, 0, 0, read_at[j - RING])
                j += 1

            def body2(i, jj, wait_of):
                for k, (kind, de, half) in enumerate(((0, 0, 1), (1, 0, 1), (2, 0, 0), (0, 1, 0), (1, 1, 0), (2, 0, 1))):
                    expert2((jj + k) % RING, kind, i + de, half, wait_of(k))

            extra = [read_at[-(4 - k)] for k in range(4)] + [base_pd2 + 1, base_pd2 + 2]
            body2(0, j, lambda k: extra[k])
            with sp.Fori(1, (n2_exp - 2) // 2) as i:
                body2(i, j, lambda k: 6 * i + (base_pd2 + 2 + k - RING + 1))
            j += 3 * (n2_exp - 2)
            for m, (kind, e, half) in enumerate(((0, NE2 - 1, 1), (1, NE2 - 1, 1), (2, NE2 - 1, 0), (2, NE2 - 1, 1))):
                expert2(j % RING, kind, e, half, base_pd2 + 3 * (n2_exp - 2) + 2 + m - RING + 1)
                j += 1
            sp.wait_ge(sem("out_ready"), 1)
            sp.dma_start(a["out"][0].rearrange("(t p) n -> p t n", p=P), X[:, :, :]).then_inc(sem("stored"), 16)
            sp.wait_ge(sem("stored"), 16)

        @block.gpsimd
        def _(pool):
            cnt = [0]

            def link(ins):
                cnt[0] += 1
                ins.then_inc(sem("pool_step"), 1)
                pool.wait_ge(sem("pool_step"), cnt[0])

            g = nc.gpsimd
            link(g.memset(ident, 0.0))
            link(g.affine_select(out=ident, in_=ident, pattern=[[-1, P]], compare_op=ALU.not_equal, fill=1.0, base=0,
                                 channel_multiplier=1))
            link(g.iota(DM, pattern=[[P, 2], [-1, T]], base=0, channel_multiplier=1,
                        allow_small_or_imprecise_dtypes=True))
            link(g.affine_select(out=DM, in_=DM, pattern=[[P, 2], [-1, T]], compare_op=ALU.is_ge, fill=BIG, base=0,
                                 channel_multiplier=1))
            link(g.affine_select(out=DMW, in_=DM, pattern=[[-P, 2], [1, T]], compare_op=ALU.is_ge, fill=BIG,
                                 base=127, channel_multiplier=-1))
            link(g.memset(U, 1.0))
            link(g.memset(MK, 0.0))
            for t, fill in ((U, 0.0), (MK, -BIG)):
                link(g.affine_select(out=t, in_=t, pattern=[[-P, 2], [1, T]], compare_op=ALU.is_ge, fill=fill, base=0,
                                     channel_multiplier=-1))
            link(g.memset(CV, 1.0))
            link(g.memset(CM, 0.0))
            for t, fill in ((CV, 0.0), (CM, -BIG)):
                link(g.affine_select(out=t, in_=t, pattern=[[P, 2], [-16, 15]], compare_op=ALU.is_ge, fill=fill,
                                     base=-31, channel_multiplier=1))
            link(g.iota(io32, pattern=[[1, 32]], base=0, channel_multiplier=0, allow_small_or_imprecise_dtypes=True))
            link(g.memset(ones, 1.0))
            link(g.memset(eps[:, 0:1], 1e-6))
            link(g.memset(eps[:, 1:2], 1e-5))
            link(g.memset(g8, -BIG))
            g.memset(xbcP[:, :, 0:3], 0.0).then_inc(sem("constants_ready"), 1)

            def gated(n):
                pool.wait_ge(sem("sig_ready"), n + 1)
                g.tensor_tensor(out=SG, in0=SG, in1=GS, op=ALU.mult).then_inc(sem("gated_ready"), 1)

            gated(0)
            with pool.Fori(0, (n2_exp - 2) // 2) as i:
                for k in range(2):
                    gated(2 * i + (1 + k))
            gated(n2_exp - 1)

        @block.scalar
        def _(act):
            s = nc.scalar
            cnt = {}

            def link(ins, name="act_step"):
                cnt[name] = cnt.get(name, 0) + 1
                ins.then_inc(sem(name), 1)
                act.wait_ge(sem(name), cnt[name])

            def products(name):
                act.wait_ge(PD, done_value(name))

            def freed(ins, name):
                ins.then_inc(pair_free[steps[name] % 2], 1)
                act.wait_ge(pair_free[steps[name] % 2], steps[name] // 2 + 1)

            def square_sums(src, dst, nseg, width, scr):
                for t in range(NT):
                    for g in range(nseg):
                        link(s.activation(scr, src[:, t, g * width:(g + 1) * width], ACT.Square,
                                          accum_out=dst[:, t * nseg + g:t * nseg + g + 1]))

            def rms(src, eps_col, name, nseg=1, width=D, scr=None):
                square_sums(src, ss_s, nseg, width, scr)
                link(s.activation(ss_s[:, 0:NT * nseg], ss_s[:, 0:NT * nseg], ACT.Sqrt, bias=eps[:, eps_col:eps_col + 1],
                                  scale=1.0 / width), name)

            def attention(c0, c1):
                for c in range(c0, c1):
                    kind, _, qt, hc, w = chunks[c]
                    b = c % 2
                    nk = 15 if kind == "cmp" else P * (qt + 1)
                    act.wait_ge(sem("scores_biased"), c + 1)
                    if kind == "swa":
                        link(s.activation(es_s[:, b], es_s[:, b], ACT.Exp))
                    for h in range(4):
                        ins = s.activation(SC[:, b, h, 0:nk], SC[:, b, h, 0:nk], ACT.Exp, bias=nm_s[:, b, h:h + 1],
                                           accum_out=rs_s[:, b, h:h + 1])
                    ins.then_inc(sem("probs_ready"), 1)
                    act.wait_ge(sem("probs_transposed"), c + 1)
                    nt = 1 if kind == "cmp" else qt + 1
                    rows = 15 if kind == "cmp" else P
                    if c >= 2:
                        act.wait_ge(sem("outputs_done"), c - 1)
                    s.copy(PT[0:rows, b, 0:4 * nt], ps[2][0:rows, 0:512 * nt]).then_inc(sem("probsT_ready"), 1)

            act.wait_ge(sem("constants_ready"), 1)
            act.wait_ge(sem("x_loaded"), 16)
            rms(X, 0, "rms_ready", scr=XN[:, 0])
            products("vec")
            link(s.copy(VT, ps[0][:, 0:P]))
            link(s.copy(VT2[:, 0:32], ps[0][:, P:P + 32]))
            freed(s.activation(VT2[:, 32:40], ps[0][:, P + 32:P + 40], ACT.Silu), "vec")
            products("q")
            freed(s.mul(qT, ps[steps["q"] % 2], 0.125), "q")
            products("k")
            freed(s.copy(kT, pair("k")), "k")
            products("v")
            freed(s.copy(v1, pair("v")), "v")
            for h in range(2):
                products(f"z{h}")
                freed(s.activation(silz[:, :, 512 * h:512 * h + 512], pair(f"z{h}").rearrange("p (t n) -> p t n", t=2),
                                   ACT.Silu), f"z{h}")
            for h in range(3):
                products(f"x{h}")
                freed(s.copy(xbcP[:, 4 * h:4 * h + 4, 3:259], pair(f"x{h}").rearrange("p (c t) -> p c t", c=4)), f"x{h}")
            act.wait_ge(sem("small_loaded"), 16 * n_small)
            act.wait_ge(sem("dt_raw"), 1)
            dr, dabs, dtt, dA, ncs = [ssd_small[:, 32 * k:32 * k + 32] for k in range(5)]
            link(s.activation(dabs, dr, ACT.Abs))
            link(s.activation(dabs, dabs, ACT.Exp, scale=-1.0))
            link(s.activation(dA[:, 0:16], alog, ACT.Exp))
            link(s.activation(dabs, dabs, ACT.Ln, bias=ones[:, 0:1]), "dt_logs")
            attention(0, n_att1)
            act.wait_ge(sem("conv_done"), 1)
            link(s.activation(cvT, cvT, ACT.Silu), "conv_ready")
            for g in range(4):
                act.wait_ge(sem("decay_biased"), g + 1)
                s.activation(Mt[:, g % 2], Mt[:, g % 2], ACT.Exp).then_inc(sem("decay_exp"), 1)
            for h in range(2):
                products(f"ga{h}")
                if h:
                    act.wait_ge(sem("merged"), 1)
                freed(s.activation(sg, pair(f"ga{h}"), ACT.Sigmoid), f"ga{h}")
            act.wait_ge(sem("ssd_gated"), 1)
            rms(Y, 0, "rms_ready", nseg=2, width=512, scr=AT.rearrange("p k t -> p (k t)")[:, 0:512])
            for h in range(2):
                products(f"gb{h}")
                act.wait_ge(sem("merged"), 2 + h)
                freed(s.activation(sg, pair(f"gb{h}"), ACT.Sigmoid), f"gb{h}")
            for t in range(2):
                products(f"mt{t}")
                freed(s.copy(AT[:, 4 * t:4 * t + 4], pair(f"mt{t}")), f"mt{t}")
            act.wait_ge(sem("resid_ready"), 1)
            act.wait_ge(PD, done_value("wo1"))
            rms(X, 0, "rms_ready", scr=AT.rearrange("p k t -> p (k t)")[:, 0:1024])
            act.wait_ge(sem("route_exp"), 1)
            for t in range(NT):
                link(s.activation(rt_s[:, 64 * t:64 * t + 5], rt_s[:, 64 * t:64 * t + 5], ACT.Exp), "route_exped")

            def silu1(gate_done, n):
                act.wait_ge(PD, gate_done)
                if n is not None:
                    act.wait_ge(sem("hidden_ready"), n)
                s.activation(SG, ps[0], ACT.Silu).then_inc(gate_free, 1)

            silu1(n_s1 + 1, None)
            with act.Fori(0, (n1_exp - 2) // 2) as i:
                for k in range(2):
                    silu1(6 * i + (n_s1 + 2 + 3 * k + 1), 2 * i + (1 + k))
            silu1(n_s1 + 3 * n1_exp - 3, n1_exp - 1)
            for h in range(2):
                products(f"p{h}")
                freed(s.copy(XT[:, 4 * h:4 * h + 4], pair(f"p{h}")), f"p{h}")
            products("ptr")
            freed(s.copy(pT, pair("ptr")[:, 0:512]), "ptr")
            for h in range(2):
                products(f"pg{h}")
                if h:
                    act.wait_ge(sem("ple_added"), 1)
                freed(s.activation(sg, pair(f"pg{h}"), ACT.Sigmoid), f"pg{h}")
            act.wait_ge(sem("ple_added"), 2)
            rms(X, 0, "rms_ready", scr=XN[:, 0])
            act.wait_ge(sem("x2_ready"), 1)
            rms(X, 1, "rms_ready", scr=XN[:, 0])
            products("qa")
            freed(s.mul(qa, pair("qa"), 0.125), "qa")
            for nm, dst in (("ka", ka), ("ksl", ksl), ("kwn", kwn)):
                products(nm)
                src = pair(nm)[:, 0:256]
                for half in range(2):
                    for h in range(2):
                        ins = s.copy(dst[64 * half:64 * half + 64, h], src[64 * h:64 * h + 64])
                        if half and h:
                            freed(ins, nm)
                        else:
                            link(ins)
                if nm == "ka":
                    products("va")
                    freed(s.copy(va, pair("va").rearrange("p (t n) -> p t n", t=2)[:, :, 0:128]), "va")
                    products("qb")
                    freed(s.mul(qb, pair("qb"), 0.125), "qb")
                    for nm2, dst2 in (("kb", kb), ("vb", vb)):
                        products(nm2)
                        freed(s.copy(dst2, pair(nm2)), nm2)
                    products("qc")
                    freed(s.mul(qc, pair("qc"), 0.125), "qc")
                    products("kc")
                    freed(s.copy(kraw, pair("kc")[:, 0:512]), "kc")
                if nm == "ksl":
                    products("vsl")
                    freed(s.copy(vsl, pair("vsl").rearrange("p (t n) -> p t n", t=2)[:, :, 0:128]), "vsl")
                if nm == "kwn":
                    products("vwn")
                    freed(s.copy(vwn, pair("vwn").rearrange("p (t n) -> p t n", t=2)[:, :, 0:128]), "vwn")
            products("gn")
            freed(s.activation(gts, pair("gn").rearrange("p (t n) -> p t n", t=2)[:, :, 0:24], ACT.Sigmoid), "gn")
            for j in range(2):
                products(f"c{j}")
                for m in range(2):
                    ins = s.activation(hid[:, j, m], pair(f"c{j}")[:, 30 * m:30 * m + 30], ACT.Gelu_apprx_tanh,
                                       bias=VT[:, 124 + 2 * j + m:125 + 2 * j + m])
                    if m:
                        freed(ins, f"c{j}")
                    else:
                        link(ins)
            products("cc")
            act.wait_ge(sem("lambda_sums"), 1)
            link(s.activation(lam_s[:, 0:2], lam_s[:, 0:2], ACT.Exp), "lambda_exp")
            attention(n_att1, len(chunks))
            act.wait_ge(sem("diff_squares"), 1)
            link(s.activation(ss_s[:, 0:8], ss_s[:, 0:8], ACT.Sqrt, bias=eps[:, 1:2], scale=1.0 / P), "diff_rms")
            k = 0
            for b in range(3):
                for h in range(2):
                    products(f"g{b}{h}")
                    if k:
                        act.wait_ge(sem("merged2"), k)
                    freed(s.activation(sg2, pair(f"g{b}{h}"), ACT.Sigmoid), f"g{b}{h}")
                    k += 1
            for t in range(2):
                products(f"nt{t + 2}")
                freed(s.copy(AT[:, 4 * t:4 * t + 4], pair(f"nt{t + 2}")), f"nt{t + 2}")
            act.wait_ge(sem("resid2_ready"), 1)
            act.dma_start(b1R, a["exp_b1_2"][0].rearrange("e (f n) -> (e f) n", n=P).rearrange("(c p) n -> p c n", p=P))\
                .then_inc(sem("b_loaded"), 16)
            act.dma_start(b2R[0:32, :], a["exp_b2_2"][0]).then_inc(sem("b_loaded"), 16)
            act.dma_start(growF, a["final_g_2"].rearrange("(o n) -> o n", o=1).broadcast_to([P, D]))\
                .then_inc(sem("last_gain_loaded"), 16)
            rms(X, 1, "rms_ready", scr=AT.rearrange("p k t -> p (k t)")[:, 0:1024])
            for t in range(2):
                act.wait_ge(sem("route2_exp"), t + 1)
                link(s.activation(w8[:, 4 * t:4 * t + 4], w8[:, 4 * t:4 * t + 4], ACT.Exp,
                                  accum_out=rt_s[:, 224 + t:225 + t]), "route2_exped")

            def sigmoid2(n, first=False):
                act.wait_ge(sem("gate_limited"), n + 1)
                if not first:
                    act.wait_ge(sem("hidden_ready"), n + n1_exp)
                s.activation(SG, GS, ACT.Sigmoid, scale=1.702).then_inc(sem("sig_ready"), 1)

            sigmoid2(0, True)
            with act.Fori(0, (n2_exp - 2) // 2) as i:
                for k in range(2):
                    sigmoid2(2 * i + (1 + k))
            sigmoid2(n2_exp - 1)
            act.wait_ge(sem("moe2_added"), 1)
            rms(X, 1, "rms_ready", scr=XN[:, 0])

        @block.vector
        def _(dve):
            v = nc.vector
            cnt = {}

            def link(ins, name="dve_step"):
                cnt[name] = cnt.get(name, 0) + 1
                ins.then_inc(sem(name), 1)
                dve.wait_ge(sem(name), cnt[name])

            def flag(name):
                cnt[name] = cnt.get(name, 0) + 1
                dve.sem_inc(sem(name), 1)

            def products(name):
                dve.wait_ge(PD, done_value(name))

            def freed(ins, name):
                ins.then_inc(pair_free[steps[name] % 2], 1)
                dve.wait_ge(pair_free[steps[name] % 2], steps[name] // 2 + 1)

            n_rms = [0]

            def scale_rows(dst, nseg=1, width=D, src=None):
                n_rms[0] += 1
                dve.wait_ge(sem("rms_ready"), n_rms[0])
                link(v.reciprocal(ss_s[:, 0:NT * nseg], ss_s[:, 0:NT * nseg]))
                for t in range(NT):
                    for g in range(nseg):
                        link(v.tensor_scalar(dst[:, t, g * width:(g + 1) * width], src[:, t, g * width:(g + 1) * width],
                                             ss_s[:, t * nseg + g:t * nseg + g + 1], None, ALU.mult))

            def scaled_T(names, scale, shift, ready):
                for h in range(2):
                    products(names[h])
                    for k in range(4):
                        kk = 4 * h + k
                        src = pair(names[h])[:, 256 * k:256 * k + 256]
                        if shift is None:
                            ins = v.tensor_scalar(XT[:, kk], src, scale[:, kk:kk + 1], None, ALU.mult)
                        else:
                            ins = v.tensor_scalar(XT[:, kk], src, scale[:, kk:kk + 1], shift[:, kk:kk + 1], ALU.mult,
                                                  ALU.add)
                        if k < 3:
                            link(ins)
                    freed(ins, names[h])
                flag(ready)

            def bias_scores(c):
                kind, _, qt, hc, w = chunks[c]
                b = c % 2
                nk = 15 if kind == "cmp" else P * (qt + 1)
                dve.wait_ge(sem("scores_done"), c + 1)
                if c >= 2:
                    dve.wait_ge(sem("probs_transposed"), c - 1)
                if kind == "cmp":
                    for r in range(2):
                        ins = v.tensor_tensor(
                            out=SC[:, b].rearrange("p (j r) k -> p r j k", r=2)[:, r, :, 0:15],
                            in0=ps[b][:, 512 * r:512 * r + 512].rearrange("p (j k) -> p j k", j=2)[:, :, 0:15],
                            in1=CM[:, qt:qt + 1, :].broadcast_to([P, 2, 15]), op=ALU.add)
                    link(ins)
                else:
                    dm = DMW if kind == "swa" else DM
                    for h in range(4):
                        ins = v.scalar_tensor_tensor(out=SC[:, b, h, 0:nk], in0=dm[:, qt, 0:nk],
                                                     scalar=-map_slope(kind, 4 * hc + h),
                                                     in1=ps[b][:, score_col(h):score_col(h) + nk],
                                                     op0=ALU.mult, op1=ALU.add)
                    link(ins)
                red = v.tensor_reduce(out=nm_s[:, b], in_=SC[:, b, :, 0:nk], axis=AX.X, op=ALU.max, negate=True)
                if kind == "swa":
                    link(red)
                    link(v.tensor_tensor(out=nm_s[:, b], in0=nm_s[:, b], in1=nsnk[:, 4 * hc:4 * hc + 4], op=ALU.min))
                    link(v.tensor_tensor(out=es_s[:, b], in0=nm_s[:, b], in1=snk[:, 4 * hc:4 * hc + 4], op=ALU.add),
                         "scores_biased")
                else:
                    link(red, "scores_biased")

            def outputs(c):
                kind, _, qt, hc, w = chunks[c]
                b = c % 2
                dve.wait_ge(sem("outputs_done"), c + 1)
                if kind == "swa":
                    link(v.tensor_tensor(out=rs_s[:, b], in0=rs_s[:, b], in1=es_s[:, b], op=ALU.add))
                link(v.reciprocal(rv_s, rs_s[:, b]))
                if kind in ("cmp", "slc", "win"):
                    n = ("cmp", "slc", "win").index(kind)
                    gv = gts.rearrange("p t (h s) -> p t s h", s=3)[:, qt, n, 4 * hc:4 * hc + 4]
                    link(v.tensor_tensor(out=rv_s, in0=rv_s, in1=gv, op=ALU.mult))
                if kind == "cmp":
                    link(v.tensor_scalar(rv_s, rv_s, CV[:, qt, 0:1], None, ALU.mult))
                if kind == "diff":
                    neg = rv_s.rearrange("p (h c) -> p h c", c=2)[:, :, 1]
                    link(v.tensor_scalar(neg, neg, lam_s[:, 4:5], None, ALU.mult))
                src = ps[3][:, 512 * b:512 * b + 4 * w].rearrange("p (h n) -> p h n", h=4)
                rvb = rv_s.unsqueeze(2).broadcast_to([P, 4, w])
                if kind in ("moba", "swa", "cmp"):
                    dst = {"moba": O1, "swa": Oa, "cmp": Oc}[kind][:, qt, 256 * hc:256 * hc + 256]
                    link(v.tensor_tensor(out=dst.rearrange("p (h n) -> p h n", h=4), in0=src, in1=rvb, op=ALU.mult),
                         "outputs_scaled")
                else:
                    t4 = tmpO[:, 0:4 * w]
                    link(v.tensor_tensor(out=t4.rearrange("p (h n) -> p h n", h=4), in0=src, in1=rvb, op=ALU.mult))
                    if kind == "diff":
                        t2 = t4.rearrange("p (h c n) -> p h c n", h=2, c=2)
                        dst = Ob[:, qt, 256 * hc:256 * hc + 256].rearrange("p (h n) -> p h n", h=2)
                        link(v.tensor_tensor(out=dst, in0=t2[:, :, 0], in1=t2[:, :, 1], op=ALU.add), "outputs_scaled")
                    else:
                        dst = Oc[:, qt, 256 * hc:256 * hc + 256]
                        link(v.tensor_tensor(out=dst, in0=dst, in1=t4, op=ALU.add), "outputs_scaled")

            def attention(c0, c1):
                for c in range(c0, c1):
                    bias_scores(c)
                    if c > c0:
                        outputs(c - 1)
                outputs(c1 - 1)

            dve.wait_ge(sem("constants_ready"), 1)
            scale_rows(XN, src=X)
            flag("xn_ready")
            dve.wait_ge(pair_free[0], 1)
            scaled_T(("xt0", "xt1"), VT[:, 0:8], None, "xT_ready")
            dve.wait_ge(sem("small_loaded"), 16 * n_small)
            dr, dabs, dtt, dA, ncs = [ssd_small[:, 32 * k:32 * k + 32] for k in range(5)]
            products("dt")
            freed(v.tensor_tensor(out=dr.rearrange("p (t h) -> p t h", t=2),
                                  in0=pair("dt").rearrange("p (t n) -> p t n", t=2)[:, :, 0:16],
                                  in1=dtb.unsqueeze(1).broadcast_to([P, 2, 16]), op=ALU.add), "dt")
            flag("dt_raw")
            dve.wait_ge(sem("dt_logs"), 1)
            link(v.scalar_tensor_tensor(out=dtt, in0=dr, scalar=0.0, in1=dabs, op0=ALU.max, op1=ALU.add))
            d3 = [x.rearrange("p (t h) -> p t h", t=2) for x in (dr, dtt, ncs)]
            link(v.scalar_tensor_tensor(out=d3[0], in0=d3[1], scalar=-1.0,
                                        in1=dA[:, 0:16].unsqueeze(1).broadcast_to([P, 2, 16]),
                                        op0=ALU.mult, op1=ALU.mult), "da_ready")
            link(v.tensor_scalar(nsnk, snk, -1.0, None, ALU.mult))
            attention(0, n_att1)
            for c in range(12):
                link(v.tensor_scalar(cvT[:, c], xbcP[:, c, 0:T], VT[:, 44 + c:45 + c], VT[:, 32 + c:33 + c], ALU.mult,
                                     ALU.add))
                for k in range(1, 4):
                    link(v.scalar_tensor_tensor(out=cvT[:, c], in0=xbcP[:, c, k:k + T],
                                                scalar=VT[:, 44 + 12 * k + c:45 + 12 * k + c], in1=cvT[:, c],
                                                op0=ALU.mult, op1=ALU.add))
            flag("conv_done")
            products("G")
            freed(v.tensor_copy(GT, pair("G").rearrange("p (g s t) -> p g s t", g=2, s=2)), "G")
            for k in range(4):
                products(f"xsT{k}")
                freed(v.tensor_copy(xs[:, :, 256 * k:256 * k + 256],
                                    pair(f"xsT{k}")[:, 0:512].rearrange("p (t n) -> p t n", t=2)), f"xsT{k}")
            link(v.tensor_tensor(out=xdt.rearrange("p t (h n) -> p t h n", n=64),
                                 in0=xs.rearrange("p t (h n) -> p t h n", n=64),
                                 in1=d3[1].unsqueeze(3).broadcast_to([P, 2, 16, 64]), op=ALU.mult), "xdt_ready")
            products("cs")
            freed(v.tensor_scalar(ncs, pair("cs")[:, 0:32], -1.0, None, ALU.mult), "cs")
            def decay(g):
                b = g % 2
                products(f"cb{g}")
                if g >= 2:
                    dve.wait_ge(sem("ssd_heads_done"), g - 1)
                S4 = pair(f"cb{g}").rearrange("p (h t) -> p h t", h=4)
                for h in range(4):
                    hh = 4 * g + h
                    link(v.scalar_tensor_tensor(out=Mt[:, b, h, 0:256], in0=S4[:, h], scalar=ncs[:, hh:hh + 1],
                                                in1=MK[:, 0], op0=ALU.add, op1=ALU.add))
                    ins = v.scalar_tensor_tensor(out=Mt[:, b, h, 256:384], in0=S4[:, h, 128:256],
                                                 scalar=ncs[:, 16 + hh:17 + hh], in1=MK[:, 1, 128:256],
                                                 op0=ALU.add, op1=ALU.add)
                    if h < 3:
                        link(ins)
                freed(ins, f"cb{g}")
                flag("decay_biased")

            def times_g(g):
                b = g % 2
                gg = g // 2
                dve.wait_ge(sem("decay_exp"), g + 1)
                link(v.tensor_tensor(out=Mt[:, b, :, 0:256], in0=Mt[:, b, :, 0:256],
                                     in1=GT[:, gg, 0:1].broadcast_to([P, 4, 256]), op=ALU.mult))
                link(v.tensor_tensor(out=Mt[:, b, :, 256:384], in0=Mt[:, b, :, 256:384],
                                     in1=GT[:, gg, 1:2, 128:256].broadcast_to([P, 4, 128]), op=ALU.mult), "decay_ready")

            for g in range(4):
                decay(g)
                if g:
                    times_g(g - 1)
            times_g(3)
            dve.wait_ge(sem("ssd_heads_done"), 4)
            link(v.tensor_tensor(out=Y.rearrange("p t (h n) -> p t h n", n=64),
                                 in0=xs.rearrange("p t (h n) -> p t h n", n=64),
                                 in1=dsk.unsqueeze(1).unsqueeze(3).broadcast_to([P, 2, 16, 64]), op=ALU.mult))
            for t in range(2):
                link(v.tensor_tensor(out=Y[:, t], in0=Y[:, t], in1=ps[2 + t], op=ALU.add))
            link(v.tensor_tensor(out=Y, in0=Y, in1=silz, op=ALU.mult), "ssd_gated")
            products("ot1")
            freed(v.tensor_copy(OT, pair("ot1")), "ot1")

            def halves(dst, h):
                return dst[:, :, 512 * h:512 * h + 512]

            def two(name):
                return pair(name).rearrange("p (t n) -> p t n", t=2)

            for h in range(2):
                products(f"a{h}")
                products(f"ga{h}")
                dve.wait_ge(pair_free[steps[f"ga{h}"] % 2], steps[f"ga{h}"] // 2 + 1)
                freed(v.tensor_tensor(out=halves(MRG, h), in0=two(f"a{h}"), in1=sg, op=ALU.mult), f"a{h}")
                flag("merged")
            scale_rows(Y, nseg=2, width=512, src=Y)
            link(v.tensor_tensor(out=Y, in0=Y, in1=growA.unsqueeze(1).broadcast_to([P, 2, D]), op=ALU.mult), "y_ready")
            for h in range(2):
                products(f"yt{h}")
                freed(v.tensor_copy(AT[:, 4 * h:4 * h + 4], pair(f"yt{h}")), f"yt{h}")
            for h in range(2):
                products(f"b{h}")
                dve.wait_ge(pair_free[steps[f"gb{h}"] % 2], steps[f"gb{h}"] // 2 + 1)
                freed(v.tensor_tensor(out=sg, in0=two(f"b{h}"), in1=sg, op=ALU.mult), f"b{h}")
                link(v.tensor_tensor(out=halves(MRG, h), in0=halves(MRG, h), in1=sg, op=ALU.add), "merged")
            for h in range(2):
                products(f"wo{h}")
                freed(v.tensor_tensor(out=halves(X, h), in0=two(f"wo{h}"), in1=halves(X, h), op=ALU.add), f"wo{h}")
            flag("resid_ready")
            scale_rows(XN, src=X)
            flag("h2n_ready")
            scaled_T(("ht0", "ht1"), VT[:, 8:16], None, "h2_ready")

            def route_parts(t):
                o = 64 * t
                return rt_s[:, o:o + 8], rt_s[:, o + 12:o + 16], rt_s[:, o + 16:o + 32], rt_s[:, o + 32:o + 36]

            products("rt1")
            lg = rt_s[:, 128:168].rearrange("p (t n) -> p t n", t=2)
            freed(v.tensor_tensor(out=lg, in0=pair("rt1").rearrange("p (t n) -> p t n", t=2)[:, :, 0:20],
                                  in1=rb1.unsqueeze(1).broadcast_to([P, 2, 20]), op=ALU.add), "rt1")
            for t in range(2):
                e_, oh, ev, w_ = route_parts(t)
                link(v.tensor_copy(g8[:, 0:4], lg[:, t, 0:4]))
                link(v.max(out=m8, in_=g8))
                link(v.max_index(out=i8, in_max=m8, in_values=g8))
                link(v.tensor_copy(f8, i8))
                link(v.tensor_scalar(oh, io32[:, 0:4], f8[:, 0:1], None, ALU.is_equal))
                link(v.tensor_scalar(e_[:, 0:4], lg[:, t, 0:4], m8[:, 0:1], None, ALU.subtract))
                link(v.tensor_scalar(oh, oh, -1.0, BIG, ALU.add, ALU.mult))
                link(v.tensor_tensor(out=ev.rearrange("p (g e) -> p g e", g=4),
                                     in0=lg[:, t, 4:20].rearrange("p (g e) -> p g e", g=4),
                                     in1=oh.unsqueeze(2).broadcast_to([P, 4, 4]), op=ALU.add))
                link(v.max(out=m8, in_=ev))
                link(v.max_index(out=i8, in_max=m8, in_values=ev))
                link(v.tensor_copy(f8, i8))
                link(v.tensor_tensor(out=e_[:, 4:5], in0=m8[:, 1:2], in1=m8[:, 0:1], op=ALU.subtract))
                link(v.tensor_copy(w_[:, 0:2], f8[:, 0:2]))
            flag("route_exp")
            dve.wait_ge(sem("route_exped"), 2)
            for t in range(2):
                e_, oh, ev, w_ = route_parts(t)
                link(v.tensor_reduce(out=w_[:, 2:3], in_=e_[:, 0:4], axis=AX.X, op=ALU.add))
                link(v.tensor_scalar(w_[:, 3:4], e_[:, 4:5], 1.0, None, ALU.add))
                link(v.tensor_tensor(out=w_[:, 2:3], in0=w_[:, 2:3], in1=w_[:, 3:4], op=ALU.mult))
                link(v.reciprocal(w_[:, 2:3], w_[:, 2:3]))
                link(v.tensor_tensor(out=w_[:, 3:4], in0=w_[:, 2:3], in1=e_[:, 4:5], op=ALU.mult))
                link(v.tensor_scalar(comb[:, t, 0:16], io32[:, 0:16], w_[:, 0:1], w_[:, 2:3], ALU.is_equal, ALU.mult))
                link(v.tensor_scalar(ev, io32[:, 0:16], w_[:, 1:2], w_[:, 3:4], ALU.is_equal, ALU.mult))
                link(v.tensor_tensor(out=comb[:, t, 0:16], in0=comb[:, t, 0:16], in1=ev, op=ALU.add))

            def add_down(n_prev, e, dst, wait_pd, first):
                dve.wait_ge(PD, wait_pd)
                for t in range(NT):
                    for h in range(2):
                        ins = v.scalar_tensor_tensor(out=dst[:, t, 512 * h:512 * h + 512],
                                                     in0=ps[2 + t][:, 512 * h:512 * h + 512],
                                                     scalar=comb[:, t, bass.ds(e, 1)],
                                                     in1=dst[:, t, 512 * h:512 * h + 512], op0=ALU.mult, op1=ALU.add)
                ins.then_inc(down_free, 1)
                dve.wait_ge(down_free, n_prev + 2)

            def hidden1(n, par, wait_pd):
                dve.wait_ge(PD, wait_pd)
                dve.wait_ge(gate_free, n + 1)
                v.tensor_tensor(out=Hb[:, par], in0=ps[1], in1=SG, op=ALU.mult).then_inc(sem("hidden_ready"), 1)

            dve.sem_inc(down_free, 1)
            hidden1(0, 0, n_s1 + 2)
            with dve.Fori(0, (n1_exp - 2) // 2) as i:
                for k in range(2):
                    hidden1(2 * i + (1 + k), (1 + k) % 2, 6 * i + (n_s1 + 2 + 3 * k + 2))
                    add_down(2 * i + k, 2 * i + k, X, 6 * i + (n_s1 + 2 + 3 * k + 3), False)
            hidden1(n1_exp - 1, 1, n_s1 + 3 * n1_exp - 2)
            add_down(n1_exp - 2, n1_exp - 2, X, n_s1 + 3 * n1_exp - 1, False)
            add_down(n1_exp - 1, n1_exp - 1, X, n_s1 + 3 * n1_exp, False)
            flag("moe1_added")
            for h in range(2):
                products(f"pp{h}")
                dve.wait_ge(pair_free[steps[f"pg{h}"] % 2], steps[f"pg{h}"] // 2 + 1)
                freed(v.tensor_tensor(out=sg, in0=two(f"pp{h}"), in1=sg, op=ALU.mult), f"pp{h}")
                link(v.tensor_tensor(out=halves(X, h), in0=halves(X, h), in1=sg, op=ALU.add), "ple_added")
            dve.wait_ge(sem("p_loaded"), 16 * n_p)
            scale_rows(X, src=X)
            link(v.tensor_tensor(out=X, in0=X, in1=growB.unsqueeze(1).broadcast_to([P, 2, D]), op=ALU.mult), "x2_ready")
            scale_rows(XN, src=X)
            flag("xn2_ready")
            for i in range(12):
                products(f"md{i}")
                part, h = i // 2, i % 2
                if part in (2, 5):
                    dst = G12[:, part // 3, 512 * h:512 * h + 512]
                    freed(v.tensor_tensor(out=dst, in0=pair(f"md{i}")[:, 0:512], in1=dst, op=ALU.add), f"md{i}")
                else:
                    c0 = 8 * (part if part < 2 else part - 1) + 4 * h
                    freed(v.tensor_tensor(out=modT[:, c0:c0 + 4], in0=pair(f"md{i}")[:, 0:4],
                                          in1=VT[:, 92 + c0:96 + c0], op=ALU.add), f"md{i}")
            link(v.scalar_tensor_tensor(out=modT[:, 8:16], in0=modT[:, 8:16], scalar=1.0, in1=VT[:, 16:24],
                                        op0=ALU.add, op1=ALU.mult))
            link(v.scalar_tensor_tensor(out=modT[:, 24:32], in0=modT[:, 24:32], scalar=1.0, in1=VT[:, 24:32],
                                        op0=ALU.add, op1=ALU.mult))
            scaled_T(("nt0", "nt1"), modT[:, 8:16], modT[:, 0:8], "xT2_ready")
            l4 = lamv.rearrange("p (a b d) -> p a b d", a=2, b=2)
            link(v.tensor_tensor(out=l4[:, :, 0], in0=l4[:, :, 0], in1=l4[:, :, 1], op=ALU.mult))
            link(v.tensor_reduce(out=lam_s[:, 0:2], in_=l4[:, :, 0], axis=AX.X, op=ALU.add), "lambda_sums")
            dve.wait_ge(pair_free[steps["kc"] % 2], steps["kc"] // 2 + 1)
            for j in range(2):
                for h in range(2):
                    for r in range(2):
                        src = kraw[64 * h:64 * h + 64, j]
                        pos = VT2[64 * r:64 * r + 64, 16 * j:16 * j + 16]
                        for half in range(2):
                            win = src[:, 16 * half:16 * half + 240].rearrange("p (c m r) -> p m c r", m=8, r=2)[:, :, :, r]
                            dst = kexp[64 * r:64 * r + 64, j, 8 * half:8 * half + 8, h, :]
                            link(v.tensor_copy(dst, win))
                            link(v.tensor_tensor(out=dst, in0=dst,
                                                 in1=pos[:, 8 * half:8 * half + 8].unsqueeze(2).broadcast_to([64, 8, 15]),
                                                 op=ALU.add))
            flag("windows_ready")
            products("cc")
            link(v.tensor_scalar(kcmp, pair("cc")[:, 0:30], cb2T, None, ALU.add))
            freed(v.tensor_tensor(out=vcmp[0:15, :, :], in0=pair("cc")[0:15, 512:640].rearrange("p (h n) -> p h n", h=2),
                                  in1=cb2[0:15, 64:128].unsqueeze(1).broadcast_to([15, 2, 64]), op=ALU.add), "cc")
            dve.wait_ge(sem("lambda_exp"), 1)
            link(v.tensor_tensor(out=lam_s[:, 4:5], in0=lam_s[:, 1:2], in1=lam_s[:, 0:1], op=ALU.subtract))
            link(v.tensor_scalar(lam_s[:, 4:5], lam_s[:, 4:5], -0.2, None, ALU.add))
            attention(n_att1, len(chunks))
            o8 = Ob.rearrange("p t (h n) -> p (t h) n", n=P)
            sq = MRG.rearrange("p t n -> p (t n)")[:, 0:1024].rearrange("p (t n) -> p t n", n=P)
            link(v.tensor_tensor(out=sq, in0=o8, in1=o8, op=ALU.mult))
            link(v.tensor_reduce(out=ss_s[:, 0:8], in_=sq, axis=AX.X, op=ALU.add), "diff_squares")
            dve.wait_ge(sem("diff_rms"), 1)
            link(v.reciprocal(ss_s[:, 0:8], ss_s[:, 0:8]))
            link(v.tensor_scalar(ss_s[:, 0:8], ss_s[:, 0:8], 0.8, None, ALU.mult))
            link(v.tensor_tensor(out=o8, in0=o8, in1=ss_s[:, 0:8].unsqueeze(2).broadcast_to([P, 8, P]), op=ALU.mult))
            link(v.tensor_tensor(out=o8, in0=o8, in1=sub_g.unsqueeze(1).broadcast_to([P, 8, P]), op=ALU.mult),
                 "branches_ready")
            for b in range(3):
                products(f"bt{b}")
                freed(v.tensor_copy(hT3[b], pair(f"bt{b}")), f"bt{b}")
                for h in range(2):
                    products(f"y{b}{h}")
                    dve.wait_ge(pair_free[steps[f"g{b}{h}"] % 2], steps[f"g{b}{h}"] // 2 + 1)
                    if b == 0:
                        freed(v.tensor_tensor(out=halves(MRG, h), in0=two(f"y{b}{h}"), in1=sg2, op=ALU.mult), f"y{b}{h}")
                        flag("merged2")
                    else:
                        freed(v.tensor_tensor(out=sg2, in0=two(f"y{b}{h}"), in1=sg2, op=ALU.mult), f"y{b}{h}")
                        link(v.tensor_tensor(out=halves(MRG, h), in0=halves(MRG, h), in1=sg2, op=ALU.add), "merged2")
            for h in range(2):
                products(f"no{h}")
                g1 = G12[:, 0, 512 * h:512 * h + 512].unsqueeze(1).broadcast_to([P, 2, 512])
                freed(v.tensor_tensor(out=halves(MRG, h), in0=two(f"no{h}"), in1=g1, op=ALU.mult), f"no{h}")
                link(v.tensor_tensor(out=halves(X, h), in0=halves(X, h), in1=halves(MRG, h), op=ALU.add))
            flag("resid2_ready")
            scale_rows(XN, src=X)
            flag("h3n_ready")
            scaled_T(("h20", "h21"), modT[:, 24:32], modT[:, 16:24], "h3_ready")
            products("rt2")
            lg2 = rt_s[:, 128:192].rearrange("p (t n) -> p t n", t=2)
            freed(v.tensor_tensor(out=lg2, in0=pair("rt2").rearrange("p (t n) -> p t n", t=2)[:, :, 0:32],
                                  in1=rb2.unsqueeze(1).broadcast_to([P, 2, 32]), op=ALU.add), "rt2")
            for t in range(2):
                link(v.max(out=m8, in_=lg2[:, t]))
                link(v.max_index(out=i8, in_max=m8, in_values=lg2[:, t]))
                link(v.tensor_copy(f8, i8))
                link(v.tensor_scalar(w8[:, 4 * t:4 * t + 4], m8[:, 0:4], m8[:, 0:1], None, ALU.subtract), "route2_exp")
                dve.wait_ge(sem("route2_exped"), t + 1)
                link(v.reciprocal(rt_s[:, 224 + t:225 + t], rt_s[:, 224 + t:225 + t]))
                link(v.tensor_scalar(w8[:, 4 * t:4 * t + 4], w8[:, 4 * t:4 * t + 4], rt_s[:, 224 + t:225 + t], None, ALU.mult))
                for q in range(4):
                    dst = comb[:, t, :] if q == 0 else rt_s[:, 192:224]
                    link(v.tensor_scalar(dst, io32, f8[:, q:q + 1], w8[:, 4 * t + q:4 * t + q + 1], ALU.is_equal,
                                         ALU.mult))
                    if q:
                        link(v.tensor_tensor(out=comb[:, t, :], in0=comb[:, t, :], in1=dst, op=ALU.add))
            flag("comb2_ready")
            products("b1t")
            freed(v.tensor_copy(b1T, pair("b1t")[:, 0:512]), "b1t")
            products("ct")
            freed(v.tensor_copy(combT[0:32, :], pair("ct")[0:32, 0:256]), "ct")
            products("cb")
            for t in range(2):
                link(v.tensor_copy(ACC[:, t], ps[2 + t]))
            flag("acc_ready")
            dve.wait_ge(PD, done_value("cb"))
            dve.sem_inc(pair_free[steps["cb"] % 2], 1)

            def hidden2(n, par, e, half, wait_g, wait_hidden=True):
                dve.wait_ge(PD, wait_g)
                if wait_hidden:
                    dve.wait_ge(sem("gated_ready"), n)
                for f in range(4):
                    ins = v.tensor_scalar(GS[:, 256 * f:256 * f + 256], ps[0][:, 256 * f:256 * f + 256],
                                          b1T[:, bass.ds(e, 1), 4 * half + f], 7.0, ALU.add, ALU.min)
                ins.then_inc(sem("gate_limited"), 1)
                dve.wait_ge(PD, wait_g + 1)
                if wait_hidden:
                    dve.wait_ge(sem("hidden_ready"), n + n1_exp)
                for f in range(4):
                    ins = v.tensor_scalar(US[:, 256 * f:256 * f + 256], ps[1][:, 256 * f:256 * f + 256],
                                          b1T[:, bass.ds(e, 1), 8 + 4 * half + f], 7.0, ALU.add, ALU.min)
                ins.then_inc(up_free, 1)
                dve.wait_ge(up_free, n + 1)
                v.tensor_scalar(US, US, -7.0, 1.0, ALU.max, ALU.add).then_inc(sem("up_ready"), 1)
                dve.wait_ge(sem("up_ready"), n + 1)
                dve.wait_ge(sem("gated_ready"), n + 1)
                v.tensor_tensor(out=Hb[:, par], in0=US, in1=SG, op=ALU.mult).then_inc(sem("hidden_ready"), 1)

            base = len(seq) + 3 * n1_exp
            hidden2(0, 0, 0, 0, base + 1, False)
            with dve.Fori(0, (n2_exp - 2) // 2) as i:
                for k in range(2):
                    hidden2(2 * i + (1 + k), (1 + k) % 2, i + k, 1 - k, 6 * i + (base + 2 + 3 * k + 1))
                    add_down(2 * i + (k + n1_exp), i, ACC, 6 * i + (base + 2 + 3 * k + 3), False)
            hidden2(n2_exp - 1, 1, NE2 - 1, 1, base + 3 * n2_exp - 3)
            add_down(n1_exp + n2_exp - 2, NE2 - 1, ACC, base + 3 * n2_exp - 1, False)
            add_down(n1_exp + n2_exp - 1, NE2 - 1, ACC, base + 3 * n2_exp, False)
            link(v.tensor_tensor(out=ACC, in0=ACC, in1=G12[:, 1].unsqueeze(1).broadcast_to([P, 2, D]), op=ALU.mult))
            link(v.tensor_tensor(out=X, in0=X, in1=ACC, op=ALU.add), "moe2_added")
            dve.wait_ge(sem("last_gain_loaded"), 16)
            scale_rows(X, src=X)
            link(v.tensor_tensor(out=X, in0=X, in1=growF.unsqueeze(1).broadcast_to([P, 2, D]), op=ALU.mult), "out_ready")

        @block.tensor
        def _(pe):
            mm = nc.tensor.matmul

            def begin(name):
                m = steps[name]
                if m >= 2:
                    pe.wait_ge(pair_free[m % 2], m // 2)
                return ps[m % 2]

            def slot(j, nk, n=None):
                pe.wait_ge(slot_loaded[j % RING], uses_before(j))
                n = n or SLOT // nk
                return ring[:, (j % RING) * SLOT:(j % RING) * SLOT + nk * n].rearrange("p (t n) -> p t n", t=nk)

            def all_free(name):
                for q in range(2):
                    pe.wait_ge(pair_free[q], (steps[name] - q) // 2 + 1)

            def lin_T(name, w, xT, nct, nk=KD, c0=0, bias=None):
                out = begin(name).rearrange("p (c t) -> p c t", t=T)
                for ct in range(nct):
                    for k in range(nk):
                        ins = mm(out[:, ct], w[:, k, c0 + P * ct:c0 + P * ct + P], xT[:, k], start=(k == 0),
                                 stop=(k == nk - 1 and bias is None))
                    if bias is not None:
                        r, bc = bias
                        ins = mm(out[:, ct], brow[r:r + 1, bc + P * ct:bc + P * ct + P], ones[r:r + 1, 0:T],
                                 start=False, stop=True)
                ins.then_inc(PD, 1)

            def lin_N(name, w, xT, n, nk=KD, c0=0, bias=None):
                out = begin(name).rearrange("p (t n) -> p t n", t=NT)
                for t in range(NT):
                    for k in range(nk):
                        ins = mm(out[:, t, 0:n], xT[:, k, P * t:P * t + P], w[:, k, c0:c0 + n], start=(k == 0),
                                 stop=(k == nk - 1 and bias is None))
                    if bias is not None:
                        r, bc = bias
                        ins = mm(out[:, t, 0:n], ones[r:r + 1, 0:P], brow[r:r + 1, bc:bc + n], start=False, stop=True)
                ins.then_inc(PD, 1)

            def transposes(name, src, k0, n=4):
                out = begin(name).rearrange("p (c t) -> p c t", t=T)
                for k in range(n):
                    for t in range(NT):
                        ins = nc.tensor.transpose(out[:, k, P * t:P * t + P], src[:, t, P * (k0 + k):P * (k0 + k) + P],
                                                  ident)
                ins.then_inc(PD, 1)

            def attention(c0, c1):
                def scores(c):
                    kind, _, qt, hc, w = chunks[c]
                    nk = 15 if kind == "cmp" else P * (qt + 1)
                    if c >= c0 + 2:
                        pe.wait_ge(sem("scores_biased"), c - 1)
                    for h in range(4):
                        q, k = map_operands(kind, 4 * hc + h)
                        ins = mm(ps[c % 2][:, score_col(h):score_col(h) + nk], q[:, P * qt:P * qt + P], k[:, 0:nk], start=True,
                                 stop=True)
                    ins.then_inc(sem("scores_done"), 1)

                scores(c0)
                for c in range(c0, c1):
                    if c + 1 < c1:
                        scores(c + 1)
                    kind, _, qt, hc, w = chunks[c]
                    cmp = kind == "cmp"
                    nt = 1 if cmp else qt + 1
                    rows = 15 if cmp else P
                    pe.wait_ge(sem("probs_ready"), c + 1)
                    if c:
                        pe.wait_ge(sem("probsT_ready"), c)
                    for m in range(4 * nt):
                        h, kt = m // nt, m % nt
                        ins = nc.tensor.transpose(ps[2][0:rows, P * m:P * m + P],
                                                  SC[:, c % 2, h, P * kt:P * kt + rows], ident)
                    ins.then_inc(sem("probs_transposed"), 1)
                    pe.wait_ge(sem("probsT_ready"), c + 1)
                    if c >= 2:
                        pe.wait_ge(sem("outputs_scaled"), c - 1)
                    for h in range(4):
                        for kt in range(nt):
                            ins = mm(ps[3][:, 512 * (c % 2) + w * h:512 * (c % 2) + w * h + w],
                                     PT[0:rows, c % 2, h * nt + kt], map_values(kind, 4 * hc + h, kt),
                                     start=(kt == 0), stop=(kt == nt - 1))
                    ins.then_inc(sem("outputs_done"), 1)

            pe.wait_ge(sem("constants_ready"), 1)
            pe.wait_ge(sem("vectors_loaded"), 16 * n_vec)
            vr = XT.rearrange("p k t -> p (k t)")
            begin("vec")
            nc.tensor.transpose(ps[0][:, 0:P], vr[:, 0:P], ident)
            nc.tensor.transpose(ps[0][:, P:P + 40], vr[0:40, P:2 * P], ident[0:40, 0:40]).then_inc(PD, 1)
            pe.wait_ge(sem("xn_ready"), 1)
            transposes("xt0", XN, 0)
            transposes("xt1", XN, 4)
            pe.wait_ge(sem("xT_ready"), 1)
            I = item_at
            lin_T("q", slot(I["q"], KD), XT, 4)
            lin_T("k", slot(I["k"], KD), XT, 4)
            lin_N("v", slot(I["v"], KD), XT, 512)
            for h in range(2):
                lin_N(f"z{h}", slot(I[f"z{h}"], KD), XT, 512)
            for h in range(3):
                lin_T(f"x{h}", slot(I[f"x{h}"], KD), XT, 4)
            pe.wait_ge(sem("small_loaded"), 16 * n_small)
            lin_N("dt", wdt, XT, 16)
            all_free("dt")
            attention(0, n_att1)
            pe.wait_ge(sem("conv_ready"), 1)
            o = begin("G").rearrange("p (g s t) -> p g s t", g=2, s=2)
            for g in range(2):
                for s_ in range(2):
                    ins = mm(o[:, g, s_], cvT[:, 8 + g, P * s_:P * s_ + P], cvT[:, 10 + g], start=True, stop=True)
            ins.then_inc(PD, 1)
            for k in range(4):
                o = begin(f"xsT{k}")[:, 0:512].rearrange("p (t n) -> p t n", t=2)
                for t in range(2):
                    for c in range(2):
                        ins = nc.tensor.transpose(o[:, t, P * c:P * c + P], cvT[:, 2 * k + c, P * t:P * t + P], ident)
                ins.then_inc(PD, 1)
            pe.wait_ge(sem("da_ready"), 1)
            da = ssd_small[:, 0:32]
            o = begin("cs")
            mm(o[:, 0:16], U[:, 0, 0:P], da[:, 0:16], start=True, stop=True)
            mm(o[:, 16:32], U[:, 0, P:T], da[:, 0:16], start=True, stop=False)
            mm(o[:, 16:32], U[:, 1, P:T], da[:, 16:32], start=False, stop=True).then_inc(PD, 1)

            def cum_rows(g):
                o = begin(f"cb{g}")
                for h in range(4):
                    for kt in range(2):
                        col = 16 * kt + 4 * g + h
                        ins = mm(o[:, 256 * h:256 * h + 256], da[:, col:col + 1].broadcast_to([P, P]), U[:, kt],
                                 start=(kt == 0), stop=(kt == 1))
                ins.then_inc(PD, 1)

            def ssd_heads(g):
                pe.wait_ge(sem("decay_ready"), g + 1)
                for h in range(4):
                    hh = 4 * g + h
                    c = slice(64 * hh, 64 * hh + 64)
                    m = Mt[:, g % 2, h]
                    mm(ps[2][:, c], m[:, 0:P], xdt[:, 0, c], start=True, stop=True)
                    mm(ps[3][:, c], m[:, P:T], xdt[:, 0, c], start=True, stop=False)
                    ins = mm(ps[3][:, c], m[:, T:T + P], xdt[:, 1, c], start=False, stop=True)
                ins.then_inc(sem("ssd_heads_done"), 1)

            pe.wait_ge(sem("xdt_ready"), 1)
            pe.wait_ge(sem("outputs_scaled"), n_att1)
            for g in range(4):
                cum_rows(g)
                if g:
                    ssd_heads(g - 1)
            ssd_heads(3)
            transposes("ot1", O1, 0)
            pe.wait_ge(pair_free[steps["ot1"] % 2], steps["ot1"] // 2 + 1)
            for h in range(2):
                lin_N(f"a{h}", slot(I["woa"], 4), OT, 512, nk=4, c0=512 * h)
                lin_N(f"ga{h}", slot(I[f"ga{h}"], KD), XT, 512)
            pe.wait_ge(sem("y_ready"), 1)
            transposes("yt0", Y, 0)
            transposes("yt1", Y, 4)
            pe.wait_ge(pair_free[steps["yt0"] % 2], steps["yt0"] // 2 + 1)
            pe.wait_ge(pair_free[steps["yt1"] % 2], steps["yt1"] // 2 + 1)
            for h in range(2):
                lin_N(f"b{h}", slot(I[f"wob{h}"], KD), AT, 512)
                lin_N(f"gb{h}", slot(I[f"gb{h}"], KD), XT, 512)
            pe.wait_ge(sem("merged"), 4)
            for h in range(2):
                transposes(f"mt{h}", MRG, 4 * h)
            for h in range(2):
                pe.wait_ge(pair_free[steps[f"mt{h}"] % 2], steps[f"mt{h}"] // 2 + 1)
            for h in range(2):
                lin_N(f"wo{h}", slot(I[f"wo{h}"], KD), AT, 512)
            pe.wait_ge(sem("h2n_ready"), 1)
            transposes("ht0", XN, 0)
            transposes("ht1", XN, 4)
            pe.wait_ge(sem("h2_ready"), 1)
            lin_N("rt1", wr1, XT, 20)
            all_free("rt1")

            def half_up(slot_n, load_value, dst, free_sem, free_value):
                pe.wait_ge(slot_loaded[slot_n], load_value)
                if free_sem is not None:
                    pe.wait_ge(free_sem, free_value)
                w = ring[:, slot_n * SLOT:(slot_n + 1) * SLOT].rearrange("p (t n) -> p t n", t=KD)
                for f in range(4):
                    for k in range(KD):
                        ins = mm(dst[:, 256 * f:256 * f + 256], w[:, k, P * f:P * f + P], XT[:, k], start=(k == 0),
                                 stop=(k == KD - 1))
                ins.then_inc(PD, 1)

            def half_down(slot_n, load_value, par, hidden_value, free_value):
                pe.wait_ge(slot_loaded[slot_n], load_value)
                pe.wait_ge(sem("hidden_ready"), hidden_value)
                if free_value is not None:
                    pe.wait_ge(down_free, free_value)
                w = ring[:, slot_n * SLOT:(slot_n + 1) * SLOT].rearrange("p (t n) -> p t n", t=4)
                for t in range(NT):
                    for h in range(2):
                        for f in range(4):
                            ins = mm(ps[2 + t][:, 512 * h:512 * h + 512], Hb[:, par, f, P * t:P * t + P],
                                     w[:, f, 512 * h:512 * h + 512], start=(f == 0), stop=(f == 3))
                ins.then_inc(PD, 1)

            def experts(j0, n_half, hid0, gate_sem, gate0, up_sem, up0):
                def load_at(j):
                    return uses_before(j)

                half_up(j0 % RING, load_at(j0), ps[0], None, None)
                half_up((j0 + 1) % RING, load_at(j0 + 1), ps[1], None, None)
                jb = j0 + 2
                with pe.Fori(0, (n_half - 2) // 2) as i:
                    for k in range(2):
                        ja = jb + 3 * k
                        half_up(ja % RING, 16 * i + load_at(ja), ps[0], gate_sem, 2 * i + (gate0 + 1 + k))
                        half_up((ja + 1) % RING, 16 * i + load_at(ja + 1), ps[1], up_sem, 2 * i + (up0 + 1 + k))
                        half_down((ja + 2) % RING, 16 * i + load_at(ja + 2), k, 2 * i + (hid0 + 1 + k),
                                  2 * i + (hid0 + k + 1))
                jc = jb + 3 * (n_half - 2)
                half_up(jc % RING, load_at(jc), ps[0], gate_sem, gate0 + n_half - 1)
                half_up((jc + 1) % RING, load_at(jc + 1), ps[1], up_sem, up0 + n_half - 1)
                half_down((jc + 2) % RING, load_at(jc + 2), 0, hid0 + n_half - 1, hid0 + n_half - 1)
                half_down((jc + 3) % RING, load_at(jc + 3), 1, hid0 + n_half, hid0 + n_half)

            experts(n_front1, n1_exp, 0, gate_free, 0, sem("hidden_ready"), 0)
            J = {k: base_mid + n for k, n in after1.items()}
            pe.wait_ge(sem("moe1_added"), 1)
            transposes("p0", X, 0)
            transposes("p1", X, 4)
            pe.wait_ge(sem("p_loaded"), 16 * n_p)
            transposes("ptr", pin, 0, n=2)
            for nm in ("p0", "p1", "ptr"):
                pe.wait_ge(pair_free[steps[nm] % 2], steps[nm] // 2 + 1)
            for h in range(2):
                lin_N(f"pg{h}", slot(J[f"pg{h}"], KD), XT, 512)
                lin_N(f"pp{h}", slot(J["pp"], 2, 1024), pT, 512, nk=2, c0=512 * h)
            cT = VT2[:, 32:40]
            for i in range(12):
                w = slot(J[f"mod{i}"], KD)
                o = begin(f"md{i}")
                if i // 2 in (2, 5):
                    for k in range(KD):
                        ins = mm(o[:, 0:512], cT[:, k:k + 1].broadcast_to([P, P]), w[:, k], start=(k == 0),
                                 stop=(k == KD - 1))
                else:
                    for ct in range(4):
                        for k in range(KD):
                            ins = mm(o[:, ct:ct + 1], w[:, k, P * ct:P * ct + P], cT[:, k:k + 1], start=(k == 0),
                                     stop=(k == KD - 1))
                ins.then_inc(PD, 1)
            pe.wait_ge(sem("xn2_ready"), 1)
            transposes("nt0", XN, 0)
            transposes("nt1", XN, 4)
            pe.wait_ge(sem("xT2_ready"), 1)

            def seg(s_, off=0):
                return 32 * (s_ % 4), 512 * (s_ // 4) + off

            lin_T("qa", slot(J["qa"], KD), XT, 4, bias=seg(0))
            wk = slot(J["kva"], KD, 256)
            lin_T("ka", wk, XT, 1, bias=seg(1))
            lin_N("va", wk, XT, 128, c0=128, bias=seg(1, 128))
            lin_T("qb", slot(J["qb"], KD), XT, 4, bias=seg(2))
            lin_T("kb", slot(J["kb"], KD), XT, 4, bias=seg(3))
            lin_N("vb", slot(J["vb"], KD), XT, 512, bias=seg(4))
            lin_T("qc", slot(J["qc"], KD), XT, 4, bias=seg(5))
            wk = slot(J["kvc"], KD)
            lin_T("kc", wk, XT, 2, bias=seg(6))
            lin_T("ksl", wk, XT, 1, c0=256, bias=seg(6, 256))
            lin_N("vsl", wk, XT, 128, c0=384, bias=seg(6, 384))
            wk = slot(J["kvw"], KD, 256)
            lin_T("kwn", wk, XT, 1, bias=seg(7))
            lin_N("vwn", wk, XT, 128, c0=128, bias=seg(7, 128))
            lin_N("gn", wgn, XT, 24, bias=seg(8))
            pe.wait_ge(sem("windows_ready"), 1)
            for j in range(2):
                w = slot(J[f"cw{j}"], 16)
                o = begin(f"c{j}")
                for m in range(2):
                    for l in range(16):
                        ins = mm(o[:, 30 * m:30 * m + 30], w[:, l, P * m:P * m + P],
                                 kexp[:, j, l].rearrange("p h c -> p (h c)"), start=(l == 0), stop=(l == 15))
                ins.then_inc(PD, 1)
            for j in range(2):
                pe.wait_ge(pair_free[steps[f"c{j}"] % 2], steps[f"c{j}"] // 2 + 1)
            o = begin("cc")
            for half in range(2):
                for m in range(2):
                    mm(o[64 * half:64 * half + 64, 0:30], cw2[:, 0, m], hid[:, 0, m], start=(m == 0), stop=(m == 1))
            for h in range(2):
                for m in range(2):
                    ins = mm(o[0:15, 512 + 64 * h:576 + 64 * h], hid[:, 1, m, 15 * h:15 * h + 15], cw2[:, 1, m],
                             start=(m == 0), stop=(m == 1))
            ins.then_inc(PD, 1)
            all_free("cc")
            attention(n_att1, len(chunks))
            pe.wait_ge(sem("branches_ready"), 1)
            for b, o_ in enumerate((Oa, Ob, Oc)):
                transposes(f"bt{b}", o_, 0)
                pe.wait_ge(pair_free[steps[f"bt{b}"] % 2], steps[f"bt{b}"] // 2 + 1)
                for h in range(2):
                    lin_N(f"y{b}{h}", slot(J[f"wb{b}"], 4), hT3[b], 512, nk=4, c0=512 * h)
                    lin_N(f"g{b}{h}", slot(J[f"gm{b}{h}"], KD), XT, 512, bias=seg(9 + 2 * b + h))
            pe.wait_ge(sem("merged2"), 6)
            for h in range(2):
                transposes(f"nt{h + 2}", MRG, 4 * h)
            for h in range(2):
                pe.wait_ge(pair_free[steps[f"nt{h + 2}"] % 2], steps[f"nt{h + 2}"] // 2 + 1)
            for h in range(2):
                lin_N(f"no{h}", slot(J[f"w2o{h}"], KD), AT, 512)
            pe.wait_ge(sem("h3n_ready"), 1)
            transposes("h20", XN, 0)
            transposes("h21", XN, 4)
            pe.wait_ge(sem("h3_ready"), 1)
            lin_N("rt2", wr2, XT, 32)
            pe.wait_ge(sem("b_loaded"), 32)
            o = begin("b1t")
            for c in range(4):
                ins = nc.tensor.transpose(o[:, P * c:P * c + P], b1R[:, c], ident)
            ins.then_inc(PD, 1)
            pe.wait_ge(sem("comb2_ready"), 1)
            o = begin("ct")
            for t in range(2):
                ins = nc.tensor.transpose(o[0:32, P * t:P * t + P], comb[:, t], ident)
            ins.then_inc(PD, 1)
            pe.wait_ge(pair_free[steps["ct"] % 2], steps["ct"] // 2 + 1)
            begin("cb")
            for t in range(2):
                for h in range(2):
                    ins = mm(ps[2 + t][:, 512 * h:512 * h + 512], combT[0:32, P * t:P * t + P],
                             b2R[0:32, 512 * h:512 * h + 512], start=True, stop=True)
            ins.then_inc(PD, 1)
            pe.wait_ge(sem("acc_ready"), 1)
            all_free("cb")
            experts(base_exp2, n2_exp, n1_exp, sem("gate_limited"), 0, up_free, 0)


_OUT = (1, T, D)
_INPUTS = ["x", "p", "mix_norm_g", "w_in", "conv_w", "conv_b", "dt_bias", "a_log", "d_skip", "ssd_norm_g", "w_out_a",
           "w_out_b", "w_out", "ffn_norm_g", "w_rg", "b_rg", "w_re", "b_re", "w_gate", "w_up", "w_down", "w_ple_proj",
           "w_ple_gate", "final_norm_g", "c_2", "mod_w_2", "mod_b_2", "norm1_g_2", "norm2_g_2", "w_in_2", "b_in_2",
           "sinks_2", "diff_lambda_2", "diff_subln_g_2", "cmp_pos_2", "cmp_w1_2", "cmp_b1_2", "cmp_w2_2", "cmp_b2_2",
           "w_branch_2", "w_out_2", "router_w_2", "router_b_2", "exp_w1_2", "exp_b1_2", "exp_w2_2", "exp_b2_2",
           "final_g_2"]


def kernel(**inputs):
    import concourse.bacc as bacc
    from concourse import mybir
    from concourse.bass_utils import run_bass_kernel_spmd

    nc = bacc.Bacc("TRN2", target_bir_lowering=False, num_devices=1)
    arrays, aps = {}, {}
    for name in _INPUTS:
        arr = np.ascontiguousarray(inputs[name])
        arrays[name] = arr
        aps[name] = nc.dram_tensor(name, arr.shape, mybir.dt.from_np(arr.dtype), kind="ExternalInput").ap()
    aps["out"] = nc.dram_tensor("out", _OUT, mybir.dt.float32, kind="ExternalOutput").ap()
    build(nc, aps)
    r = run_bass_kernel_spmd(nc, [arrays], core_ids=[0])
    return r.results[0]["out"]
```

```python
from contextlib import ExitStack

import numpy as np

P = 128
T = 256
NT = T // P
D = 1024
KD = D // P
RING = 6
SLOT = 4096
BIG = 1e30
R_BIG = 12484


def layouts():
    w1 = dict(q=0, k=512, v=1024, z=1536, xbc=2560, dt=4096, ga=4112, gb=5136)
    w2 = dict(qa=0, kva=512, qb=768, kb=1280, vb=1792, qc=2304, kvc=2816, kvw=3328, gn=3584, gm=3608)
    return w1, w2


def build(nc, a):
    import concourse.bass as bass
    from concourse import mybir
    from concourse.alu_op_type import AluOpType as ALU

    F32 = mybir.dt.float32
    U32 = mybir.dt.uint32
    ACT = mybir.ActivationFunctionType
    AX = mybir.AxisListType
    W1, W2 = layouts()
    NE1, NE2 = 16, 32
    ctx = ExitStack()
    with ctx:
        sems = {}

        def sem(name):
            if name not in sems:
                sems[name] = ctx.enter_context(nc.semaphore(name))
            return sems[name]

        def sb(name, cols, dt=F32, parts=P):
            return ctx.enter_context(nc.sbuf_tensor(name, [parts, cols], dt))[:, :]

        ring = sb("ring", RING * SLOT)
        X = sb("x_resid", NT * D).rearrange("p (t n) -> p t n", t=NT)
        XT = sb("x_T", KD * T).rearrange("p (k t) -> p k t", k=KD)
        r_mix = sb("r_mix", 2048)
        XN = r_mix.rearrange("p (t n) -> p t n", t=NT)
        SC = r_mix.rearrange("p (b h k) -> p b h k", b=2, h=4)
        MRG = XN
        r_at = sb("r_at", 2048)
        PT = r_at.rearrange("p (b m q) -> p b m q", b=2, m=8)
        AT = r_at.rearrange("p (k t) -> p k t", k=KD)
        ident = sb("ident", P)
        DM = sb("dist_causal", 512).rearrange("p (t k) -> p t k", t=2)
        DMW = sb("dist_window", 512).rearrange("p (t k) -> p t k", t=2)
        r_u = sb("r_u", 2048)
        U = r_u[:, 0:512].rearrange("p (t k) -> p t k", t=2)
        MK = r_u[:, 512:1024].rearrange("p (t k) -> p t k", t=2)
        GT = r_u[:, 1024:2048].rearrange("p (g s t) -> p g s t", g=2, s=2)
        brow = r_u
        CV = sb("cmp_valid", 30).rearrange("p (t k) -> p t k", t=2)
        CM = sb("cmp_mask", 30).rearrange("p (t k) -> p t k", t=2)
        iota = sb("iota", P)
        io32 = iota[:, 0:32]
        ones = sb("ones", 256)
        VT = sb("vec_T", P)
        VT2 = sb("vec_T2", 40)
        modT = sb("mod_T", 32)
        eps = sb("eps", 2)
        dtb, alog, dsk = sb("dt_bias_b", 16), sb("a_log_b", 16), sb("d_skip_b", 16)
        rb1, rb2 = sb("router_bias1", 20), sb("router_bias2", 32)
        snk, nsnk = sb("sinks_b", 8), sb("neg_sinks_b", 8)
        lamv = sb("lambda_b", 256)
        sub_g = sb("subln_b", P)
        cb2 = sb("cmp_b2_b", 64)
        cb2T = sb("cmp_b2_T", 1)
        cw2 = sb("cmp_w2", 4 * 64).rearrange("p (j k n) -> p j k n", j=2, k=2)
        wr1 = sb("router_w1", KD * 20).rearrange("p (k n) -> p k n", k=KD)
        wr2 = sb("router_w2", KD * 32).rearrange("p (k n) -> p k n", k=KD)
        r_wsm = sb("w_small", KD * 24)
        wdt = r_wsm[:, 0:KD * 16].rearrange("p (k n) -> p k n", k=KD)
        wgn = r_wsm.rearrange("p (k n) -> p k n", k=KD)
        st = sb("stats", 84)
        rt_s = sb("route", 228)
        comb0 = sb("combine", NT * 33).rearrange("p (t e) -> p t e", t=NT)
        comb = comb0[:, :, 1:33]
        rank = sb("rank", NT * 33).rearrange("p (t e) -> p t e", t=NT)
        sizes = sb("sizes", 34, mybir.dt.int32)
        r_big = sb("r_big", R_BIG)
        used = [0]

        def take(n):
            used[0] += n
            assert used[0] <= R_BIG, used[0]
            return r_big[:, used[0] - n:used[0]]

        qT = take(1024).rearrange("p (c t) -> p c t", c=4)
        kT = take(1024).rearrange("p (c t) -> p c t", c=4)
        v1 = take(1024).rearrange("p (t n) -> p t n", t=2)
        O1 = take(1024).rearrange("p (t n) -> p t n", t=2)
        silz = take(2048).rearrange("p (t n) -> p t n", t=2)
        xbcP = take(12 * 259).rearrange("p (c t) -> p c t", c=12)
        cvT = take(3072).rearrange("p (c t) -> p c t", c=12)
        ssd_small = take(5 * 32)
        xs = r_big[:, 0:2048].rearrange("p (t n) -> p t n", t=2)
        xdt = XN
        Y = xbcP.rearrange("p c t -> p (c t)")[:, 0:2048].rearrange("p (t n) -> p t n", t=2)
        Mt = cvT.rearrange("p c t -> p (c t)").rearrange("p (b h n) -> p b h n", b=2, h=4)
        OT = r_big[:, 2048:3072].rearrange("p (c t) -> p c t", c=4)
        sg = r_big[:, 3072:4096].rearrange("p (t n) -> p t n", t=2)
        pin = r_big[:, 0:512].rearrange("p (t n) -> p t n", t=2)
        pT = r_big[:, 512:1024].rearrange("p (c t) -> p c t", c=2)
        growB = r_big[:, 4096:5120]
        used1 = used[0]
        used[0] = 5120
        Hb = take(2048).rearrange("p (b f t) -> p b f t", b=2, f=4)
        GS = take(1024)
        US = take(1024)
        SG = take(1024)
        ACC = take(2048).rearrange("p (t n) -> p t n", t=2)
        b1T = r_big[:, 0:512].rearrange("p (e f) -> p e f", e=32)
        b1R = r_big[:, 512:1024].rearrange("p (c n) -> p c n", c=4)
        b2R = r_big[:, 1024:2048]
        combT = r_big[:, 2048:2304]
        pick = r_big[:, 3072:3584].rearrange("p (b t s) -> p b t s", b=2, t=NT)
        tri = r_big[:, 3072:3584].rearrange("p (t k) -> p t k", t=NT)
        pickT = r_big[:, 3584:3840]
        YS = r_at[:, 0:1024]
        XG = r_at[:, 1024:2048].rearrange("p (k s) -> p k s", k=KD)
        HT = XN
        used[0] = 0
        qa = take(1024).rearrange("p (c t) -> p c t", c=4)
        qb = take(1024).rearrange("p (c t) -> p c t", c=4)
        kb = take(1024).rearrange("p (c t) -> p c t", c=4)
        vb = take(1024).rearrange("p (t n) -> p t n", t=2)
        qc = take(1024).rearrange("p (c t) -> p c t", c=4)
        ka = take(512).rearrange("p (h t) -> p h t", h=2)
        ksl = take(512).rearrange("p (h t) -> p h t", h=2)
        kwn = take(512).rearrange("p (h t) -> p h t", h=2)
        va = take(256).rearrange("p (t n) -> p t n", t=2)
        vsl = take(256).rearrange("p (t n) -> p t n", t=2)
        vwn = take(256).rearrange("p (t n) -> p t n", t=2)
        kraw = take(512).rearrange("p (j t) -> p j t", j=2)
        kexp = take(960).rearrange("p (j l h c) -> p j l h c", j=2, l=16, h=2)
        hid = take(120).rearrange("p (j m c) -> p j m c", j=2, m=2)
        kcmp = take(30).rearrange("p (h c) -> p h c", h=2)
        vcmp = take(128).rearrange("p (h n) -> p h n", h=2)
        gts = take(48).rearrange("p (t n) -> p t n", t=2)
        Oa = take(1024).rearrange("p (t n) -> p t n", t=2)
        Ob = take(1024).rearrange("p (t n) -> p t n", t=2)
        Oc = take(1024).rearrange("p (t n) -> p t n", t=2)
        tmpO = kraw.rearrange("p j t -> p (j t)")
        hT3 = [x for x in (qb, kb, qc)]
        sg2 = qa.rearrange("p c t -> p (c t)").rearrange("p (t n) -> p t n", t=2)
        G12 = sb("mod_gates", 2048).rearrange("p (g n) -> p g n", g=2)

        growA = G12[:, 0]
        growF = r_u[:, 0:1024]

        ps = [ctx.enter_context(nc.psum_tensor(f"pair{i}", [P, 1024], F32))[:, :] for i in range(4)]

        def blk(w, r0, nk, c0, n):
            return w[r0:r0 + nk * P, c0:c0 + n].rearrange("(t p) n -> p t n", p=P)

        items, item_at = [], {}

        def item(name, w, r0, nk, c0, n):
            item_at[name] = len(items)
            items.append((blk(w, r0, nk, c0, n), nk, n))

        w_in, w_in2 = a["w_in"][0], a["w_in_2"][0]
        for nm, c0 in (("q", W1["q"]), ("k", W1["k"]), ("v", W1["v"]), ("z0", W1["z"]), ("z1", W1["z"] + 512),
                       ("x0", W1["xbc"]), ("x1", W1["xbc"] + 512), ("x2", W1["xbc"] + 1024)):
            item(nm, w_in, 0, KD, c0, 512)
        item("woa", a["w_out_a"][0], 0, 4, 0, 1024)
        item("ga0", w_in, 0, KD, W1["ga"], 512)
        item("ga1", w_in, 0, KD, W1["ga"] + 512, 512)
        for h in range(2):
            item(f"wob{h}", a["w_out_b"][0], 0, KD, 512 * h, 512)
            item(f"gb{h}", w_in, 0, KD, W1["gb"] + 512 * h, 512)
        for h in range(2):
            item(f"wo{h}", a["w_out"][0], 0, KD, 512 * h, 512)
        n_front1 = len(items)
        moe1_slot = n_front1 % RING
        front1 = list(items)
        items.clear()
        after1 = {}

        def item2(name, w, r0, nk, c0, n):
            after1[name] = len(items)
            items.append((blk(w, r0, nk, c0, n), nk, n))

        for h in range(2):
            item2(f"pg{h}", a["w_ple_gate"][0], 0, KD, 512 * h, 512)
        item2("pp", a["w_ple_proj"][0], 0, 2, 0, 1024)
        for i in range(12):
            item2(f"mod{i}", a["mod_w_2"][0], 0, KD, 512 * i, 512)
        for nm, c0, n in (("qa", W2["qa"], 512), ("kva", W2["kva"], 256), ("qb", W2["qb"], 512), ("kb", W2["kb"], 512),
                          ("vb", W2["vb"], 512), ("qc", W2["qc"], 512), ("kvc", W2["kvc"], 512),
                          ("kvw", W2["kvw"], 256)):
            item2(nm, w_in2, 0, KD, c0, n)
        for j in range(2):
            item2(f"cw{j}", a["cmp_w1_2"][0, j], 0, 16, 0, 256)
        for b in range(3):
            item2(f"wb{b}", a["w_branch_2"][0, b], 0, 4, 0, 1024)
            for h in range(2):
                item2(f"gm{b}{h}", w_in2, 0, KD, W2["gm"] + 1024 * b + 512 * h, 512)
        for h in range(2):
            item2(f"w2o{h}", a["w_out_2"][0], 0, KD, 512 * h, 512)
        front2 = list(items)
        n1_exp, n2_exp = NE1, 2 * NE2
        base_mid = n_front1 + 3 * n1_exp
        base_exp2 = base_mid + len(front2)

        steps = {}
        seq = []

        def step(name, *names):
            for nm in (name,) + names:
                steps[nm] = len(seq)
                seq.append(nm)

        step("vec", "xt0", "xt1", "q", "k", "v", "z0", "z1", "x0", "x1", "x2", "dt")
        step("G", "xsT0", "xsT1", "xsT2", "xsT3", "cs", "cb0", "cb1", "cb2", "cb3")
        step("ot1", "a0", "ga0", "a1", "ga1", "yt0", "yt1", "b0", "gb0", "b1", "gb1")
        step("mt0", "mt1", "wo0", "wo1", "ht0", "ht1", "rt1", "hb0", "hb1", "rk1")
        n_s1 = len(seq)
        step("p0", "p1", "ptr", "pg0", "pp0", "pg1", "pp1")
        step("md0", "md1", "md2", "md3", "md4", "md5", "md6", "md7", "md8", "md9", "md10", "md11")
        step("nt0", "nt1", "qa", "ka", "va", "qb", "kb", "vb", "qc", "kc", "ksl", "vsl", "kwn", "vwn", "gn")
        step("c0", "c1", "cc")
        for b in range(3):
            step(f"bt{b}", f"y{b}0", f"g{b}0", f"y{b}1", f"g{b}1")
        step("nt2", "nt3", "no0", "no1", "h20", "h21", "rt2", "hb2", "hb3", "rk2", "b1t", "ct", "cb")
        last_step_of_item = dict(q="q", k="k", v="v", z0="z0", z1="z1", x0="x0", x1="x1", x2="x2", woa="a1", ga0="ga0",
                                 ga1="ga1", wob0="b0", gb0="gb0", wob1="b1", gb1="gb1", wo0="wo0", wo1="wo1",
                                 pg0="pg0", pg1="pg1", pp="pp1", qa="qa", kva="va", qb="qb", kb="kb", vb="vb",
                                 qc="qc", kvc="vsl", kvw="vwn", cw0="c0", cw1="c1", w2o0="no0", w2o1="no1")
        for i in range(12):
            last_step_of_item[f"mod{i}"] = f"md{i}"
        for b in range(3):
            last_step_of_item[f"wb{b}"] = f"y{b}1"
            for h in range(2):
                last_step_of_item[f"gm{b}{h}"] = f"g{b}{h}"

        def done_value(name):
            n = steps[name] + 1
            return n if steps[name] < n_s1 else n + 3 * n1_exp

        base_pd2 = len(seq) + 3 * n1_exp
        PD = sem("products_done")
        pair_free = [sem("pair0_free"), sem("pair1_free")]
        gate_free, up_free = sem("gate_psum_free"), sem("up_psum_free")
        slot_loaded = [sem(f"slot{i}_loaded") for i in range(RING)]

        def pair(name):
            return ps[steps[name] % 2]

        def uses_before(j):
            return 16 * (j // RING + 1)

        def slopes(n):
            return [2.0 ** (-8.0 * (i + 1) / n) for i in range(n)]

        chunks = []

        def add_maps(kind, tag, w=64):
            for qt in range(NT):
                for hc in range(2):
                    chunks.append((kind, tag, qt, hc, w))

        add_maps("moba", 0)
        n_att1 = len(chunks)
        add_maps("swa", 0)
        add_maps("diff", 0, 128)
        add_maps("cmp", 0)
        add_maps("slc", 0)
        add_maps("win", 0)

        def map_operands(kind, h):
            lo = 64 * (h % 2)
            r = slice(lo, lo + 64)
            if kind == "moba":
                return qT[r, h // 2], kT[r, h // 2]
            if kind == "swa":
                return qa[r, h // 2], ka[r, h // 4]
            if kind == "diff":
                return qb[r, h // 2], kb[r, h // 2]
            k = {"cmp": kcmp, "slc": ksl, "win": kwn}[kind]
            return qc[r, h // 2], k[r, h // 4]

        def map_values(kind, h, kt):
            if kind == "moba":
                return v1[:, kt, 64 * h:64 * h + 64]
            if kind == "diff":
                return vb[:, kt, 128 * (h // 2):128 * (h // 2) + 128]
            if kind == "cmp":
                return vcmp[0:15, h // 4, :]
            vv = {"swa": va, "slc": vsl, "win": vwn}[kind]
            return vv[:, kt, 64 * (h // 4):64 * (h // 4) + 64]

        def score_col(h):
            return 512 * (h % 2) + 256 * (h // 2)

        def map_slope(kind, h):
            return slopes(4)[h // 2] if kind == "diff" else slopes(8)[h]

        nm_s = st[:, 0:8].rearrange("p (b h) -> p b h", b=2)
        rs_s = st[:, 8:16].rearrange("p (b h) -> p b h", b=2)
        es_s = st[:, 16:24].rearrange("p (b h) -> p b h", b=2)
        rv_s = st[:, 24:28]
        lam_s = st[:, 28:36]
        ss_s = st[:, 36:52]
        g8 = st[:, 52:60]
        m8 = st[:, 60:68]
        i8 = sb("top_index", 8, U32)
        f8 = st[:, 68:76]
        w8 = st[:, 76:84]

        n_vec, n_small, n_p = 11, 19, 20

        block = ctx.enter_context(nc.Block())

        @block.sync
        def _(sp):
            loads = {}

            def load(dst, src, s="vectors_loaded"):
                loads[s] = loads.get(s, 0) + 1
                sp.dma_start(dst, src).then_inc(sem(s), 16)

            def ring_load(j, ap, nk, n, wait):
                if wait is not None:
                    sp.wait_ge(PD, wait)
                s = j % RING
                dst = ring[:, s * SLOT:s * SLOT + nk * n].rearrange("p (t n) -> p t n", t=nk)
                sp.dma_start(dst, ap).then_inc(slot_loaded[s], 16)

            read_at = []
            for nm, idx in item_at.items():
                read_at.append(done_value(last_step_of_item[nm]))
            for k in range(3 * n1_exp):
                read_at.append(n_s1 + k + 1)
            for nm, idx in after1.items():
                read_at.append(done_value(last_step_of_item[nm]))

            load(X[:, :, :], a["x"][0].rearrange("(t p) n -> p t n", p=P), "x_loaded")
            r0 = 0
            vr = XT.rearrange("p k t -> p (k t)")[:, 0:P]
            vr2 = XT.rearrange("p k t -> p (k t)")[:, P:2 * P]
            for src, n in ((a["mix_norm_g"][0], 8), (a["ffn_norm_g"][0], 8), (a["norm1_g_2"][0], 8),
                           (a["norm2_g_2"][0], 8), (a["conv_b"][0], 12)):
                load(vr[r0:r0 + n, :], src.rearrange("(r n) -> r n", n=P))
                r0 += n
            load(vr[r0:r0 + 48, :], a["conv_w"][0].rearrange("k (r n) -> (k r) n", n=P))
            load(vr[92:108, :], a["mod_b_2"][0, 0:2048].rearrange("(r n) -> r n", n=P))
            load(vr[108:124, :], a["mod_b_2"][0, 3072:5120].rearrange("(r n) -> r n", n=P))
            load(vr[124:128, :], a["cmp_b1_2"][0].rearrange("j (r n) -> (j r) n", n=P))
            load(vr2[0:32, :], a["cmp_pos_2"][0].rearrange("j (l r) d -> (j l) (r d)", r=2))
            load(vr2[32:40, :], a["c_2"][0].rearrange("(r n) -> r n", n=P))
            for j in range(RING):
                ap, nk, n = front1[j]
                ring_load(j, ap, nk, n, None)
            load(wdt[:, :, :], blk(w_in, 0, KD, W1["dt"], 16), "small_loaded")
            load(wr1[:, :, 0:4], blk(a["w_rg"][0], 0, KD, 0, 4), "small_loaded")
            load(wr1[:, :, 4:20], blk(a["w_re"][0], 0, KD, 0, 16), "small_loaded")
            load(wr2[:, :, :], blk(a["router_w_2"][0], 0, KD, 0, 32), "small_loaded")
            for j in range(2):
                load(cw2[:, j], blk(a["cmp_w2_2"][0, j], 0, 2, 0, 64), "small_loaded")
            for half in range(2):
                load(cb2T[64 * half:64 * half + 64, :], a["cmp_b2_2"][0, 0].rearrange("(n o) -> n o", o=1), "small_loaded")
            for dst, src in ((dtb, a["dt_bias"][0]), (alog, a["a_log"][0]), (dsk, a["d_skip"][0]),
                             (rb1[:, 0:4], a["b_rg"][0]), (rb1[:, 4:20], a["b_re"][0]), (rb2, a["router_b_2"][0]),
                             (snk, a["sinks_2"][0]), (lamv, a["diff_lambda_2"][0].rearrange("a b -> (a b)")),
                             (sub_g, a["diff_subln_g_2"][0]),
                             (cb2, a["cmp_b2_2"][0, 1]),
                             (growA, a["ssd_norm_g"][0])):
                load(dst, src.rearrange("(o n) -> o n", o=1).broadcast_to([P, src.shape[0]]), "small_loaded")
            assert loads["vectors_loaded"] == n_vec and loads["small_loaded"] == n_small
            starts = [(W2["qa"], 512), (W2["kva"], 256), (W2["qb"], 512), (W2["kb"], 512), (W2["vb"], 512),
                      (W2["qc"], 512), (W2["kvc"], 512), (W2["kvw"], 256), (W2["gn"], 24)] + \
                     [(W2["gm"] + 512 * i, 512) for i in range(6)]
            for j in range(RING, n_front1):
                ap, nk, n = front1[j]
                ring_load(j, ap, nk, n, read_at[j - RING])
            wg = a["w_gate"][0].rearrange("e d f -> (e d) f")
            wu = a["w_up"][0].rearrange("e d f -> (e d) f")
            wd = a["w_down"][0].rearrange("e f d -> (e f) d")

            def expert1(slot, kind, e, wait):
                w, nk, n = ((wg, KD, 512), (wu, KD, 512), (wd, 4, 1024))[kind]
                sp.wait_ge(PD, wait)
                src = w[bass.ds(e * (nk * P), nk * P), :].rearrange("(t p) n -> p t n", p=P)
                dst = ring[:, slot * SLOT:(slot + 1) * SLOT].rearrange("p (t n) -> p t n", t=nk)
                sp.dma_start(dst, src).then_inc(slot_loaded[slot], 16)

            j = n_front1

            def pair1(i, wait_of):
                for k in range(6):
                    expert1((j + k) % RING, k % 3, 2 * i + k // 3, wait_of(k))

            pair1(0, lambda k: read_at[j + k - RING])
            with sp.Fori(1, n1_exp // 2) as i:
                pair1(i, lambda k: 6 * i + (n_s1 + k - RING + 1))
            assert j + 3 * n1_exp == base_mid
            sp.wait_ge(sem("ssd_gated"), 1)
            sp.wait_ge(sem("h2_ready"), 1)
            for s, (c0, n) in enumerate(starts):
                load(brow[32 * (s % 4):32 * (s % 4) + 1, 512 * (s // 4):512 * (s // 4) + n],
                     a["b_in_2"][0:1, c0:c0 + n], "p_loaded")
            load(pin[:, :, :], a["p"][0, 0].rearrange("(t p) n -> p t n", p=P), "p_loaded")
            for dst, src in ((growB, a["final_norm_g"]), (G12[:, 0], a["mod_b_2"][0, 2048:3072]),
                             (G12[:, 1], a["mod_b_2"][0, 5120:6144])):
                load(dst, src.rearrange("(o n) -> o n", o=1).broadcast_to([P, D]), "p_loaded")
            load(wgn[:, :, :], blk(w_in2, 0, KD, W2["gn"], 24), "p_loaded")
            assert loads["p_loaded"] == n_p
            for k, (ap, nk, n) in enumerate(front2):
                ring_load(base_mid + k, ap, nk, n, read_at[base_mid + k - RING])
            w1e = a["exp_w1_2"][0].rearrange("e d f -> (e d) f")
            w2e = a["exp_w2_2"][0].rearrange("e f d -> (e f) d")

            def expert2(slot, kind, e, half, wait):
                sp.wait_ge(PD, wait)
                if kind < 2:
                    src = w1e[bass.ds(e * D, D), 1024 * kind + 512 * half:1024 * kind + 512 * half + 512]
                    nk = KD
                else:
                    src = w2e[bass.ds(e * D + 512 * half, 512), :]
                    nk = 4
                dst = ring[:, slot * SLOT:(slot + 1) * SLOT].rearrange("p (t n) -> p t n", t=nk)
                sp.dma_start(dst, src.rearrange("(t p) n -> p t n", p=P)).then_inc(slot_loaded[slot], 16)

            j = base_exp2
            parts2 = ((0, 0), (1, 0), (0, 1), (1, 1), (2, 0), (2, 1))

            def pair2(i, wait_of):
                for k in range(12):
                    kind, half = parts2[k % 6]
                    expert2((j + k) % RING, kind, 2 * i + k // 6, half, wait_of(k))

            pair2(0, lambda k: read_at[k - RING] if k < RING else base_pd2 + k - RING + 1)
            with sp.Fori(1, NE2 // 2) as i:
                pair2(i, lambda k: 12 * i + (base_pd2 + k - RING + 1))
            sp.wait_ge(sem("out_ready"), 1)
            sp.dma_start(a["out"][0].rearrange("(t p) n -> p t n", p=P), X[:, :, :]).then_inc(sem("stored"), 16)
            sp.wait_ge(sem("stored"), 16)

        @block.gpsimd
        def _(pool):
            cnt = [0]

            def link(ins):
                cnt[0] += 1
                ins.then_inc(sem("pool_step"), 1)
                pool.wait_ge(sem("pool_step"), cnt[0])

            g = nc.gpsimd
            link(g.memset(ident, 0.0))
            link(g.affine_select(out=ident, in_=ident, pattern=[[-1, P]], compare_op=ALU.not_equal, fill=1.0, base=0,
                                 channel_multiplier=1))
            link(g.iota(DM, pattern=[[P, 2], [-1, T]], base=0, channel_multiplier=1,
                        allow_small_or_imprecise_dtypes=True))
            link(g.affine_select(out=DM, in_=DM, pattern=[[P, 2], [-1, T]], compare_op=ALU.is_ge, fill=BIG, base=0,
                                 channel_multiplier=1))
            link(g.affine_select(out=DMW, in_=DM, pattern=[[-P, 2], [1, T]], compare_op=ALU.is_ge, fill=BIG,
                                 base=127, channel_multiplier=-1))
            link(g.memset(U, 1.0))
            link(g.memset(MK, 0.0))
            for t, fill in ((U, 0.0), (MK, -BIG)):
                link(g.affine_select(out=t, in_=t, pattern=[[-P, 2], [1, T]], compare_op=ALU.is_ge, fill=fill, base=0,
                                     channel_multiplier=-1))
            link(g.memset(CV, 1.0))
            link(g.memset(CM, 0.0))
            for t, fill in ((CV, 0.0), (CM, -BIG)):
                link(g.affine_select(out=t, in_=t, pattern=[[P, 2], [-16, 15]], compare_op=ALU.is_ge, fill=fill,
                                     base=-31, channel_multiplier=1))
            link(g.iota(iota, pattern=[[1, P]], base=0, channel_multiplier=0, allow_small_or_imprecise_dtypes=True))
            link(g.memset(ones, 1.0))
            link(g.memset(eps[:, 0:1], 1e-6))
            link(g.memset(eps[:, 1:2], 1e-5))
            link(g.memset(g8, -BIG))
            g.memset(xbcP[:, :, 0:3], 0.0).then_inc(sem("constants_ready"), 1)

            with pool.Fori(0, n2_exp) as i:
                pool.wait_ge(sem("sig_ready"), i + 1)
                g.tensor_tensor(out=SG, in0=SG, in1=GS, op=ALU.mult).then_inc(sem("gated_ready"), 1)

        @block.scalar
        def _(act):
            s = nc.scalar
            cnt = {}

            def link(ins, name="act_step"):
                cnt[name] = cnt.get(name, 0) + 1
                ins.then_inc(sem(name), 1)
                act.wait_ge(sem(name), cnt[name])

            def products(name):
                act.wait_ge(PD, done_value(name))

            def freed(ins, name):
                ins.then_inc(pair_free[steps[name] % 2], 1)
                act.wait_ge(pair_free[steps[name] % 2], steps[name] // 2 + 1)

            def square_sums(src, dst, nseg, width, scr):
                for t in range(NT):
                    for g in range(nseg):
                        link(s.activation(scr, src[:, t, g * width:(g + 1) * width], ACT.Square,
                                          accum_out=dst[:, t * nseg + g:t * nseg + g + 1]))

            def rms(src, eps_col, name, nseg=1, width=D, scr=None):
                square_sums(src, ss_s, nseg, width, scr)
                link(s.activation(ss_s[:, 0:NT * nseg], ss_s[:, 0:NT * nseg], ACT.Sqrt, bias=eps[:, eps_col:eps_col + 1],
                                  scale=1.0 / width), name)

            def attention(c0, c1):
                for c in range(c0, c1):
                    kind, _, qt, hc, w = chunks[c]
                    b = c % 2
                    nk = 15 if kind == "cmp" else P * (qt + 1)
                    act.wait_ge(sem("scores_biased"), c + 1)
                    if kind == "swa":
                        link(s.activation(es_s[:, b], es_s[:, b], ACT.Exp))
                    for h in range(4):
                        ins = s.activation(SC[:, b, h, 0:nk], SC[:, b, h, 0:nk], ACT.Exp, bias=nm_s[:, b, h:h + 1],
                                           accum_out=rs_s[:, b, h:h + 1])
                    ins.then_inc(sem("probs_ready"), 1)
                    act.wait_ge(sem("probs_transposed"), c + 1)
                    nt = 1 if kind == "cmp" else qt + 1
                    rows = 15 if kind == "cmp" else P
                    if c >= 2:
                        act.wait_ge(sem("outputs_done"), c - 1)
                    s.copy(PT[0:rows, b, 0:4 * nt], ps[2][0:rows, 0:512 * nt]).then_inc(sem("probsT_ready"), 1)

            act.wait_ge(sem("constants_ready"), 1)
            act.wait_ge(sem("x_loaded"), 16)
            rms(X, 0, "rms_ready", scr=XN[:, 0])
            products("vec")
            link(s.copy(VT, ps[0][:, 0:P]))
            link(s.copy(VT2[:, 0:32], ps[0][:, P:P + 32]))
            freed(s.activation(VT2[:, 32:40], ps[0][:, P + 32:P + 40], ACT.Silu), "vec")
            products("q")
            freed(s.mul(qT, ps[steps["q"] % 2], 0.125), "q")
            products("k")
            freed(s.copy(kT, pair("k")), "k")
            products("v")
            freed(s.copy(v1, pair("v")), "v")
            for h in range(2):
                products(f"z{h}")
                freed(s.activation(silz[:, :, 512 * h:512 * h + 512], pair(f"z{h}").rearrange("p (t n) -> p t n", t=2),
                                   ACT.Silu), f"z{h}")
            for h in range(3):
                products(f"x{h}")
                freed(s.copy(xbcP[:, 4 * h:4 * h + 4, 3:259], pair(f"x{h}").rearrange("p (c t) -> p c t", c=4)), f"x{h}")
            act.wait_ge(sem("small_loaded"), 16 * n_small)
            act.wait_ge(sem("dt_raw"), 1)
            dr, dabs, dtt, dA, ncs = [ssd_small[:, 32 * k:32 * k + 32] for k in range(5)]
            link(s.activation(dabs, dr, ACT.Abs))
            link(s.activation(dabs, dabs, ACT.Exp, scale=-1.0))
            link(s.activation(dA[:, 0:16], alog, ACT.Exp))
            link(s.activation(dabs, dabs, ACT.Ln, bias=ones[:, 0:1]), "dt_logs")
            attention(0, n_att1)
            act.wait_ge(sem("conv_done"), 1)
            link(s.activation(cvT, cvT, ACT.Silu), "conv_ready")
            for g in range(4):
                act.wait_ge(sem("decay_biased"), g + 1)
                s.activation(Mt[:, g % 2], Mt[:, g % 2], ACT.Exp).then_inc(sem("decay_exp"), 1)
            for h in range(2):
                products(f"ga{h}")
                if h:
                    act.wait_ge(sem("merged"), 1)
                freed(s.activation(sg, pair(f"ga{h}"), ACT.Sigmoid), f"ga{h}")
            act.wait_ge(sem("ssd_gated"), 1)
            rms(Y, 0, "rms_ready", nseg=2, width=512, scr=AT.rearrange("p k t -> p (k t)")[:, 0:512])
            for h in range(2):
                products(f"gb{h}")
                act.wait_ge(sem("merged"), 2 + h)
                freed(s.activation(sg, pair(f"gb{h}"), ACT.Sigmoid), f"gb{h}")
            for t in range(2):
                products(f"mt{t}")
                freed(s.copy(AT[:, 4 * t:4 * t + 4], pair(f"mt{t}")), f"mt{t}")
            act.wait_ge(sem("resid_ready"), 1)
            act.wait_ge(PD, done_value("wo1"))
            rms(X, 0, "rms_ready", scr=AT.rearrange("p k t -> p (k t)")[:, 0:1024])
            act.wait_ge(sem("route_exp"), 1)
            for t in range(NT):
                link(s.activation(rt_s[:, 64 * t:64 * t + 5], rt_s[:, 64 * t:64 * t + 5], ACT.Exp), "route_exped")

            def tail(b, e, pd_down):
                act.wait_ge(sem(f"gathered{b}"), e + 2)
                s.copy(XG.rearrange("p k s -> p (k s)"), ps[0]).then_inc(sem(f"xg_ready{b}"), 1)
                act.wait_ge(PD, pd_down)
                s.copy(YS, ps[2]).then_inc(sem(f"ys_ready{b}"), 1)
                act.wait_ge(sem(f"pick_turned{b}"), e + 1)
                s.copy(pickT, ps[1][:, 0:256]).then_inc(sem(f"pickT_ready{b}"), 1)

            def head(b):
                act.wait_ge(sem(f"gathered{b}"), 1)
                s.copy(XG.rearrange("p k s -> p (k s)"), ps[0]).then_inc(sem(f"xg_ready{b}"), 1)

            head(1)
            with act.Fori(0, n1_exp) as e:
                act.wait_ge(PD, 3 * e + (n_s1 + 1))
                act.wait_ge(sem("sg_free"), e + 1)
                s.activation(SG, ps[0], ACT.Silu).then_inc(gate_free, 1)
                tail(1, e, 3 * e + (n_s1 + 3))
            for h in range(2):
                products(f"p{h}")
                freed(s.copy(XT[:, 4 * h:4 * h + 4], pair(f"p{h}")), f"p{h}")
            products("ptr")
            freed(s.copy(pT, pair("ptr")[:, 0:512]), "ptr")
            for h in range(2):
                products(f"pg{h}")
                if h:
                    act.wait_ge(sem("ple_added"), 1)
                freed(s.activation(sg, pair(f"pg{h}"), ACT.Sigmoid), f"pg{h}")
            act.wait_ge(sem("ple_added"), 2)
            rms(X, 0, "rms_ready", scr=XN[:, 0])
            act.wait_ge(sem("x2_ready"), 1)
            rms(X, 1, "rms_ready", scr=XN[:, 0])
            products("qa")
            freed(s.mul(qa, pair("qa"), 0.125), "qa")
            for nm, dst in (("ka", ka), ("ksl", ksl), ("kwn", kwn)):
                products(nm)
                src = pair(nm)[:, 0:256]
                for half in range(2):
                    for h in range(2):
                        ins = s.copy(dst[64 * half:64 * half + 64, h], src[64 * h:64 * h + 64])
                        if half and h:
                            freed(ins, nm)
                        else:
                            link(ins)
                if nm == "ka":
                    products("va")
                    freed(s.copy(va, pair("va").rearrange("p (t n) -> p t n", t=2)[:, :, 0:128]), "va")
                    products("qb")
                    freed(s.mul(qb, pair("qb"), 0.125), "qb")
                    for nm2, dst2 in (("kb", kb), ("vb", vb)):
                        products(nm2)
                        freed(s.copy(dst2, pair(nm2)), nm2)
                    products("qc")
                    freed(s.mul(qc, pair("qc"), 0.125), "qc")
                    products("kc")
                    freed(s.copy(kraw, pair("kc")[:, 0:512]), "kc")
                if nm == "ksl":
                    products("vsl")
                    freed(s.copy(vsl, pair("vsl").rearrange("p (t n) -> p t n", t=2)[:, :, 0:128]), "vsl")
                if nm == "kwn":
                    products("vwn")
                    freed(s.copy(vwn, pair("vwn").rearrange("p (t n) -> p t n", t=2)[:, :, 0:128]), "vwn")
            products("gn")
            freed(s.activation(gts, pair("gn").rearrange("p (t n) -> p t n", t=2)[:, :, 0:24], ACT.Sigmoid), "gn")
            for j in range(2):
                products(f"c{j}")
                for m in range(2):
                    ins = s.activation(hid[:, j, m], pair(f"c{j}")[:, 30 * m:30 * m + 30], ACT.Gelu_apprx_tanh,
                                       bias=VT[:, 124 + 2 * j + m:125 + 2 * j + m])
                    if m:
                        freed(ins, f"c{j}")
                    else:
                        link(ins)
            products("cc")
            act.wait_ge(sem("lambda_sums"), 1)
            link(s.activation(lam_s[:, 0:2], lam_s[:, 0:2], ACT.Exp), "lambda_exp")
            attention(n_att1, len(chunks))
            act.wait_ge(sem("diff_squares"), 1)
            link(s.activation(ss_s[:, 0:8], ss_s[:, 0:8], ACT.Sqrt, bias=eps[:, 1:2], scale=1.0 / P), "diff_rms")
            k = 0
            for b in range(3):
                for h in range(2):
                    products(f"g{b}{h}")
                    if k:
                        act.wait_ge(sem("merged2"), k)
                    freed(s.activation(sg2, pair(f"g{b}{h}"), ACT.Sigmoid), f"g{b}{h}")
                    k += 1
            for t in range(2):
                products(f"nt{t + 2}")
                freed(s.copy(AT[:, 4 * t:4 * t + 4], pair(f"nt{t + 2}")), f"nt{t + 2}")
            act.wait_ge(sem("resid2_ready"), 1)
            act.dma_start(b1R, a["exp_b1_2"][0].rearrange("e (f n) -> (e f) n", n=P).rearrange("(c p) n -> p c n", p=P))\
                .then_inc(sem("b_loaded"), 16)
            act.dma_start(b2R[0:32, :], a["exp_b2_2"][0]).then_inc(sem("b_loaded"), 16)
            act.dma_start(growF, a["final_g_2"].rearrange("(o n) -> o n", o=1).broadcast_to([P, D]))\
                .then_inc(sem("last_gain_loaded"), 16)
            rms(X, 1, "rms_ready", scr=AT.rearrange("p k t -> p (k t)")[:, 0:1024])
            for t in range(2):
                act.wait_ge(sem("route2_exp"), t + 1)
                link(s.activation(w8[:, 4 * t:4 * t + 4], w8[:, 4 * t:4 * t + 4], ACT.Exp,
                                  accum_out=rt_s[:, 224 + t:225 + t]), "route2_exped")

            head(2)
            with act.Fori(0, NE2) as e:
                for half in range(2):
                    act.wait_ge(sem("gate_limited"), 2 * e + (1 + half))
                    if half:
                        act.wait_ge(sem("hidden_ready2"), 2 * e + 1)
                    s.activation(SG, GS, ACT.Sigmoid, scale=1.702).then_inc(sem("sig_ready"), 1)
                tail(2, e, 6 * e + (base_pd2 + 6))
            act.wait_ge(sem("moe2_added"), 1)
            rms(X, 1, "rms_ready", scr=XN[:, 0])

        @block.vector
        def _(dve):
            v = nc.vector
            cnt = {}

            def link(ins, name="dve_step"):
                cnt[name] = cnt.get(name, 0) + 1
                ins.then_inc(sem(name), 1)
                dve.wait_ge(sem(name), cnt[name])

            def flag(name):
                cnt[name] = cnt.get(name, 0) + 1
                dve.sem_inc(sem(name), 1)

            def products(name):
                dve.wait_ge(PD, done_value(name))

            def freed(ins, name):
                ins.then_inc(pair_free[steps[name] % 2], 1)
                dve.wait_ge(pair_free[steps[name] % 2], steps[name] // 2 + 1)

            n_rms = [0]

            def scale_rows(dst, nseg=1, width=D, src=None):
                n_rms[0] += 1
                dve.wait_ge(sem("rms_ready"), n_rms[0])
                link(v.reciprocal(ss_s[:, 0:NT * nseg], ss_s[:, 0:NT * nseg]))
                for t in range(NT):
                    for g in range(nseg):
                        link(v.tensor_scalar(dst[:, t, g * width:(g + 1) * width], src[:, t, g * width:(g + 1) * width],
                                             ss_s[:, t * nseg + g:t * nseg + g + 1], None, ALU.mult))

            def scaled_T(names, scale, shift, ready):
                for h in range(2):
                    products(names[h])
                    for k in range(4):
                        kk = 4 * h + k
                        src = pair(names[h])[:, 256 * k:256 * k + 256]
                        if shift is None:
                            ins = v.tensor_scalar(XT[:, kk], src, scale[:, kk:kk + 1], None, ALU.mult)
                        else:
                            ins = v.tensor_scalar(XT[:, kk], src, scale[:, kk:kk + 1], shift[:, kk:kk + 1], ALU.mult,
                                                  ALU.add)
                        if k < 3:
                            link(ins)
                    freed(ins, names[h])
                flag(ready)

            def bias_scores(c):
                kind, _, qt, hc, w = chunks[c]
                b = c % 2
                nk = 15 if kind == "cmp" else P * (qt + 1)
                dve.wait_ge(sem("scores_done"), c + 1)
                if c >= 2:
                    dve.wait_ge(sem("probs_transposed"), c - 1)
                if kind == "cmp":
                    for r in range(2):
                        ins = v.tensor_tensor(
                            out=SC[:, b].rearrange("p (j r) k -> p r j k", r=2)[:, r, :, 0:15],
                            in0=ps[b][:, 512 * r:512 * r + 512].rearrange("p (j k) -> p j k", j=2)[:, :, 0:15],
                            in1=CM[:, qt:qt + 1, :].broadcast_to([P, 2, 15]), op=ALU.add)
                    link(ins)
                else:
                    dm = DMW if kind == "swa" else DM
                    for h in range(4):
                        ins = v.scalar_tensor_tensor(out=SC[:, b, h, 0:nk], in0=dm[:, qt, 0:nk],
                                                     scalar=-map_slope(kind, 4 * hc + h),
                                                     in1=ps[b][:, score_col(h):score_col(h) + nk],
                                                     op0=ALU.mult, op1=ALU.add)
                    link(ins)
                red = v.tensor_reduce(out=nm_s[:, b], in_=SC[:, b, :, 0:nk], axis=AX.X, op=ALU.max, negate=True)
                if kind == "swa":
                    link(red)
                    link(v.tensor_tensor(out=nm_s[:, b], in0=nm_s[:, b], in1=nsnk[:, 4 * hc:4 * hc + 4], op=ALU.min))
                    link(v.tensor_tensor(out=es_s[:, b], in0=nm_s[:, b], in1=snk[:, 4 * hc:4 * hc + 4], op=ALU.add),
                         "scores_biased")
                else:
                    link(red, "scores_biased")

            def outputs(c):
                kind, _, qt, hc, w = chunks[c]
                b = c % 2
                dve.wait_ge(sem("outputs_done"), c + 1)
                if kind == "swa":
                    link(v.tensor_tensor(out=rs_s[:, b], in0=rs_s[:, b], in1=es_s[:, b], op=ALU.add))
                link(v.reciprocal(rv_s, rs_s[:, b]))
                if kind in ("cmp", "slc", "win"):
                    n = ("cmp", "slc", "win").index(kind)
                    gv = gts.rearrange("p t (h s) -> p t s h", s=3)[:, qt, n, 4 * hc:4 * hc + 4]
                    link(v.tensor_tensor(out=rv_s, in0=rv_s, in1=gv, op=ALU.mult))
                if kind == "cmp":
                    link(v.tensor_scalar(rv_s, rv_s, CV[:, qt, 0:1], None, ALU.mult))
                if kind == "diff":
                    neg = rv_s.rearrange("p (h c) -> p h c", c=2)[:, :, 1]
                    link(v.tensor_scalar(neg, neg, lam_s[:, 4:5], None, ALU.mult))
                src = ps[3][:, 512 * b:512 * b + 4 * w].rearrange("p (h n) -> p h n", h=4)
                rvb = rv_s.unsqueeze(2).broadcast_to([P, 4, w])
                if kind in ("moba", "swa", "cmp"):
                    dst = {"moba": O1, "swa": Oa, "cmp": Oc}[kind][:, qt, 256 * hc:256 * hc + 256]
                    link(v.tensor_tensor(out=dst.rearrange("p (h n) -> p h n", h=4), in0=src, in1=rvb, op=ALU.mult),
                         "outputs_scaled")
                else:
                    t4 = tmpO[:, 0:4 * w]
                    link(v.tensor_tensor(out=t4.rearrange("p (h n) -> p h n", h=4), in0=src, in1=rvb, op=ALU.mult))
                    if kind == "diff":
                        t2 = t4.rearrange("p (h c n) -> p h c n", h=2, c=2)
                        dst = Ob[:, qt, 256 * hc:256 * hc + 256].rearrange("p (h n) -> p h n", h=2)
                        link(v.tensor_tensor(out=dst, in0=t2[:, :, 0], in1=t2[:, :, 1], op=ALU.add), "outputs_scaled")
                    else:
                        dst = Oc[:, qt, 256 * hc:256 * hc + 256]
                        link(v.tensor_tensor(out=dst, in0=dst, in1=t4, op=ALU.add), "outputs_scaled")

            def attention(c0, c1):
                for c in range(c0, c1):
                    bias_scores(c)
                    if c > c0:
                        outputs(c - 1)
                outputs(c1 - 1)

            dve.wait_ge(sem("constants_ready"), 1)
            scale_rows(XN, src=X)
            flag("xn_ready")
            dve.wait_ge(pair_free[0], 1)
            scaled_T(("xt0", "xt1"), VT[:, 0:8], None, "xT_ready")
            dve.wait_ge(sem("small_loaded"), 16 * n_small)
            dr, dabs, dtt, dA, ncs = [ssd_small[:, 32 * k:32 * k + 32] for k in range(5)]
            products("dt")
            freed(v.tensor_tensor(out=dr.rearrange("p (t h) -> p t h", t=2),
                                  in0=pair("dt").rearrange("p (t n) -> p t n", t=2)[:, :, 0:16],
                                  in1=dtb.unsqueeze(1).broadcast_to([P, 2, 16]), op=ALU.add), "dt")
            flag("dt_raw")
            dve.wait_ge(sem("dt_logs"), 1)
            link(v.scalar_tensor_tensor(out=dtt, in0=dr, scalar=0.0, in1=dabs, op0=ALU.max, op1=ALU.add))
            d3 = [x.rearrange("p (t h) -> p t h", t=2) for x in (dr, dtt, ncs)]
            link(v.scalar_tensor_tensor(out=d3[0], in0=d3[1], scalar=-1.0,
                                        in1=dA[:, 0:16].unsqueeze(1).broadcast_to([P, 2, 16]),
                                        op0=ALU.mult, op1=ALU.mult), "da_ready")
            link(v.tensor_scalar(nsnk, snk, -1.0, None, ALU.mult))
            attention(0, n_att1)
            for c in range(12):
                link(v.tensor_scalar(cvT[:, c], xbcP[:, c, 0:T], VT[:, 44 + c:45 + c], VT[:, 32 + c:33 + c], ALU.mult,
                                     ALU.add))
                for k in range(1, 4):
                    link(v.scalar_tensor_tensor(out=cvT[:, c], in0=xbcP[:, c, k:k + T],
                                                scalar=VT[:, 44 + 12 * k + c:45 + 12 * k + c], in1=cvT[:, c],
                                                op0=ALU.mult, op1=ALU.add))
            flag("conv_done")
            products("G")
            freed(v.tensor_copy(GT, pair("G").rearrange("p (g s t) -> p g s t", g=2, s=2)), "G")
            for k in range(4):
                products(f"xsT{k}")
                freed(v.tensor_copy(xs[:, :, 256 * k:256 * k + 256],
                                    pair(f"xsT{k}")[:, 0:512].rearrange("p (t n) -> p t n", t=2)), f"xsT{k}")
            link(v.tensor_tensor(out=xdt.rearrange("p t (h n) -> p t h n", n=64),
                                 in0=xs.rearrange("p t (h n) -> p t h n", n=64),
                                 in1=d3[1].unsqueeze(3).broadcast_to([P, 2, 16, 64]), op=ALU.mult), "xdt_ready")
            products("cs")
            freed(v.tensor_scalar(ncs, pair("cs")[:, 0:32], -1.0, None, ALU.mult), "cs")
            def decay(g):
                b = g % 2
                products(f"cb{g}")
                if g >= 2:
                    dve.wait_ge(sem("ssd_heads_done"), g - 1)
                S4 = pair(f"cb{g}").rearrange("p (h t) -> p h t", h=4)
                for h in range(4):
                    hh = 4 * g + h
                    link(v.scalar_tensor_tensor(out=Mt[:, b, h, 0:256], in0=S4[:, h], scalar=ncs[:, hh:hh + 1],
                                                in1=MK[:, 0], op0=ALU.add, op1=ALU.add))
                    ins = v.scalar_tensor_tensor(out=Mt[:, b, h, 256:384], in0=S4[:, h, 128:256],
                                                 scalar=ncs[:, 16 + hh:17 + hh], in1=MK[:, 1, 128:256],
                                                 op0=ALU.add, op1=ALU.add)
                    if h < 3:
                        link(ins)
                freed(ins, f"cb{g}")
                flag("decay_biased")

            def times_g(g):
                b = g % 2
                gg = g // 2
                dve.wait_ge(sem("decay_exp"), g + 1)
                link(v.tensor_tensor(out=Mt[:, b, :, 0:256], in0=Mt[:, b, :, 0:256],
                                     in1=GT[:, gg, 0:1].broadcast_to([P, 4, 256]), op=ALU.mult))
                link(v.tensor_tensor(out=Mt[:, b, :, 256:384], in0=Mt[:, b, :, 256:384],
                                     in1=GT[:, gg, 1:2, 128:256].broadcast_to([P, 4, 128]), op=ALU.mult), "decay_ready")

            for g in range(4):
                decay(g)
                if g:
                    times_g(g - 1)
            times_g(3)
            dve.wait_ge(sem("ssd_heads_done"), 4)
            link(v.tensor_tensor(out=Y.rearrange("p t (h n) -> p t h n", n=64),
                                 in0=xs.rearrange("p t (h n) -> p t h n", n=64),
                                 in1=dsk.unsqueeze(1).unsqueeze(3).broadcast_to([P, 2, 16, 64]), op=ALU.mult))
            for t in range(2):
                link(v.tensor_tensor(out=Y[:, t], in0=Y[:, t], in1=ps[2 + t], op=ALU.add))
            link(v.tensor_tensor(out=Y, in0=Y, in1=silz, op=ALU.mult), "ssd_gated")
            products("ot1")
            freed(v.tensor_copy(OT, pair("ot1")), "ot1")

            def halves(dst, h):
                return dst[:, :, 512 * h:512 * h + 512]

            def two(name):
                return pair(name).rearrange("p (t n) -> p t n", t=2)

            for h in range(2):
                products(f"a{h}")
                products(f"ga{h}")
                dve.wait_ge(pair_free[steps[f"ga{h}"] % 2], steps[f"ga{h}"] // 2 + 1)
                freed(v.tensor_tensor(out=halves(MRG, h), in0=two(f"a{h}"), in1=sg, op=ALU.mult), f"a{h}")
                flag("merged")
            scale_rows(Y, nseg=2, width=512, src=Y)
            link(v.tensor_tensor(out=Y, in0=Y, in1=growA.unsqueeze(1).broadcast_to([P, 2, D]), op=ALU.mult), "y_ready")
            for h in range(2):
                products(f"yt{h}")
                freed(v.tensor_copy(AT[:, 4 * h:4 * h + 4], pair(f"yt{h}")), f"yt{h}")
            for h in range(2):
                products(f"b{h}")
                dve.wait_ge(pair_free[steps[f"gb{h}"] % 2], steps[f"gb{h}"] // 2 + 1)
                freed(v.tensor_tensor(out=sg, in0=two(f"b{h}"), in1=sg, op=ALU.mult), f"b{h}")
                link(v.tensor_tensor(out=halves(MRG, h), in0=halves(MRG, h), in1=sg, op=ALU.add), "merged")
            for h in range(2):
                products(f"wo{h}")
                freed(v.tensor_tensor(out=halves(X, h), in0=two(f"wo{h}"), in1=halves(X, h), op=ALU.add), f"wo{h}")
            flag("resid_ready")
            scale_rows(XN, src=X)
            flag("h2n_ready")
            scaled_T(("ht0", "ht1"), VT[:, 8:16], None, "h2_ready")

            def route_parts(t):
                o = 64 * t
                return rt_s[:, o:o + 8], rt_s[:, o + 12:o + 16], rt_s[:, o + 16:o + 32], rt_s[:, o + 32:o + 36]

            products("rt1")
            lg = rt_s[:, 128:168].rearrange("p (t n) -> p t n", t=2)
            freed(v.tensor_tensor(out=lg, in0=pair("rt1").rearrange("p (t n) -> p t n", t=2)[:, :, 0:20],
                                  in1=rb1.unsqueeze(1).broadcast_to([P, 2, 20]), op=ALU.add), "rt1")
            for t in range(2):
                e_, oh, ev, w_ = route_parts(t)
                link(v.tensor_copy(g8[:, 0:4], lg[:, t, 0:4]))
                link(v.max(out=m8, in_=g8))
                link(v.max_index(out=i8, in_max=m8, in_values=g8))
                link(v.tensor_copy(f8, i8))
                link(v.tensor_scalar(oh, io32[:, 0:4], f8[:, 0:1], None, ALU.is_equal))
                link(v.tensor_scalar(e_[:, 0:4], lg[:, t, 0:4], m8[:, 0:1], None, ALU.subtract))
                link(v.tensor_scalar(oh, oh, -1.0, BIG, ALU.add, ALU.mult))
                link(v.tensor_tensor(out=ev.rearrange("p (g e) -> p g e", g=4),
                                     in0=lg[:, t, 4:20].rearrange("p (g e) -> p g e", g=4),
                                     in1=oh.unsqueeze(2).broadcast_to([P, 4, 4]), op=ALU.add))
                link(v.max(out=m8, in_=ev))
                link(v.max_index(out=i8, in_max=m8, in_values=ev))
                link(v.tensor_copy(f8, i8))
                link(v.tensor_tensor(out=e_[:, 4:5], in0=m8[:, 1:2], in1=m8[:, 0:1], op=ALU.subtract))
                link(v.tensor_copy(w_[:, 0:2], f8[:, 0:2]))
            flag("route_exp")
            dve.wait_ge(sem("route_exped"), 2)
            for t in range(2):
                e_, oh, ev, w_ = route_parts(t)
                link(v.tensor_reduce(out=w_[:, 2:3], in_=e_[:, 0:4], axis=AX.X, op=ALU.add))
                link(v.tensor_scalar(w_[:, 3:4], e_[:, 4:5], 1.0, None, ALU.add))
                link(v.tensor_tensor(out=w_[:, 2:3], in0=w_[:, 2:3], in1=w_[:, 3:4], op=ALU.mult))
                link(v.reciprocal(w_[:, 2:3], w_[:, 2:3]))
                link(v.tensor_tensor(out=w_[:, 3:4], in0=w_[:, 2:3], in1=e_[:, 4:5], op=ALU.mult))
                link(v.tensor_scalar(comb[:, t, 0:16], io32[:, 0:16], w_[:, 0:1], w_[:, 2:3], ALU.is_equal, ALU.mult))
                link(v.tensor_scalar(ev, io32[:, 0:16], w_[:, 1:2], w_[:, 3:4], ALU.is_equal, ALU.mult))
                link(v.tensor_tensor(out=comb[:, t, 0:16], in0=comb[:, t, 0:16], in1=ev, op=ALU.add))


            def ranks(n, step_name):
                sel = rt_s[:, 0:64].rearrange("p (t e) -> p t e", t=NT)
                link(v.tensor_scalar(sel[:, :, 0:n], comb[:, :, 0:n], 0.0, None, ALU.is_gt))
                link(v.tensor_scalar(tri, DM, 0.5 * BIG, None, ALU.is_lt), "tri_ready")
                products(step_name)
                cum = pair(step_name)[:, 0:2 * n].rearrange("p (t e) -> p t e", t=NT)
                link(v.memset(rank[:, :, 32:33], -1.0))
                link(v.memset(rank[:, :, n:n + 1], -1.0))
                link(v.memset(comb0[:, :, 0:1], 0.0))
                big = rt_s[0:1, 64:64 + n]
                size = rt_s[0:1, 96:96 + n]
                link(v.tensor_scalar(big, cum[0:1, 0], float(P), None, ALU.is_gt))
                link(v.tensor_scalar(size, cum[0:1, 0], float(P // 2), None, ALU.is_gt))
                link(v.memset(sizes[0:1, :], 0))
                link(v.tensor_tensor(out=sizes[0:1, 1:n + 1], in0=big, in1=size, op=ALU.add))
                link(v.tensor_tensor(out=rank[:, :, 0:n], in0=cum, in1=sel[:, :, 0:n], op=ALU.mult))
                freed(v.tensor_scalar(rank[:, :, 0:n], rank[:, :, 0:n], -1.0, None, ALU.add), step_name)

            def rows_back(names):
                for t in range(NT):
                    products(names[t])
                    freed(v.tensor_copy(HT[:, t], pair(names[t])), names[t])

            def picks(b, e, buf):
                for t in range(NT):
                    ins = v.tensor_scalar(pick[:, buf, t], iota, rank[:, t, bass.ds(e, 1)], None, ALU.is_equal)
                ins.then_inc(sem(f"picked{b}"), 1)

            def start_experts(b):
                link(v.memset(YS, 0.0))
                link(v.memset(pickT, 0.0))
                dve.sem_inc(sem(f"ys_ready{b}"), 1)
                dve.sem_inc(sem(f"pickT_ready{b}"), 1)
                picks(b, 0, 0)

            def add_outputs(b, e, dst):
                dve.wait_ge(sem(f"scattered{b}"), e + 1)
                for t in range(NT):
                    for h in range(2):
                        ins = v.scalar_tensor_tensor(out=dst[:, t, 512 * h:512 * h + 512],
                                                     in0=ps[2 + t][:, 512 * h:512 * h + 512],
                                                     scalar=comb0[:, t, bass.ds(e, 1)],
                                                     in1=dst[:, t, 512 * h:512 * h + 512], op0=ALU.mult, op1=ALU.add)
                ins.then_inc(sem(f"outputs_added{b}"), 1)
                dve.wait_ge(sem(f"outputs_added{b}"), e + 1)

            rows_back(("hb0", "hb1"))
            ranks(n1_exp, "rk1")
            start_experts(1)
            dve.sem_inc(sem("sg_free"), 1)
            with dve.Fori(0, n1_exp // 2) as i:
                for k in range(2):
                    e = 2 * i + k
                    dve.wait_ge(PD, 3 * e + (n_s1 + 1))
                    picks(1, e + 1, 1 - k)
                    dve.wait_ge(PD, 3 * e + (n_s1 + 2))
                    dve.wait_ge(gate_free, e + 1)
                    v.tensor_tensor(out=Hb[:, 0], in0=ps[1], in1=SG, op=ALU.mult).then_inc(sem("hidden_ready1"), 1)
                    dve.wait_ge(sem("hidden_ready1"), e + 1)
                    dve.sem_inc(sem("sg_free"), 1)
                    add_outputs(1, e, X)
            add_outputs(1, n1_exp, X)
            flag("moe1_added")
            for h in range(2):
                products(f"pp{h}")
                dve.wait_ge(pair_free[steps[f"pg{h}"] % 2], steps[f"pg{h}"] // 2 + 1)
                freed(v.tensor_tensor(out=sg, in0=two(f"pp{h}"), in1=sg, op=ALU.mult), f"pp{h}")
                link(v.tensor_tensor(out=halves(X, h), in0=halves(X, h), in1=sg, op=ALU.add), "ple_added")
            dve.wait_ge(sem("p_loaded"), 16 * n_p)
            scale_rows(X, src=X)
            link(v.tensor_tensor(out=X, in0=X, in1=growB.unsqueeze(1).broadcast_to([P, 2, D]), op=ALU.mult), "x2_ready")
            scale_rows(XN, src=X)
            flag("xn2_ready")
            for i in range(12):
                products(f"md{i}")
                part, h = i // 2, i % 2
                if part in (2, 5):
                    dst = G12[:, part // 3, 512 * h:512 * h + 512]
                    freed(v.tensor_tensor(out=dst, in0=pair(f"md{i}")[:, 0:512], in1=dst, op=ALU.add), f"md{i}")
                else:
                    c0 = 8 * (part if part < 2 else part - 1) + 4 * h
                    freed(v.tensor_tensor(out=modT[:, c0:c0 + 4], in0=pair(f"md{i}")[:, 0:4],
                                          in1=VT[:, 92 + c0:96 + c0], op=ALU.add), f"md{i}")
            link(v.scalar_tensor_tensor(out=modT[:, 8:16], in0=modT[:, 8:16], scalar=1.0, in1=VT[:, 16:24],
                                        op0=ALU.add, op1=ALU.mult))
            link(v.scalar_tensor_tensor(out=modT[:, 24:32], in0=modT[:, 24:32], scalar=1.0, in1=VT[:, 24:32],
                                        op0=ALU.add, op1=ALU.mult))
            scaled_T(("nt0", "nt1"), modT[:, 8:16], modT[:, 0:8], "xT2_ready")
            l4 = lamv.rearrange("p (a b d) -> p a b d", a=2, b=2)
            link(v.tensor_tensor(out=l4[:, :, 0], in0=l4[:, :, 0], in1=l4[:, :, 1], op=ALU.mult))
            link(v.tensor_reduce(out=lam_s[:, 0:2], in_=l4[:, :, 0], axis=AX.X, op=ALU.add), "lambda_sums")
            dve.wait_ge(pair_free[steps["kc"] % 2], steps["kc"] // 2 + 1)
            for j in range(2):
                for h in range(2):
                    for r in range(2):
                        src = kraw[64 * h:64 * h + 64, j]
                        pos = VT2[64 * r:64 * r + 64, 16 * j:16 * j + 16]
                        for half in range(2):
                            win = src[:, 16 * half:16 * half + 240].rearrange("p (c m r) -> p m c r", m=8, r=2)[:, :, :, r]
                            dst = kexp[64 * r:64 * r + 64, j, 8 * half:8 * half + 8, h, :]
                            link(v.tensor_copy(dst, win))
                            link(v.tensor_tensor(out=dst, in0=dst,
                                                 in1=pos[:, 8 * half:8 * half + 8].unsqueeze(2).broadcast_to([64, 8, 15]),
                                                 op=ALU.add))
            flag("windows_ready")
            products("cc")
            link(v.tensor_scalar(kcmp, pair("cc")[:, 0:30], cb2T, None, ALU.add))
            freed(v.tensor_tensor(out=vcmp[0:15, :, :], in0=pair("cc")[0:15, 512:640].rearrange("p (h n) -> p h n", h=2),
                                  in1=cb2[0:15, :].unsqueeze(1).broadcast_to([15, 2, 64]), op=ALU.add), "cc")
            dve.wait_ge(sem("lambda_exp"), 1)
            link(v.tensor_tensor(out=lam_s[:, 4:5], in0=lam_s[:, 1:2], in1=lam_s[:, 0:1], op=ALU.subtract))
            link(v.tensor_scalar(lam_s[:, 4:5], lam_s[:, 4:5], -0.2, None, ALU.add))
            attention(n_att1, len(chunks))
            o8 = Ob.rearrange("p t (h n) -> p (t h) n", n=P)
            sq = MRG.rearrange("p t n -> p (t n)")[:, 0:1024].rearrange("p (t n) -> p t n", n=P)
            link(v.tensor_tensor(out=sq, in0=o8, in1=o8, op=ALU.mult))
            link(v.tensor_reduce(out=ss_s[:, 0:8], in_=sq, axis=AX.X, op=ALU.add), "diff_squares")
            dve.wait_ge(sem("diff_rms"), 1)
            link(v.reciprocal(ss_s[:, 0:8], ss_s[:, 0:8]))
            link(v.tensor_scalar(ss_s[:, 0:8], ss_s[:, 0:8], 0.8, None, ALU.mult))
            link(v.tensor_tensor(out=o8, in0=o8, in1=ss_s[:, 0:8].unsqueeze(2).broadcast_to([P, 8, P]), op=ALU.mult))
            link(v.tensor_tensor(out=o8, in0=o8, in1=sub_g.unsqueeze(1).broadcast_to([P, 8, P]), op=ALU.mult),
                 "branches_ready")
            for b in range(3):
                products(f"bt{b}")
                freed(v.tensor_copy(hT3[b], pair(f"bt{b}")), f"bt{b}")
                for h in range(2):
                    products(f"y{b}{h}")
                    dve.wait_ge(pair_free[steps[f"g{b}{h}"] % 2], steps[f"g{b}{h}"] // 2 + 1)
                    if b == 0:
                        freed(v.tensor_tensor(out=halves(MRG, h), in0=two(f"y{b}{h}"), in1=sg2, op=ALU.mult), f"y{b}{h}")
                        flag("merged2")
                    else:
                        freed(v.tensor_tensor(out=sg2, in0=two(f"y{b}{h}"), in1=sg2, op=ALU.mult), f"y{b}{h}")
                        link(v.tensor_tensor(out=halves(MRG, h), in0=halves(MRG, h), in1=sg2, op=ALU.add), "merged2")
            for h in range(2):
                products(f"no{h}")
                g1 = G12[:, 0, 512 * h:512 * h + 512].unsqueeze(1).broadcast_to([P, 2, 512])
                freed(v.tensor_tensor(out=halves(MRG, h), in0=two(f"no{h}"), in1=g1, op=ALU.mult), f"no{h}")
                link(v.tensor_tensor(out=halves(X, h), in0=halves(X, h), in1=halves(MRG, h), op=ALU.add))
            flag("resid2_ready")
            scale_rows(XN, src=X)
            flag("h3n_ready")
            scaled_T(("h20", "h21"), modT[:, 24:32], modT[:, 16:24], "h3_ready")
            products("rt2")
            lg2 = rt_s[:, 128:192].rearrange("p (t n) -> p t n", t=2)
            freed(v.tensor_tensor(out=lg2, in0=pair("rt2").rearrange("p (t n) -> p t n", t=2)[:, :, 0:32],
                                  in1=rb2.unsqueeze(1).broadcast_to([P, 2, 32]), op=ALU.add), "rt2")
            for t in range(2):
                link(v.max(out=m8, in_=lg2[:, t]))
                link(v.max_index(out=i8, in_max=m8, in_values=lg2[:, t]))
                link(v.tensor_copy(f8, i8))
                link(v.tensor_scalar(w8[:, 4 * t:4 * t + 4], m8[:, 0:4], m8[:, 0:1], None, ALU.subtract), "route2_exp")
                dve.wait_ge(sem("route2_exped"), t + 1)
                link(v.reciprocal(rt_s[:, 224 + t:225 + t], rt_s[:, 224 + t:225 + t]))
                link(v.tensor_scalar(w8[:, 4 * t:4 * t + 4], w8[:, 4 * t:4 * t + 4], rt_s[:, 224 + t:225 + t], None, ALU.mult))
                for q in range(4):
                    dst = comb[:, t, :] if q == 0 else rt_s[:, 192:224]
                    link(v.tensor_scalar(dst, io32, f8[:, q:q + 1], w8[:, 4 * t + q:4 * t + q + 1], ALU.is_equal,
                                         ALU.mult))
                    if q:
                        link(v.tensor_tensor(out=comb[:, t, :], in0=comb[:, t, :], in1=dst, op=ALU.add))
            rows_back(("hb2", "hb3"))
            ranks(NE2, "rk2")
            products("b1t")
            freed(v.tensor_copy(b1T, pair("b1t")[:, 0:512]), "b1t")
            products("ct")
            freed(v.tensor_copy(combT[0:32, :], pair("ct")[0:32, 0:256]), "ct")
            products("cb")
            for t in range(2):
                link(v.tensor_copy(ACC[:, t], ps[2 + t]))
            flag("acc_ready")
            dve.wait_ge(PD, done_value("cb"))
            dve.sem_inc(pair_free[steps["cb"] % 2], 1)

            start_experts(2)

            def hidden2(e, half):
                n = 2 * e + half
                pd = 6 * e + (base_pd2 + 2 * half + 1)
                dve.wait_ge(PD, pd)
                for f in range(4):
                    ins = v.tensor_scalar(GS[:, 256 * f:256 * f + 256], ps[0][:, 256 * f:256 * f + 256],
                                          b1T[:, bass.ds(e, 1), 4 * half + f], 7.0, ALU.add, ALU.min)
                ins.then_inc(sem("gate_limited"), 1)
                dve.wait_ge(PD, pd + 1)
                for f in range(4):
                    ins = v.tensor_scalar(US[:, 256 * f:256 * f + 256], ps[1][:, 256 * f:256 * f + 256],
                                          b1T[:, bass.ds(e, 1), 8 + 4 * half + f], 7.0, ALU.add, ALU.min)
                ins.then_inc(up_free, 1)
                dve.wait_ge(up_free, n + 1)
                v.tensor_scalar(US, US, -7.0, 1.0, ALU.max, ALU.add).then_inc(sem("up_ready"), 1)
                dve.wait_ge(sem("up_ready"), n + 1)
                dve.wait_ge(sem("gated_ready"), n + 1)
                v.tensor_tensor(out=Hb[:, half], in0=US, in1=SG, op=ALU.mult).then_inc(sem("hidden_ready2"), 1)
                dve.wait_ge(sem("hidden_ready2"), n + 1)

            with dve.Fori(0, NE2 // 2) as i:
                for k in range(2):
                    e = 2 * i + k
                    dve.wait_ge(PD, 6 * e + (base_pd2 + 1))
                    picks(2, e + 1, 1 - k)
                    hidden2(e, 0)
                    add_outputs(2, e, ACC)
                    hidden2(e, 1)
            add_outputs(2, NE2, ACC)
            link(v.tensor_tensor(out=ACC, in0=ACC, in1=G12[:, 1].unsqueeze(1).broadcast_to([P, 2, D]), op=ALU.mult))
            link(v.tensor_tensor(out=X, in0=X, in1=ACC, op=ALU.add), "moe2_added")
            dve.wait_ge(sem("last_gain_loaded"), 16)
            scale_rows(X, src=X)
            link(v.tensor_tensor(out=X, in0=X, in1=growF.unsqueeze(1).broadcast_to([P, 2, D]), op=ALU.mult), "out_ready")

        @block.tensor
        def _(pe):
            mm = nc.tensor.matmul

            def begin(name):
                m = steps[name]
                if m >= 2:
                    pe.wait_ge(pair_free[m % 2], m // 2)
                return ps[m % 2]

            def slot(j, nk, n=None):
                pe.wait_ge(slot_loaded[j % RING], uses_before(j))
                n = n or SLOT // nk
                return ring[:, (j % RING) * SLOT:(j % RING) * SLOT + nk * n].rearrange("p (t n) -> p t n", t=nk)

            def all_free(name):
                for q in range(2):
                    pe.wait_ge(pair_free[q], (steps[name] - q) // 2 + 1)

            def lin_T(name, w, xT, nct, nk=KD, c0=0, bias=None):
                out = begin(name).rearrange("p (c t) -> p c t", t=T)
                for ct in range(nct):
                    for k in range(nk):
                        ins = mm(out[:, ct], w[:, k, c0 + P * ct:c0 + P * ct + P], xT[:, k], start=(k == 0),
                                 stop=(k == nk - 1 and bias is None))
                    if bias is not None:
                        r, bc = bias
                        ins = mm(out[:, ct], brow[r:r + 1, bc + P * ct:bc + P * ct + P], ones[r:r + 1, 0:T],
                                 start=False, stop=True)
                ins.then_inc(PD, 1)

            def lin_N(name, w, xT, n, nk=KD, c0=0, bias=None):
                out = begin(name).rearrange("p (t n) -> p t n", t=NT)
                for t in range(NT):
                    for k in range(nk):
                        ins = mm(out[:, t, 0:n], xT[:, k, P * t:P * t + P], w[:, k, c0:c0 + n], start=(k == 0),
                                 stop=(k == nk - 1 and bias is None))
                    if bias is not None:
                        r, bc = bias
                        ins = mm(out[:, t, 0:n], ones[r:r + 1, 0:P], brow[r:r + 1, bc:bc + n], start=False, stop=True)
                ins.then_inc(PD, 1)

            def transposes(name, src, k0, n=4):
                out = begin(name).rearrange("p (c t) -> p c t", t=T)
                for k in range(n):
                    for t in range(NT):
                        ins = nc.tensor.transpose(out[:, k, P * t:P * t + P], src[:, t, P * (k0 + k):P * (k0 + k) + P],
                                                  ident)
                ins.then_inc(PD, 1)

            def attention(c0, c1):
                def scores(c):
                    kind, _, qt, hc, w = chunks[c]
                    nk = 15 if kind == "cmp" else P * (qt + 1)
                    if c >= c0 + 2:
                        pe.wait_ge(sem("scores_biased"), c - 1)
                    for h in range(4):
                        q, k = map_operands(kind, 4 * hc + h)
                        ins = mm(ps[c % 2][:, score_col(h):score_col(h) + nk], q[:, P * qt:P * qt + P], k[:, 0:nk], start=True,
                                 stop=True)
                    ins.then_inc(sem("scores_done"), 1)

                scores(c0)
                for c in range(c0, c1):
                    if c + 1 < c1:
                        scores(c + 1)
                    kind, _, qt, hc, w = chunks[c]
                    cmp = kind == "cmp"
                    nt = 1 if cmp else qt + 1
                    rows = 15 if cmp else P
                    pe.wait_ge(sem("probs_ready"), c + 1)
                    if c:
                        pe.wait_ge(sem("probsT_ready"), c)
                    for m in range(4 * nt):
                        h, kt = m // nt, m % nt
                        ins = nc.tensor.transpose(ps[2][0:rows, P * m:P * m + P],
                                                  SC[:, c % 2, h, P * kt:P * kt + rows], ident)
                    ins.then_inc(sem("probs_transposed"), 1)
                    pe.wait_ge(sem("probsT_ready"), c + 1)
                    if c >= 2:
                        pe.wait_ge(sem("outputs_scaled"), c - 1)
                    for h in range(4):
                        for kt in range(nt):
                            ins = mm(ps[3][:, 512 * (c % 2) + w * h:512 * (c % 2) + w * h + w],
                                     PT[0:rows, c % 2, h * nt + kt], map_values(kind, 4 * hc + h, kt),
                                     start=(kt == 0), stop=(kt == nt - 1))
                    ins.then_inc(sem("outputs_done"), 1)

            pe.wait_ge(sem("constants_ready"), 1)
            pe.wait_ge(sem("vectors_loaded"), 16 * n_vec)
            vr = XT.rearrange("p k t -> p (k t)")
            begin("vec")
            nc.tensor.transpose(ps[0][:, 0:P], vr[:, 0:P], ident)
            nc.tensor.transpose(ps[0][:, P:P + 40], vr[0:40, P:2 * P], ident[0:40, 0:40]).then_inc(PD, 1)
            pe.wait_ge(sem("xn_ready"), 1)
            transposes("xt0", XN, 0)
            transposes("xt1", XN, 4)
            pe.wait_ge(sem("xT_ready"), 1)
            I = item_at
            lin_T("q", slot(I["q"], KD), XT, 4)
            lin_T("k", slot(I["k"], KD), XT, 4)
            lin_N("v", slot(I["v"], KD), XT, 512)
            for h in range(2):
                lin_N(f"z{h}", slot(I[f"z{h}"], KD), XT, 512)
            for h in range(3):
                lin_T(f"x{h}", slot(I[f"x{h}"], KD), XT, 4)
            pe.wait_ge(sem("small_loaded"), 16 * n_small)
            lin_N("dt", wdt, XT, 16)
            all_free("dt")
            attention(0, n_att1)
            pe.wait_ge(sem("conv_ready"), 1)
            o = begin("G").rearrange("p (g s t) -> p g s t", g=2, s=2)
            for g in range(2):
                for s_ in range(2):
                    ins = mm(o[:, g, s_], cvT[:, 8 + g, P * s_:P * s_ + P], cvT[:, 10 + g], start=True, stop=True)
            ins.then_inc(PD, 1)
            for k in range(4):
                o = begin(f"xsT{k}")[:, 0:512].rearrange("p (t n) -> p t n", t=2)
                for t in range(2):
                    for c in range(2):
                        ins = nc.tensor.transpose(o[:, t, P * c:P * c + P], cvT[:, 2 * k + c, P * t:P * t + P], ident)
                ins.then_inc(PD, 1)
            pe.wait_ge(sem("da_ready"), 1)
            da = ssd_small[:, 0:32]
            o = begin("cs")
            mm(o[:, 0:16], U[:, 0, 0:P], da[:, 0:16], start=True, stop=True)
            mm(o[:, 16:32], U[:, 0, P:T], da[:, 0:16], start=True, stop=False)
            mm(o[:, 16:32], U[:, 1, P:T], da[:, 16:32], start=False, stop=True).then_inc(PD, 1)

            def cum_rows(g):
                o = begin(f"cb{g}")
                for h in range(4):
                    for kt in range(2):
                        col = 16 * kt + 4 * g + h
                        ins = mm(o[:, 256 * h:256 * h + 256], da[:, col:col + 1].broadcast_to([P, P]), U[:, kt],
                                 start=(kt == 0), stop=(kt == 1))
                ins.then_inc(PD, 1)

            def ssd_heads(g):
                pe.wait_ge(sem("decay_ready"), g + 1)
                for h in range(4):
                    hh = 4 * g + h
                    c = slice(64 * hh, 64 * hh + 64)
                    m = Mt[:, g % 2, h]
                    mm(ps[2][:, c], m[:, 0:P], xdt[:, 0, c], start=True, stop=True)
                    mm(ps[3][:, c], m[:, P:T], xdt[:, 0, c], start=True, stop=False)
                    ins = mm(ps[3][:, c], m[:, T:T + P], xdt[:, 1, c], start=False, stop=True)
                ins.then_inc(sem("ssd_heads_done"), 1)

            pe.wait_ge(sem("xdt_ready"), 1)
            pe.wait_ge(sem("outputs_scaled"), n_att1)
            for g in range(4):
                cum_rows(g)
                if g:
                    ssd_heads(g - 1)
            ssd_heads(3)
            transposes("ot1", O1, 0)
            pe.wait_ge(pair_free[steps["ot1"] % 2], steps["ot1"] // 2 + 1)
            for h in range(2):
                lin_N(f"a{h}", slot(I["woa"], 4), OT, 512, nk=4, c0=512 * h)
                lin_N(f"ga{h}", slot(I[f"ga{h}"], KD), XT, 512)
            pe.wait_ge(sem("y_ready"), 1)
            transposes("yt0", Y, 0)
            transposes("yt1", Y, 4)
            pe.wait_ge(pair_free[steps["yt0"] % 2], steps["yt0"] // 2 + 1)
            pe.wait_ge(pair_free[steps["yt1"] % 2], steps["yt1"] // 2 + 1)
            for h in range(2):
                lin_N(f"b{h}", slot(I[f"wob{h}"], KD), AT, 512)
                lin_N(f"gb{h}", slot(I[f"gb{h}"], KD), XT, 512)
            pe.wait_ge(sem("merged"), 4)
            for h in range(2):
                transposes(f"mt{h}", MRG, 4 * h)
            for h in range(2):
                pe.wait_ge(pair_free[steps[f"mt{h}"] % 2], steps[f"mt{h}"] // 2 + 1)
            for h in range(2):
                lin_N(f"wo{h}", slot(I[f"wo{h}"], KD), AT, 512)
            pe.wait_ge(sem("h2n_ready"), 1)
            transposes("ht0", XN, 0)
            transposes("ht1", XN, 4)
            pe.wait_ge(sem("h2_ready"), 1)
            lin_N("rt1", wr1, XT, 20)

            def rows_back(names):
                for t in range(NT):
                    o = begin(names[t])
                    for k in range(KD):
                        ins = nc.tensor.transpose(o[:, P * k:P * k + P], XT[:, k, P * t:P * t + P], ident)
                    ins.then_inc(PD, 1)

            def ranks(n, step_name, turn):
                pe.wait_ge(sem("tri_ready"), turn)
                sel = rt_s[:, 0:64].rearrange("p (t e) -> p t e", t=NT)
                o = begin(step_name)
                mm(o[:, 0:n], tri[:, 0, 0:P], sel[:, 0, 0:n], start=True, stop=False)
                mm(o[:, 0:n], tri[:, 1, 0:P], sel[:, 1, 0:n], start=False, stop=True)
                mm(o[:, n:2 * n], tri[:, 1, P:T], sel[:, 1, 0:n], start=True, stop=True).then_inc(PD, 1)

            rows_back(("hb0", "hb1"))
            ranks(n1_exp, "rk1", 1)
            all_free("rk1")

            def size_of(e):
                return pe.value_load(sizes[0:1, bass.ds(e + 1, 1)], min_val=0, max_val=2)

            def by_size(size, body):
                for c, w in enumerate((P // 2, P, T)):
                    with pe.If(size == c):
                        body(w)

            def half_up(j, load_value, dst, size):
                pe.wait_ge(slot_loaded[j % RING], load_value)
                w_ = ring[:, (j % RING) * SLOT:(j % RING + 1) * SLOT].rearrange("p (t n) -> p t n", t=KD)

                def body(w):
                    for f in range(4):
                        for k in range(KD):
                            ins = mm(dst[:, 256 * f:256 * f + w], w_[:, k, P * f:P * f + P],
                                     XT[:, k] if w == T else XG[:, k, 0:w], start=(k == 0), stop=(k == KD - 1))
                    ins.then_inc(PD, 1)

                by_size(size, body)

            def half_down(j, load_value, hidden, size, first, last):
                pe.wait_ge(slot_loaded[j % RING], load_value)
                w_ = ring[:, (j % RING) * SLOT:(j % RING + 1) * SLOT].rearrange("p (t n) -> p t n", t=4)

                def body(w):
                    rows = min(w, P)
                    for t in range(max(1, w // P)):
                        for h in range(2):
                            for f in range(4):
                                ins = mm(ps[2 + t][0:rows, 512 * h:512 * h + 512], hidden[:, f, P * t:P * t + rows],
                                         w_[:, f, 512 * h:512 * h + 512], start=(first and f == 0),
                                         stop=(last and f == 3))
                    ins.then_inc(PD, 1)

                by_size(size, body)

            def gather(b, e, buf):
                size = size_of(e)
                pe.wait_ge(sem(f"picked{b}"), e + 1)

                def body(w):
                    if w == T:
                        pe.drain().then_inc(sem(f"gathered{b}"), 1)
                        return
                    for k in range(KD):
                        for t in range(NT):
                            ins = mm(ps[0][:, P * k:P * k + w], HT[:, t, P * k:P * k + P], pick[:, buf, t, 0:w],
                                     start=(t == 0), stop=(t == NT - 1))
                    ins.then_inc(sem(f"gathered{b}"), 1)

                by_size(size, body)
                return size

            def scatter(b, e, size):
                pe.wait_ge(sem(f"ys_ready{b}"), e + 1)

                def body(w):
                    if w == T:
                        pe.drain().then_inc(sem(f"scattered{b}"), 1)
                        return
                    for t in range(NT):
                        for h in range(2):
                            ins = mm(ps[2 + t][:, 512 * h:512 * h + 512], pickT[0:w, P * t:P * t + P],
                                     YS[0:w, 512 * h:512 * h + 512], start=True, stop=True)
                    ins.then_inc(sem(f"scattered{b}"), 1)

                by_size(size, body)

            def turn_picks(b, buf):
                for t in range(NT):
                    ins = nc.tensor.transpose(ps[1][:, P * t:P * t + P], pick[:, buf, t], ident)
                ins.then_inc(sem(f"pick_turned{b}"), 1)

            def experts(b, j0, n, halves_, hidden_sem):
                gather(b, 0, 0)
                nk = 3 * halves_
                with pe.Fori(0, n // 2) as i:
                    for k in range(2):
                        e = 2 * i + k
                        size = size_of(e)
                        j = j0 + nk * k
                        up = 16 * (2 * nk // RING) * i

                        def value(jj):
                            return up + uses_before(jj)

                        for half in range(halves_):
                            if half:
                                pe.wait_ge(sem("gate_limited"), 2 * e + 1)
                            else:
                                pe.wait_ge(sem(f"xg_ready{b}"), e + 1)
                            half_up(j, value(j), ps[0], size)
                            if half:
                                pe.wait_ge(up_free, 2 * e + 1)
                            else:
                                pe.wait_ge(sem(f"pickT_ready{b}"), e + 1)
                            half_up(j + 1, value(j + 1), ps[1], size)
                            j += 2
                            if half == 0:
                                size_before = pe.value_load(sizes[0:1, bass.ds(e, 1)], min_val=0, max_val=2)
                                scatter(b, e, size_before)
                        if b == 1:
                            pe.wait_ge(gate_free, e + 1)
                        else:
                            pe.wait_ge(sem("gate_limited"), 2 * e + 2)
                        gather(b, e + 1, 1 - k)
                        for half in range(halves_):
                            pe.wait_ge(hidden_sem, halves_ * e + (half + 1))
                            if half == 0:
                                pe.wait_ge(sem(f"outputs_added{b}"), e + 1)
                            half_down(j, value(j), Hb[:, half], size, half == 0, half == halves_ - 1)
                            j += 1
                        turn_picks(b, k)
                pe.wait_ge(sem(f"pickT_ready{b}"), n + 1)
                scatter(b, n, pe.value_load(sizes[0:1, bass.ds(n, 1)], min_val=0, max_val=2))

            experts(1, n_front1, n1_exp, 1, sem("hidden_ready1"))
            J = {k: base_mid + n for k, n in after1.items()}
            pe.wait_ge(sem("moe1_added"), 1)
            transposes("p0", X, 0)
            transposes("p1", X, 4)
            pe.wait_ge(sem("p_loaded"), 16 * n_p)
            transposes("ptr", pin, 0, n=2)
            for nm in ("p0", "p1", "ptr"):
                pe.wait_ge(pair_free[steps[nm] % 2], steps[nm] // 2 + 1)
            for h in range(2):
                lin_N(f"pg{h}", slot(J[f"pg{h}"], KD), XT, 512)
                lin_N(f"pp{h}", slot(J["pp"], 2, 1024), pT, 512, nk=2, c0=512 * h)
            cT = VT2[:, 32:40]
            for i in range(12):
                w = slot(J[f"mod{i}"], KD)
                o = begin(f"md{i}")
                if i // 2 in (2, 5):
                    for k in range(KD):
                        ins = mm(o[:, 0:512], cT[:, k:k + 1].broadcast_to([P, P]), w[:, k], start=(k == 0),
                                 stop=(k == KD - 1))
                else:
                    for ct in range(4):
                        for k in range(KD):
                            ins = mm(o[:, ct:ct + 1], w[:, k, P * ct:P * ct + P], cT[:, k:k + 1], start=(k == 0),
                                     stop=(k == KD - 1))
                ins.then_inc(PD, 1)
            pe.wait_ge(sem("xn2_ready"), 1)
            transposes("nt0", XN, 0)
            transposes("nt1", XN, 4)
            pe.wait_ge(sem("xT2_ready"), 1)

            def seg(s_, off=0):
                return 32 * (s_ % 4), 512 * (s_ // 4) + off

            lin_T("qa", slot(J["qa"], KD), XT, 4, bias=seg(0))
            wk = slot(J["kva"], KD, 256)
            lin_T("ka", wk, XT, 1, bias=seg(1))
            lin_N("va", wk, XT, 128, c0=128, bias=seg(1, 128))
            lin_T("qb", slot(J["qb"], KD), XT, 4, bias=seg(2))
            lin_T("kb", slot(J["kb"], KD), XT, 4, bias=seg(3))
            lin_N("vb", slot(J["vb"], KD), XT, 512, bias=seg(4))
            lin_T("qc", slot(J["qc"], KD), XT, 4, bias=seg(5))
            wk = slot(J["kvc"], KD)
            lin_T("kc", wk, XT, 2, bias=seg(6))
            lin_T("ksl", wk, XT, 1, c0=256, bias=seg(6, 256))
            lin_N("vsl", wk, XT, 128, c0=384, bias=seg(6, 384))
            wk = slot(J["kvw"], KD, 256)
            lin_T("kwn", wk, XT, 1, bias=seg(7))
            lin_N("vwn", wk, XT, 128, c0=128, bias=seg(7, 128))
            lin_N("gn", wgn, XT, 24, bias=seg(8))
            pe.wait_ge(sem("windows_ready"), 1)
            for j in range(2):
                w = slot(J[f"cw{j}"], 16)
                o = begin(f"c{j}")
                for m in range(2):
                    for l in range(16):
                        ins = mm(o[:, 30 * m:30 * m + 30], w[:, l, P * m:P * m + P],
                                 kexp[:, j, l].rearrange("p h c -> p (h c)"), start=(l == 0), stop=(l == 15))
                ins.then_inc(PD, 1)
            for j in range(2):
                pe.wait_ge(pair_free[steps[f"c{j}"] % 2], steps[f"c{j}"] // 2 + 1)
            o = begin("cc")
            for half in range(2):
                for m in range(2):
                    mm(o[64 * half:64 * half + 64, 0:30], cw2[:, 0, m], hid[:, 0, m], start=(m == 0), stop=(m == 1))
            for h in range(2):
                for m in range(2):
                    ins = mm(o[0:15, 512 + 64 * h:576 + 64 * h], hid[:, 1, m, 15 * h:15 * h + 15], cw2[:, 1, m],
                             start=(m == 0), stop=(m == 1))
            ins.then_inc(PD, 1)
            all_free("cc")
            attention(n_att1, len(chunks))
            pe.wait_ge(sem("branches_ready"), 1)
            for b, o_ in enumerate((Oa, Ob, Oc)):
                transposes(f"bt{b}", o_, 0)
                pe.wait_ge(pair_free[steps[f"bt{b}"] % 2], steps[f"bt{b}"] // 2 + 1)
                for h in range(2):
                    lin_N(f"y{b}{h}", slot(J[f"wb{b}"], 4), hT3[b], 512, nk=4, c0=512 * h)
                    lin_N(f"g{b}{h}", slot(J[f"gm{b}{h}"], KD), XT, 512, bias=seg(9 + 2 * b + h))
            pe.wait_ge(sem("merged2"), 6)
            for h in range(2):
                transposes(f"nt{h + 2}", MRG, 4 * h)
            for h in range(2):
                pe.wait_ge(pair_free[steps[f"nt{h + 2}"] % 2], steps[f"nt{h + 2}"] // 2 + 1)
            for h in range(2):
                lin_N(f"no{h}", slot(J[f"w2o{h}"], KD), AT, 512)
            pe.wait_ge(sem("h3n_ready"), 1)
            transposes("h20", XN, 0)
            transposes("h21", XN, 4)
            pe.wait_ge(sem("h3_ready"), 1)
            lin_N("rt2", wr2, XT, 32)
            rows_back(("hb2", "hb3"))
            ranks(NE2, "rk2", 2)
            pe.wait_ge(sem("b_loaded"), 32)
            o = begin("b1t")
            for c in range(4):
                ins = nc.tensor.transpose(o[:, P * c:P * c + P], b1R[:, c], ident)
            ins.then_inc(PD, 1)
            o = begin("ct")
            for t in range(2):
                ins = nc.tensor.transpose(o[0:32, P * t:P * t + P], comb[:, t], ident)
            ins.then_inc(PD, 1)
            pe.wait_ge(pair_free[steps["ct"] % 2], steps["ct"] // 2 + 1)
            begin("cb")
            for t in range(2):
                for h in range(2):
                    ins = mm(ps[2 + t][:, 512 * h:512 * h + 512], combT[0:32, P * t:P * t + P],
                             b2R[0:32, 512 * h:512 * h + 512], start=True, stop=True)
            ins.then_inc(PD, 1)
            pe.wait_ge(sem("acc_ready"), 1)
            all_free("cb")
            experts(2, base_exp2, NE2, 2, sem("hidden_ready2"))


_OUT = (1, T, D)
_INPUTS = ["x", "p", "mix_norm_g", "w_in", "conv_w", "conv_b", "dt_bias", "a_log", "d_skip", "ssd_norm_g", "w_out_a",
           "w_out_b", "w_out", "ffn_norm_g", "w_rg", "b_rg", "w_re", "b_re", "w_gate", "w_up", "w_down", "w_ple_proj",
           "w_ple_gate", "final_norm_g", "c_2", "mod_w_2", "mod_b_2", "norm1_g_2", "norm2_g_2", "w_in_2", "b_in_2",
           "sinks_2", "diff_lambda_2", "diff_subln_g_2", "cmp_pos_2", "cmp_w1_2", "cmp_b1_2", "cmp_w2_2", "cmp_b2_2",
           "w_branch_2", "w_out_2", "router_w_2", "router_b_2", "exp_w1_2", "exp_b1_2", "exp_w2_2", "exp_b2_2",
           "final_g_2"]


def kernel(**inputs):
    import concourse.bacc as bacc
    from concourse import mybir
    from concourse.bass_utils import run_bass_kernel_spmd

    nc = bacc.Bacc("TRN2", target_bir_lowering=False, num_devices=1)
    arrays, aps = {}, {}
    for name in _INPUTS:
        arr = np.ascontiguousarray(inputs[name])
        arrays[name] = arr
        aps[name] = nc.dram_tensor(name, arr.shape, mybir.dt.from_np(arr.dtype), kind="ExternalInput").ap()
    aps["out"] = nc.dram_tensor("out", _OUT, mybir.dt.float32, kind="ExternalOutput").ap()
    build(nc, aps)
    r = run_bass_kernel_spmd(nc, [arrays], core_ids=[0])
    return r.results[0]["out"]
```

```python
from contextlib import ExitStack

import numpy as np

P = 128
T = 256
NT = T // P
D = 1024
KD = D // P
RING = 6
SLOT = 4096
BIG = 1e30
R_BIG = 12484


def layouts():
    w1 = dict(q=0, k=512, v=1024, z=1536, xbc=2560, dt=4096, ga=4112, gb=5136)
    w2 = dict(qa=0, kva=512, qb=768, kb=1280, vb=1792, qc=2304, kvc=2816, kvw=3328, gn=3584, gm=3608)
    return w1, w2


def build(nc, a):
    import concourse.bass as bass
    from concourse import mybir
    from concourse.alu_op_type import AluOpType as ALU

    F32 = mybir.dt.float32
    U32 = mybir.dt.uint32
    ACT = mybir.ActivationFunctionType
    AX = mybir.AxisListType
    W1, W2 = layouts()
    NE1, NE2 = 16, 32
    ctx = ExitStack()
    with ctx:
        sems = {}

        def sem(name):
            if name not in sems:
                sems[name] = ctx.enter_context(nc.semaphore(name))
            return sems[name]

        def sb(name, cols, dt=F32, parts=P):
            return ctx.enter_context(nc.sbuf_tensor(name, [parts, cols], dt))[:, :]

        ring = sb("ring", RING * SLOT)
        X = sb("x_resid", NT * D).rearrange("p (t n) -> p t n", t=NT)
        XT = sb("x_T", KD * T).rearrange("p (k t) -> p k t", k=KD)
        r_mix = sb("r_mix", 2048)
        XN = r_mix.rearrange("p (t n) -> p t n", t=NT)
        SC = r_mix.rearrange("p (b h k) -> p b h k", b=2, h=4)
        MRG = XN
        r_at = sb("r_at", 2048)
        PT = r_at.rearrange("p (b m q) -> p b m q", b=2, m=8)
        AT = r_at.rearrange("p (k t) -> p k t", k=KD)
        ident = sb("ident", P)
        DM = sb("dist_causal", 512).rearrange("p (t k) -> p t k", t=2)
        DMW = sb("dist_window", 512).rearrange("p (t k) -> p t k", t=2)
        r_u = sb("r_u", 2048)
        U = r_u[:, 0:512].rearrange("p (t k) -> p t k", t=2)
        MK = r_u[:, 512:1024].rearrange("p (t k) -> p t k", t=2)
        GT = r_u[:, 1024:2048].rearrange("p (g s t) -> p g s t", g=2, s=2)
        brow = r_u
        CV = sb("cmp_valid", 30).rearrange("p (t k) -> p t k", t=2)
        CM = sb("cmp_mask", 30).rearrange("p (t k) -> p t k", t=2)
        iota = sb("iota", P)
        io32 = iota[:, 0:32]
        ones = sb("ones", 256)
        VT = sb("vec_T", P)
        VT2 = sb("vec_T2", 40)
        modT = sb("mod_T", 32)
        eps = sb("eps", 2)
        dtb, alog, dsk = sb("dt_bias_b", 16), sb("a_log_b", 16), sb("d_skip_b", 16)
        rb1, rb2 = sb("router_bias1", 20), sb("router_bias2", 32)
        snk, nsnk = sb("sinks_b", 8), sb("neg_sinks_b", 8)
        lamv = sb("lambda_b", 256)
        sub_g = sb("subln_b", P)
        cb2 = sb("cmp_b2_b", 64)
        cb2T = sb("cmp_b2_T", 1)
        cw2 = sb("cmp_w2", 4 * 64).rearrange("p (j k n) -> p j k n", j=2, k=2)
        wr1 = sb("router_w1", KD * 20).rearrange("p (k n) -> p k n", k=KD)
        wr2 = sb("router_w2", KD * 32).rearrange("p (k n) -> p k n", k=KD)
        r_wsm = sb("w_small", KD * 24)
        wdt = r_wsm[:, 0:KD * 16].rearrange("p (k n) -> p k n", k=KD)
        wgn = r_wsm.rearrange("p (k n) -> p k n", k=KD)
        st = sb("stats", 84)
        rt_s = sb("route", 228)
        comb0 = sb("combine", NT * 33).rearrange("p (t e) -> p t e", t=NT)
        comb = comb0[:, :, 1:33]
        rank = sb("rank", NT * 33).rearrange("p (t e) -> p t e", t=NT)
        sizes = sb("sizes", 34, mybir.dt.int32)
        r_big = sb("r_big", R_BIG)
        used = [0]

        def take(n):
            used[0] += n
            assert used[0] <= R_BIG, used[0]
            return r_big[:, used[0] - n:used[0]]

        qT = take(1024).rearrange("p (c t) -> p c t", c=4)
        kT = take(1024).rearrange("p (c t) -> p c t", c=4)
        v1 = take(1024).rearrange("p (t n) -> p t n", t=2)
        O1 = take(1024).rearrange("p (t n) -> p t n", t=2)
        silz = take(2048).rearrange("p (t n) -> p t n", t=2)
        xbcP = take(12 * 259).rearrange("p (c t) -> p c t", c=12)
        cvT = take(3072).rearrange("p (c t) -> p c t", c=12)
        ssd_small = take(5 * 32)
        xs = r_big[:, 0:2048].rearrange("p (t n) -> p t n", t=2)
        xdt = XN
        Y = xbcP.rearrange("p c t -> p (c t)")[:, 0:2048].rearrange("p (t n) -> p t n", t=2)
        Mt = cvT.rearrange("p c t -> p (c t)").rearrange("p (b h n) -> p b h n", b=2, h=4)
        OT = r_big[:, 2048:3072].rearrange("p (c t) -> p c t", c=4)
        sg = r_big[:, 3072:4096].rearrange("p (t n) -> p t n", t=2)
        pin = r_big[:, 0:512].rearrange("p (t n) -> p t n", t=2)
        pT = r_big[:, 512:1024].rearrange("p (c t) -> p c t", c=2)
        growB = r_big[:, 4096:5120]
        used1 = used[0]
        used[0] = 5120
        HID = take(2048).rearrange("p (b n) -> p b n", b=2)
        GS = take(1024)
        US = take(1024)
        SG = take(1024)
        ACC = take(2048).rearrange("p (t n) -> p t n", t=2)
        b1q = r_big[:, 0:1024].rearrange("p (b n) -> p b n", b=2)
        HIDT = r_big[:, 1024:3072].rearrange("p (b n) -> p b n", b=2)
        b2R = r_big[:, 1024:2048]
        combT = r_big[:, 2048:2304]
        pick = r_big[:, 3072:3584].rearrange("p (b t s) -> p b t s", b=2, t=NT)
        tri = r_big[:, 3072:3584].rearrange("p (t k) -> p t k", t=NT)
        pickT = r_big[:, 3584:3840]
        YS = r_at[:, 0:1024]
        XG = r_at[:, 1024:2048].rearrange("p (k s) -> p k s", k=KD)
        HT = XN
        used[0] = 0
        qa = take(1024).rearrange("p (c t) -> p c t", c=4)
        qb = take(1024).rearrange("p (c t) -> p c t", c=4)
        kb = take(1024).rearrange("p (c t) -> p c t", c=4)
        vb = take(1024).rearrange("p (t n) -> p t n", t=2)
        qc = take(1024).rearrange("p (c t) -> p c t", c=4)
        ka = take(512).rearrange("p (h t) -> p h t", h=2)
        ksl = take(512).rearrange("p (h t) -> p h t", h=2)
        kwn = take(512).rearrange("p (h t) -> p h t", h=2)
        va = take(256).rearrange("p (t n) -> p t n", t=2)
        vsl = take(256).rearrange("p (t n) -> p t n", t=2)
        vwn = take(256).rearrange("p (t n) -> p t n", t=2)
        kraw = take(512).rearrange("p (j t) -> p j t", j=2)
        kexp = take(960).rearrange("p (j l h c) -> p j l h c", j=2, l=16, h=2)
        hid = take(120).rearrange("p (j m c) -> p j m c", j=2, m=2)
        kcmp = take(30).rearrange("p (h c) -> p h c", h=2)
        vcmp = take(128).rearrange("p (h n) -> p h n", h=2)
        gts = take(48).rearrange("p (t n) -> p t n", t=2)
        Oa = take(1024).rearrange("p (t n) -> p t n", t=2)
        Ob = take(1024).rearrange("p (t n) -> p t n", t=2)
        Oc = take(1024).rearrange("p (t n) -> p t n", t=2)
        tmpO = kraw.rearrange("p j t -> p (j t)")
        hT3 = [x for x in (qb, kb, qc)]
        sg2 = qa.rearrange("p c t -> p (c t)").rearrange("p (t n) -> p t n", t=2)
        G12 = sb("mod_gates", 2048).rearrange("p (g n) -> p g n", g=2)

        mod_sum = G12[:, 1].rearrange("p (b n) -> p b n", b=2)
        gate_sum = r_at[:, 0:1024].rearrange("p (b n) -> p b n", b=2)
        growA = G12[:, 0]
        growF = r_u[:, 0:1024]

        ps = [ctx.enter_context(nc.psum_tensor(f"pair{i}", [P, 1024], F32))[:, :] for i in range(4)]

        def blk(w, r0, nk, c0, n):
            return w[r0:r0 + nk * P, c0:c0 + n].rearrange("(t p) n -> p t n", p=P)

        items, item_at = [], {}

        def item(name, w, r0, nk, c0, n):
            item_at[name] = len(items)
            items.append((blk(w, r0, nk, c0, n), nk, n))

        w_in, w_in2 = a["w_in"][0], a["w_in_2"][0]
        mods_early, mods_late = (0, 1, 2, 3, 6, 7, 8, 9), (10, 11, 4, 5)
        for m, (nm, c0) in zip(mods_early[0:6], (("k", W1["k"]), ("v", W1["v"]), ("z0", W1["z"]), ("z1", W1["z"] + 512),
                                                 ("x0", W1["xbc"]), ("x1", W1["xbc"] + 512))):
            if nm == "k":
                item("q", w_in, 0, KD, W1["q"], 512)
            item(nm, w_in, 0, KD, c0, 512)
            item(f"mod{m}", a["mod_w_2"][0], 0, KD, 512 * m, 512)
        item("x2", w_in, 0, KD, W1["xbc"] + 1024, 512)
        item("woa", a["w_out_a"][0], 0, 4, 0, 1024)
        item("ga0", w_in, 0, KD, W1["ga"], 512)
        item("ga1", w_in, 0, KD, W1["ga"] + 512, 512)
        for m in mods_early[6:8]:
            item(f"mod{m}", a["mod_w_2"][0], 0, KD, 512 * m, 512)
        for h in range(2):
            item(f"wob{h}", a["w_out_b"][0], 0, KD, 512 * h, 512)
            item(f"gb{h}", w_in, 0, KD, W1["gb"] + 512 * h, 512)
        for h in range(2):
            item(f"wo{h}", a["w_out"][0], 0, KD, 512 * h, 512)
        n_front1 = len(items)
        moe1_slot = n_front1 % RING
        front1 = list(items)
        items.clear()
        after1 = {}

        def item2(name, w, r0, nk, c0, n):
            after1[name] = len(items)
            items.append((blk(w, r0, nk, c0, n), nk, n))

        for h in range(2):
            item2(f"pg{h}", a["w_ple_gate"][0], 0, KD, 512 * h, 512)
        item2("pp", a["w_ple_proj"][0], 0, 2, 0, 1024)
        for i in (4, 5, 10, 11):
            item2(f"mod{i}", a["mod_w_2"][0], 0, KD, 512 * i, 512)
        for nm, c0, n in (("qa", W2["qa"], 512), ("kva", W2["kva"], 256), ("qb", W2["qb"], 512), ("kb", W2["kb"], 512),
                          ("vb", W2["vb"], 512), ("qc", W2["qc"], 512), ("kvc", W2["kvc"], 512),
                          ("kvw", W2["kvw"], 256)):
            item2(nm, w_in2, 0, KD, c0, n)
        for j in range(2):
            item2(f"cw{j}", a["cmp_w1_2"][0, j], 0, 16, 0, 256)
        for b in range(3):
            item2(f"wb{b}", a["w_branch_2"][0, b], 0, 4, 0, 1024)
            for h in range(2):
                item2(f"gm{b}{h}", w_in2, 0, KD, W2["gm"] + 1024 * b + 512 * h, 512)
        for h in range(2):
            item2(f"w2o{h}", a["w_out_2"][0], 0, KD, 512 * h, 512)
        front2 = list(items)
        n1_exp, n2_exp = NE1, 2 * NE2
        base_mid = n_front1 + 3 * n1_exp
        base_exp2 = base_mid + len(front2)

        steps = {}
        seq = []

        def step(name, *names):
            for nm in (name,) + names:
                steps[nm] = len(seq)
                seq.append(nm)

        step("vec", "xt0", "xt1", "q", "k", "md0", "v", "md1", "z0", "md2", "z1", "md3", "x0", "md6",
             "x1", "md7", "x2", "dt")
        step("G", "xsT0", "xsT1", "xsT2", "xsT3", "cs", "cb0", "cb1", "cb2", "cb3")
        step("ot1", "a0", "ga0", "a1", "ga1", "yt0", "yt1", "b0", "gb0", "md8", "md9", "b1", "gb1")
        step("mt0", "mt1", "wo0", "wo1", "ht0", "ht1", "rt1", "hb0", "hb1", "rk1")
        n_s1 = len(seq)
        step("p0", "p1", "ptr", "pg0", "pp0", "pg1", "pp1")
        step("md10", "md11", "md4", "md5")
        step("nt0", "nt1", "qa", "ka", "va", "qb", "kb", "vb", "qc", "kc", "ksl", "vsl", "kwn", "vwn", "gn")
        step("c0", "c1", "cc")
        for b in range(3):
            step(f"bt{b}", f"y{b}0", f"g{b}0", f"y{b}1", f"g{b}1")
        step("nt2", "nt3", "no0", "no1", "h20", "h21", "rt2", "hb2", "hb3", "rk2", "ct", "cb")
        last_step_of_item = dict(q="q", k="k", v="v", z0="z0", z1="z1", x0="x0", x1="x1", x2="x2", woa="a1", ga0="ga0",
                                 ga1="ga1", wob0="b0", gb0="gb0", wob1="b1", gb1="gb1", wo0="wo0", wo1="wo1",
                                 pg0="pg0", pg1="pg1", pp="pp1", qa="qa", kva="va", qb="qb", kb="kb", vb="vb",
                                 qc="qc", kvc="vsl", kvw="vwn", cw0="c0", cw1="c1", w2o0="no0", w2o1="no1")
        for i in range(12):
            last_step_of_item[f"mod{i}"] = f"md{i}"
        for b in range(3):
            last_step_of_item[f"wb{b}"] = f"y{b}1"
            for h in range(2):
                last_step_of_item[f"gm{b}{h}"] = f"g{b}{h}"

        def done_value(name):
            n = steps[name] + 1
            return n if steps[name] < n_s1 else n + 3 * n1_exp

        base_pd2 = len(seq) + 3 * n1_exp
        PD = sem("products_done")
        pair_free = [sem("pair0_free"), sem("pair1_free")]
        gate_free, up_free = sem("gate_psum_free"), sem("up_psum_free")
        slot_loaded = [sem(f"slot{i}_loaded") for i in range(RING)]

        def pair(name):
            return ps[steps[name] % 2]

        def uses_before(j):
            return 16 * (j // RING + 1)

        def slopes(n):
            return [2.0 ** (-8.0 * (i + 1) / n) for i in range(n)]

        chunks = []

        def add_maps(kind, tag, w=64):
            for qt in range(NT):
                for hc in range(2):
                    chunks.append((kind, tag, qt, hc, w))

        add_maps("moba", 0)
        n_att1 = len(chunks)
        add_maps("swa", 0)
        add_maps("diff", 0, 128)
        add_maps("cmp", 0)
        add_maps("slc", 0)
        add_maps("win", 0)

        def map_operands(kind, h):
            lo = 64 * (h % 2)
            r = slice(lo, lo + 64)
            if kind == "moba":
                return qT[r, h // 2], kT[r, h // 2]
            if kind == "swa":
                return qa[r, h // 2], ka[r, h // 4]
            if kind == "diff":
                return qb[r, h // 2], kb[r, h // 2]
            k = {"cmp": kcmp, "slc": ksl, "win": kwn}[kind]
            return qc[r, h // 2], k[r, h // 4]

        def map_values(kind, h, kt):
            if kind == "moba":
                return v1[:, kt, 64 * h:64 * h + 64]
            if kind == "diff":
                return vb[:, kt, 128 * (h // 2):128 * (h // 2) + 128]
            if kind == "cmp":
                return vcmp[0:15, h // 4, :]
            vv = {"swa": va, "slc": vsl, "win": vwn}[kind]
            return vv[:, kt, 64 * (h // 4):64 * (h // 4) + 64]

        def score_col(h):
            return 512 * (h % 2) + 256 * (h // 2)

        def map_slope(kind, h):
            return slopes(4)[h // 2] if kind == "diff" else slopes(8)[h]

        nm_s = st[:, 0:8].rearrange("p (b h) -> p b h", b=2)
        rs_s = st[:, 8:16].rearrange("p (b h) -> p b h", b=2)
        es_s = st[:, 16:24].rearrange("p (b h) -> p b h", b=2)
        rv_s = st[:, 24:28]
        lam_s = st[:, 28:36]
        ss_s = st[:, 36:52]
        g8 = st[:, 52:60]
        m8 = st[:, 60:68]
        i8 = sb("top_index", 8, U32)
        f8 = st[:, 68:76]
        w8 = st[:, 76:84]

        n_vec, n_small, n_p = 11, 19, 20

        block = ctx.enter_context(nc.Block())

        H2 = P // 2

        def size_of(eng, e):
            return eng.value_load(sizes[0:1, bass.ds(e + 1, 1)], min_val=0, max_val=2)

        def by_size(eng, size, body):
            for c, w in enumerate((H2, P, T)):
                with eng.If(size == c):
                    body(w)

        @block.sync
        def _(sp):
            loads = {}

            def load(dst, src, s="vectors_loaded"):
                loads[s] = loads.get(s, 0) + 1
                sp.dma_start(dst, src).then_inc(sem(s), 16)

            def ring_load(j, ap, nk, n, wait):
                if wait is not None:
                    sp.wait_ge(PD, wait)
                s = j % RING
                dst = ring[:, s * SLOT:s * SLOT + nk * n].rearrange("p (t n) -> p t n", t=nk)
                sp.dma_start(dst, ap).then_inc(slot_loaded[s], 16)

            read_at = []
            for nm, idx in item_at.items():
                read_at.append(done_value(last_step_of_item[nm]))
            for k in range(3 * n1_exp):
                read_at.append(n_s1 + k + 1)
            for nm, idx in after1.items():
                read_at.append(done_value(last_step_of_item[nm]))

            load(X[:, :, :], a["x"][0].rearrange("(t p) n -> p t n", p=P), "x_loaded")
            r0 = 0
            vr = XT.rearrange("p k t -> p (k t)")[:, 0:P]
            vr2 = XT.rearrange("p k t -> p (k t)")[:, P:2 * P]
            for src, n in ((a["mix_norm_g"][0], 8), (a["ffn_norm_g"][0], 8), (a["norm1_g_2"][0], 8),
                           (a["norm2_g_2"][0], 8), (a["conv_b"][0], 12)):
                load(vr[r0:r0 + n, :], src.rearrange("(r n) -> r n", n=P))
                r0 += n
            load(vr[r0:r0 + 48, :], a["conv_w"][0].rearrange("k (r n) -> (k r) n", n=P))
            load(vr[92:108, :], a["mod_b_2"][0, 0:2048].rearrange("(r n) -> r n", n=P))
            load(vr[108:124, :], a["mod_b_2"][0, 3072:5120].rearrange("(r n) -> r n", n=P))
            load(vr[124:128, :], a["cmp_b1_2"][0].rearrange("j (r n) -> (j r) n", n=P))
            load(vr2[0:32, :], a["cmp_pos_2"][0].rearrange("j (l r) d -> (j l) (r d)", r=2))
            load(vr2[32:40, :], a["c_2"][0].rearrange("(r n) -> r n", n=P))
            for j in range(RING):
                ap, nk, n = front1[j]
                ring_load(j, ap, nk, n, None)
            load(wdt[:, :, :], blk(w_in, 0, KD, W1["dt"], 16), "small_loaded")
            load(wr1[:, :, 0:4], blk(a["w_rg"][0], 0, KD, 0, 4), "small_loaded")
            load(wr1[:, :, 4:20], blk(a["w_re"][0], 0, KD, 0, 16), "small_loaded")
            load(wr2[:, :, :], blk(a["router_w_2"][0], 0, KD, 0, 32), "small_loaded")
            for j in range(2):
                load(cw2[:, j], blk(a["cmp_w2_2"][0, j], 0, 2, 0, 64), "small_loaded")
            for half in range(2):
                load(cb2T[64 * half:64 * half + 64, :], a["cmp_b2_2"][0, 0].rearrange("(n o) -> n o", o=1), "small_loaded")
            for dst, src in ((dtb, a["dt_bias"][0]), (alog, a["a_log"][0]), (dsk, a["d_skip"][0]),
                             (rb1[:, 0:4], a["b_rg"][0]), (rb1[:, 4:20], a["b_re"][0]), (rb2, a["router_b_2"][0]),
                             (snk, a["sinks_2"][0]), (lamv, a["diff_lambda_2"][0].rearrange("a b -> (a b)")),
                             (sub_g, a["diff_subln_g_2"][0]),
                             (cb2, a["cmp_b2_2"][0, 1]),
                             (growA, a["ssd_norm_g"][0])):
                load(dst, src.rearrange("(o n) -> o n", o=1).broadcast_to([P, src.shape[0]]), "small_loaded")
            assert loads["vectors_loaded"] == n_vec and loads["small_loaded"] == n_small
            starts = [(W2["qa"], 512), (W2["kva"], 256), (W2["qb"], 512), (W2["kb"], 512), (W2["vb"], 512),
                      (W2["qc"], 512), (W2["kvc"], 512), (W2["kvw"], 256), (W2["gn"], 24)] + \
                     [(W2["gm"] + 512 * i, 512) for i in range(6)]
            for j in range(RING, n_front1):
                ap, nk, n = front1[j]
                ring_load(j, ap, nk, n, read_at[j - RING])
            wg = a["w_gate"][0].rearrange("e d f -> (e d) f")
            wu = a["w_up"][0].rearrange("e d f -> (e d) f")
            wd = a["w_down"][0].rearrange("e f d -> (e f) d")

            def expert1(slot, kind, e, wait):
                w, nk, n = ((wg, KD, 512), (wu, KD, 512), (wd, 4, 1024))[kind]
                sp.wait_ge(PD, wait)
                src = w[bass.ds(e * (nk * P), nk * P), :].rearrange("(t p) n -> p t n", p=P)
                dst = ring[:, slot * SLOT:(slot + 1) * SLOT].rearrange("p (t n) -> p t n", t=nk)
                sp.dma_start(dst, src).then_inc(slot_loaded[slot], 16)

            j = n_front1

            def pair1(i, wait_of):
                for k in range(6):
                    expert1((j + k) % RING, k % 3, 2 * i + k // 3, wait_of(k))

            pair1(0, lambda k: read_at[j + k - RING])
            with sp.Fori(1, n1_exp // 2) as i:
                pair1(i, lambda k: 6 * i + (n_s1 + k - RING + 1))
            assert j + 3 * n1_exp == base_mid
            sp.wait_ge(sem("ssd_gated"), 1)
            sp.wait_ge(sem("h2_ready"), 1)
            for s, (c0, n) in enumerate(starts):
                load(brow[32 * (s % 4):32 * (s % 4) + 1, 512 * (s // 4):512 * (s // 4) + n],
                     a["b_in_2"][0:1, c0:c0 + n], "p_loaded")
            load(pin[:, :, :], a["p"][0, 0].rearrange("(t p) n -> p t n", p=P), "p_loaded")
            for dst, src in ((growB, a["final_norm_g"]), (G12[:, 0], a["mod_b_2"][0, 2048:3072]),
                             (G12[:, 1], a["mod_b_2"][0, 5120:6144])):
                load(dst, src.rearrange("(o n) -> o n", o=1).broadcast_to([P, D]), "p_loaded")
            load(wgn[:, :, :], blk(w_in2, 0, KD, W2["gn"], 24), "p_loaded")
            assert loads["p_loaded"] == n_p
            for k, (ap, nk, n) in enumerate(front2):
                ring_load(base_mid + k, ap, nk, n, read_at[base_mid + k - RING])
            w1e = a["exp_w1_2"][0].rearrange("e d f -> (e d) f")
            w2e = a["exp_w2_2"][0].rearrange("e f d -> (e f) d")

            def expert2(slot, kind, e, half, wait):
                sp.wait_ge(PD, wait)
                if kind < 2:
                    src = w1e[bass.ds(e * D, D), 1024 * kind + 512 * half:1024 * kind + 512 * half + 512]
                    nk = KD
                else:
                    src = w2e[bass.ds(e * D + 512 * half, 512), :]
                    nk = 4
                dst = ring[:, slot * SLOT:(slot + 1) * SLOT].rearrange("p (t n) -> p t n", t=nk)
                sp.dma_start(dst, src.rearrange("(t p) n -> p t n", p=P)).then_inc(slot_loaded[slot], 16)

            j = base_exp2
            b1e = a["exp_b1_2"][0].rearrange("e (q n) -> (e q) n", q=4)
            parts2 = ((0, 0), (1, 0), (0, 1), (1, 1), (2, 0), (2, 1))

            def pair2(i, wait_of, first=False):
                for k in range(12):
                    kind, half = parts2[k % 6]
                    if k % 6 == 0 and not first:
                        sp.wait_ge(PD, wait_of(k))
                        sp.dma_start(b1q[0:97:32, k // 6], b1e[bass.ds(8 * i + 4 * (k // 6), 4), :])\
                            .then_inc(sem(f"b1_loaded{k // 6}"), 16)
                    expert2((j + k) % RING, kind, 2 * i + k // 6, half, wait_of(k))

            pair2(0, lambda k: read_at[k - RING] if k < RING else base_pd2 + k - RING + 1, first=True)
            with sp.Fori(1, NE2 // 2) as i:
                pair2(i, lambda k: 12 * i + (base_pd2 + k - RING + 1))
            for t in range(NT):
                sp.wait_ge(sem("out_ready"), t + 1)
                sp.dma_start(a["out"][0, P * t:P * t + P, :], X[:, t]).then_inc(sem("stored"), 16)
            sp.wait_ge(sem("stored"), 16 * NT)

        @block.gpsimd
        def _(pool):
            cnt = [0]

            def link(ins):
                cnt[0] += 1
                ins.then_inc(sem("pool_step"), 1)
                pool.wait_ge(sem("pool_step"), cnt[0])

            g = nc.gpsimd
            link(g.memset(ident, 0.0))
            link(g.affine_select(out=ident, in_=ident, pattern=[[-1, P]], compare_op=ALU.not_equal, fill=1.0, base=0,
                                 channel_multiplier=1))
            link(g.iota(DM, pattern=[[P, 2], [-1, T]], base=0, channel_multiplier=1,
                        allow_small_or_imprecise_dtypes=True))
            link(g.affine_select(out=DM, in_=DM, pattern=[[P, 2], [-1, T]], compare_op=ALU.is_ge, fill=BIG, base=0,
                                 channel_multiplier=1))
            link(g.affine_select(out=DMW, in_=DM, pattern=[[-P, 2], [1, T]], compare_op=ALU.is_ge, fill=BIG,
                                 base=127, channel_multiplier=-1))
            link(g.memset(U, 1.0))
            link(g.memset(MK, 0.0))
            for t, fill in ((U, 0.0), (MK, -BIG)):
                link(g.affine_select(out=t, in_=t, pattern=[[-P, 2], [1, T]], compare_op=ALU.is_ge, fill=fill, base=0,
                                     channel_multiplier=-1))
            link(g.memset(CV, 1.0))
            link(g.memset(CM, 0.0))
            for t, fill in ((CV, 0.0), (CM, -BIG)):
                link(g.affine_select(out=t, in_=t, pattern=[[P, 2], [-16, 15]], compare_op=ALU.is_ge, fill=fill,
                                     base=-31, channel_multiplier=1))
            link(g.iota(iota, pattern=[[1, P]], base=0, channel_multiplier=0, allow_small_or_imprecise_dtypes=True))
            link(g.memset(ones, 1.0))
            link(g.memset(eps[:, 0:1], 1e-6))
            link(g.memset(eps[:, 1:2], 1e-5))
            link(g.memset(g8, -BIG))
            g.memset(xbcP[:, :, 0:3], 0.0).then_inc(sem("constants_ready"), 1)

        @block.scalar
        def _(act):
            s = nc.scalar
            cnt = {}

            def link(ins, name="act_step"):
                cnt[name] = cnt.get(name, 0) + 1
                ins.then_inc(sem(name), 1)
                act.wait_ge(sem(name), cnt[name])

            def products(name):
                act.wait_ge(PD, done_value(name))

            def freed(ins, name):
                ins.then_inc(pair_free[steps[name] % 2], 1)
                act.wait_ge(pair_free[steps[name] % 2], steps[name] // 2 + 1)

            def square_sums(src, dst, nseg, width, scr):
                for t in range(NT):
                    for g in range(nseg):
                        link(s.activation(scr, src[:, t, g * width:(g + 1) * width], ACT.Square,
                                          accum_out=dst[:, t * nseg + g:t * nseg + g + 1]))

            def rms(src, eps_col, name, nseg=1, width=D, scr=None):
                square_sums(src, ss_s, nseg, width, scr)
                link(s.activation(ss_s[:, 0:NT * nseg], ss_s[:, 0:NT * nseg], ACT.Sqrt, bias=eps[:, eps_col:eps_col + 1],
                                  scale=1.0 / width), name)

            def attention(c0, c1):
                for c in range(c0, c1):
                    kind, _, qt, hc, w = chunks[c]
                    b = c % 2
                    nk = 15 if kind == "cmp" else P * (qt + 1)
                    act.wait_ge(sem("scores_biased"), c + 1)
                    if kind == "swa":
                        link(s.activation(es_s[:, b], es_s[:, b], ACT.Exp))
                    for h in range(4):
                        ins = s.activation(SC[:, b, h, 0:nk], SC[:, b, h, 0:nk], ACT.Exp, bias=nm_s[:, b, h:h + 1],
                                           accum_out=rs_s[:, b, h:h + 1])
                    ins.then_inc(sem("probs_ready"), 1)
                    act.wait_ge(sem("probs_transposed"), c + 1)
                    nt = 1 if kind == "cmp" else qt + 1
                    rows = 15 if kind == "cmp" else P
                    if c >= 2:
                        act.wait_ge(sem("outputs_done"), c - 1)
                    s.copy(PT[0:rows, b, 0:4 * nt], ps[2][0:rows, 0:512 * nt]).then_inc(sem("probsT_ready"), 1)

            act.wait_ge(sem("constants_ready"), 1)
            act.wait_ge(sem("x_loaded"), 16)
            rms(X, 0, "rms_ready", scr=XN[:, 0])
            products("vec")
            link(s.copy(VT, ps[0][:, 0:P]))
            link(s.copy(VT2[:, 0:32], ps[0][:, P:P + 32]))
            freed(s.activation(VT2[:, 32:40], ps[0][:, P + 32:P + 40], ACT.Silu), "vec")
            products("q")
            freed(s.mul(qT, ps[steps["q"] % 2], 0.125), "q")
            products("k")
            freed(s.copy(kT, pair("k")), "k")
            products("v")
            freed(s.copy(v1, pair("v")), "v")
            for h in range(2):
                products(f"z{h}")
                freed(s.activation(silz[:, :, 512 * h:512 * h + 512], pair(f"z{h}").rearrange("p (t n) -> p t n", t=2),
                                   ACT.Silu), f"z{h}")
            for h in range(3):
                products(f"x{h}")
                freed(s.copy(xbcP[:, 4 * h:4 * h + 4, 3:259], pair(f"x{h}").rearrange("p (c t) -> p c t", c=4)), f"x{h}")
            act.wait_ge(sem("conv_done"), 1)
            link(s.activation(cvT, cvT, ACT.Silu), "conv_ready")
            act.wait_ge(sem("small_loaded"), 16 * n_small)
            act.wait_ge(sem("dt_raw"), 1)
            dr, dabs, dtt, dA, ncs = [ssd_small[:, 32 * k:32 * k + 32] for k in range(5)]
            link(s.activation(dabs, dr, ACT.Abs))
            link(s.activation(dabs, dabs, ACT.Exp, scale=-1.0))
            link(s.activation(dA[:, 0:16], alog, ACT.Exp))
            link(s.activation(dabs, dabs, ACT.Ln, bias=ones[:, 0:1]), "dt_logs")
            attention(0, n_att1)
            for g in range(4):
                act.wait_ge(sem("decay_biased"), g + 1)
                s.activation(Mt[:, g % 2], Mt[:, g % 2], ACT.Exp).then_inc(sem("decay_exp"), 1)
            for h in range(2):
                products(f"ga{h}")
                if h:
                    act.wait_ge(sem("merged"), 1)
                freed(s.activation(sg, pair(f"ga{h}"), ACT.Sigmoid), f"ga{h}")
            act.wait_ge(sem("ssd_gated"), 1)
            rms(Y, 0, "rms_ready", nseg=2, width=512, scr=AT.rearrange("p k t -> p (k t)")[:, 0:512])
            for h in range(2):
                products(f"gb{h}")
                act.wait_ge(sem("merged"), 2 + h)
                freed(s.activation(sg, pair(f"gb{h}"), ACT.Sigmoid), f"gb{h}")
            for t in range(2):
                products(f"mt{t}")
                freed(s.copy(AT[:, 4 * t:4 * t + 4], pair(f"mt{t}")), f"mt{t}")
            act.wait_ge(sem("resid_ready"), 1)
            act.wait_ge(PD, done_value("wo1"))
            rms(X, 0, "rms_ready", scr=AT.rearrange("p k t -> p (k t)")[:, 0:1024])

            def rows_back(names):
                for t in range(NT):
                    products(names[t])
                    freed(s.copy(HT[:, t], pair(names[t])), names[t])

            rows_back(("hb0", "hb1"))
            act.wait_ge(sem("route_exp"), 1)
            for t in range(NT):
                link(s.activation(rt_s[:, 64 * t:64 * t + 5], rt_s[:, 64 * t:64 * t + 5], ACT.Exp), "route_exped")

            def rows_of(b, e):
                got = ps[b - 1].rearrange("p (k s) -> p k s", k=KD)

                def body(w):
                    n = min(w, P)
                    act.wait_ge(sem(f"gathered{b}"), e + 1)
                    s.copy(XG[:, :, 0:n], got[:, :, 0:n]).then_inc(sem(f"xg_ready{b}"), 1)

                return body

            def turned(b, half, e, w):
                act.wait_ge(sem(f"hidden_turned{b}"), b * e + (half + 1))
                s.copy(HIDT[:, half, 0:4 * w], ps[2 - b][:, 0:4 * w]).then_inc(sem(f"hiddenT_ready{b}"), 1)

            def outputs_and_picks(b, e, w, pd_down):
                n = 512 if w == H2 else 1024
                act.wait_ge(PD, pd_down)
                s.copy(YS[:, 0:n], ps[2][:, 0:n]).then_inc(sem(f"ys_ready{b}"), 1)
                act.wait_ge(sem(f"pick_turned{b}"), e + 1)
                s.copy(pickT, ps[1][:, 0:256]).then_inc(sem(f"pickT_ready{b}"), 1)

            act.wait_ge(sem("gathered1"), 1)
            by_size(act, size_of(act, 0), rows_of(1, 0))
            with act.Fori(0, n1_exp) as e:
                size, size_next = size_of(act, e), size_of(act, e + 1)

                def body(w):
                    act.wait_ge(PD, 3 * e + (n_s1 + 1))
                    act.wait_ge(sem("sg_free"), e + 1)
                    s.activation(SG[:, 0:4 * w], ps[0][:, 0:4 * w], ACT.Silu).then_inc(gate_free, 1)
                    turned(1, 0, e, w)
                    by_size(act, size_next, rows_of(1, e + 1))
                    outputs_and_picks(1, e, w, 3 * e + (n_s1 + 3))

                by_size(act, size, body)
            for h in range(2):
                products(f"p{h}")
                freed(s.copy(XT[:, 4 * h:4 * h + 4], pair(f"p{h}")), f"p{h}")
            products("ptr")
            freed(s.copy(pT, pair("ptr")[:, 0:512]), "ptr")
            for h in range(2):
                products(f"pg{h}")
                if h:
                    act.wait_ge(sem("ple_added"), 1)
                freed(s.activation(sg, pair(f"pg{h}"), ACT.Sigmoid), f"pg{h}")
            act.wait_ge(sem("ple_added"), 2)
            rms(X, 0, "rms_ready", scr=XN[:, 0])
            act.wait_ge(sem("x2_ready"), 1)
            rms(X, 1, "rms_ready", scr=XN[:, 0])
            products("qa")
            freed(s.mul(qa, pair("qa"), 0.125), "qa")
            for nm, dst in (("ka", ka), ("ksl", ksl), ("kwn", kwn)):
                products(nm)
                src = pair(nm)[:, 0:256]
                for half in range(2):
                    for h in range(2):
                        ins = s.copy(dst[64 * half:64 * half + 64, h], src[64 * h:64 * h + 64])
                        if half and h:
                            freed(ins, nm)
                        else:
                            link(ins)
                if nm == "ka":
                    products("va")
                    freed(s.copy(va, pair("va").rearrange("p (t n) -> p t n", t=2)[:, :, 0:128]), "va")
                    products("qb")
                    freed(s.mul(qb, pair("qb"), 0.125), "qb")
                    for nm2, dst2 in (("kb", kb), ("vb", vb)):
                        products(nm2)
                        freed(s.copy(dst2, pair(nm2)), nm2)
                    products("qc")
                    freed(s.mul(qc, pair("qc"), 0.125), "qc")
                    products("kc")
                    freed(s.copy(kraw, pair("kc")[:, 0:512]), "kc")
                if nm == "ksl":
                    products("vsl")
                    freed(s.copy(vsl, pair("vsl").rearrange("p (t n) -> p t n", t=2)[:, :, 0:128]), "vsl")
                if nm == "kwn":
                    products("vwn")
                    freed(s.copy(vwn, pair("vwn").rearrange("p (t n) -> p t n", t=2)[:, :, 0:128]), "vwn")
            products("gn")
            freed(s.activation(gts, pair("gn").rearrange("p (t n) -> p t n", t=2)[:, :, 0:24], ACT.Sigmoid), "gn")
            for j in range(2):
                products(f"c{j}")
                for m in range(2):
                    ins = s.activation(hid[:, j, m], pair(f"c{j}")[:, 30 * m:30 * m + 30], ACT.Gelu_apprx_tanh,
                                       bias=VT[:, 124 + 2 * j + m:125 + 2 * j + m])
                    if m:
                        freed(ins, f"c{j}")
                    else:
                        link(ins)
            products("cc")
            act.wait_ge(sem("lambda_sums"), 1)
            link(s.activation(lam_s[:, 0:2], lam_s[:, 0:2], ACT.Exp), "lambda_exp")
            attention(n_att1, len(chunks))
            act.wait_ge(sem("diff_squares"), 1)
            link(s.activation(ss_s[:, 0:8], ss_s[:, 0:8], ACT.Sqrt, bias=eps[:, 1:2], scale=1.0 / P), "diff_rms")
            k = 0
            for b in range(3):
                for h in range(2):
                    products(f"g{b}{h}")
                    if k:
                        act.wait_ge(sem("merged2"), k)
                    freed(s.activation(sg2, pair(f"g{b}{h}"), ACT.Sigmoid), f"g{b}{h}")
                    k += 1
            for t in range(2):
                products(f"nt{t + 2}")
                freed(s.copy(AT[:, 4 * t:4 * t + 4], pair(f"nt{t + 2}")), f"nt{t + 2}")
            act.wait_ge(sem("resid2_ready"), 1)
            b1e = a["exp_b1_2"][0].rearrange("e (q n) -> (e q) n", q=4)
            for par in range(2):
                act.dma_start(b1q[0:97:32, par], b1e[4 * par:4 * par + 4, :]).then_inc(sem(f"b1_loaded{par}"), 16)
            act.dma_start(b2R[0:32, :], a["exp_b2_2"][0]).then_inc(sem("b2_loaded"), 16)
            act.dma_start(growF, a["final_g_2"].rearrange("(o n) -> o n", o=1).broadcast_to([P, D]))\
                .then_inc(sem("last_gain_loaded"), 16)
            rms(X, 1, "rms_ready", scr=AT.rearrange("p k t -> p (k t)")[:, 0:1024])
            rows_back(("hb2", "hb3"))
            for t in range(2):
                act.wait_ge(sem("route2_exp"), t + 1)
                link(s.activation(w8[:, 4 * t:4 * t + 4], w8[:, 4 * t:4 * t + 4], ACT.Exp,
                                  accum_out=rt_s[:, 224 + t:225 + t]), "route2_exped")

            act.wait_ge(sem("gathered2"), 1)
            by_size(act, size_of(act, 0), rows_of(2, 0))
            with act.Fori(0, NE2) as e:
                size, size_next = size_of(act, e), size_of(act, e + 1)

                def body(w):
                    for half in range(2):
                        act.wait_ge(sem("gate_limited"), 2 * e + (1 + half))
                        if half:
                            act.wait_ge(sem("hidden_ready2"), 2 * e + 1)
                        s.activation(SG[:, 0:4 * w], GS[:, 0:4 * w], ACT.Sigmoid, scale=1.702)\
                            .then_inc(sem("sig_ready"), 1)
                    turned(2, 0, e, w)
                    by_size(act, size_next, rows_of(2, e + 1))
                    turned(2, 1, e, w)
                    outputs_and_picks(2, e, w, 6 * e + (base_pd2 + 6))

                by_size(act, size, body)
            act.wait_ge(sem("moe2_added"), 1)
            rms(X, 1, "rms_ready", scr=XN[:, 0])

        @block.vector
        def _(dve):
            v = nc.vector
            cnt = {}

            def link(ins, name="dve_step"):
                cnt[name] = cnt.get(name, 0) + 1
                ins.then_inc(sem(name), 1)
                dve.wait_ge(sem(name), cnt[name])

            def flag(name):
                cnt[name] = cnt.get(name, 0) + 1
                dve.sem_inc(sem(name), 1)

            def products(name):
                dve.wait_ge(PD, done_value(name))

            def freed(ins, name):
                ins.then_inc(pair_free[steps[name] % 2], 1)
                dve.wait_ge(pair_free[steps[name] % 2], steps[name] // 2 + 1)

            n_rms = [0]

            def scale_rows(dst, nseg=1, width=D, src=None):
                n_rms[0] += 1
                dve.wait_ge(sem("rms_ready"), n_rms[0])
                link(v.reciprocal(ss_s[:, 0:NT * nseg], ss_s[:, 0:NT * nseg]))
                for t in range(NT):
                    for g in range(nseg):
                        link(v.tensor_scalar(dst[:, t, g * width:(g + 1) * width], src[:, t, g * width:(g + 1) * width],
                                             ss_s[:, t * nseg + g:t * nseg + g + 1], None, ALU.mult))

            def scaled_T(names, scale, shift, ready):
                for h in range(2):
                    products(names[h])
                    for k in range(4):
                        kk = 4 * h + k
                        src = pair(names[h])[:, 256 * k:256 * k + 256]
                        if shift is None:
                            ins = v.tensor_scalar(XT[:, kk], src, scale[:, kk:kk + 1], None, ALU.mult)
                        else:
                            ins = v.tensor_scalar(XT[:, kk], src, scale[:, kk:kk + 1], shift[:, kk:kk + 1], ALU.mult,
                                                  ALU.add)
                        if k < 3:
                            link(ins)
                    freed(ins, names[h])
                flag(ready)

            def bias_scores(c):
                kind, _, qt, hc, w = chunks[c]
                b = c % 2
                nk = 15 if kind == "cmp" else P * (qt + 1)
                dve.wait_ge(sem("scores_done"), c + 1)
                if c >= 2:
                    dve.wait_ge(sem("probs_transposed"), c - 1)
                if kind == "cmp":
                    for r in range(2):
                        ins = v.tensor_tensor(
                            out=SC[:, b].rearrange("p (j r) k -> p r j k", r=2)[:, r, :, 0:15],
                            in0=ps[b][:, 512 * r:512 * r + 512].rearrange("p (j k) -> p j k", j=2)[:, :, 0:15],
                            in1=CM[:, qt:qt + 1, :].broadcast_to([P, 2, 15]), op=ALU.add)
                    link(ins)
                else:
                    dm = DMW if kind == "swa" else DM
                    for h in range(4):
                        ins = v.scalar_tensor_tensor(out=SC[:, b, h, 0:nk], in0=dm[:, qt, 0:nk],
                                                     scalar=-map_slope(kind, 4 * hc + h),
                                                     in1=ps[b][:, score_col(h):score_col(h) + nk],
                                                     op0=ALU.mult, op1=ALU.add)
                    link(ins)
                red = v.tensor_reduce(out=nm_s[:, b], in_=SC[:, b, :, 0:nk], axis=AX.X, op=ALU.max, negate=True)
                if kind == "swa":
                    link(red)
                    link(v.tensor_tensor(out=nm_s[:, b], in0=nm_s[:, b], in1=nsnk[:, 4 * hc:4 * hc + 4], op=ALU.min))
                    link(v.tensor_tensor(out=es_s[:, b], in0=nm_s[:, b], in1=snk[:, 4 * hc:4 * hc + 4], op=ALU.add),
                         "scores_biased")
                else:
                    link(red, "scores_biased")

            def outputs(c):
                kind, _, qt, hc, w = chunks[c]
                b = c % 2
                dve.wait_ge(sem("outputs_done"), c + 1)
                if kind == "swa":
                    link(v.tensor_tensor(out=rs_s[:, b], in0=rs_s[:, b], in1=es_s[:, b], op=ALU.add))
                link(v.reciprocal(rv_s, rs_s[:, b]))
                if kind in ("cmp", "slc", "win"):
                    n = ("cmp", "slc", "win").index(kind)
                    gv = gts.rearrange("p t (h s) -> p t s h", s=3)[:, qt, n, 4 * hc:4 * hc + 4]
                    link(v.tensor_tensor(out=rv_s, in0=rv_s, in1=gv, op=ALU.mult))
                if kind == "cmp":
                    link(v.tensor_scalar(rv_s, rv_s, CV[:, qt, 0:1], None, ALU.mult))
                if kind == "diff":
                    neg = rv_s.rearrange("p (h c) -> p h c", c=2)[:, :, 1]
                    link(v.tensor_scalar(neg, neg, lam_s[:, 4:5], None, ALU.mult))
                src = ps[3][:, 512 * b:512 * b + 4 * w].rearrange("p (h n) -> p h n", h=4)
                rvb = rv_s.unsqueeze(2).broadcast_to([P, 4, w])
                if kind in ("moba", "swa", "cmp"):
                    dst = {"moba": O1, "swa": Oa, "cmp": Oc}[kind][:, qt, 256 * hc:256 * hc + 256]
                    link(v.tensor_tensor(out=dst.rearrange("p (h n) -> p h n", h=4), in0=src, in1=rvb, op=ALU.mult),
                         "outputs_scaled")
                else:
                    t4 = tmpO[:, 0:4 * w]
                    link(v.tensor_tensor(out=t4.rearrange("p (h n) -> p h n", h=4), in0=src, in1=rvb, op=ALU.mult))
                    if kind == "diff":
                        t2 = t4.rearrange("p (h c n) -> p h c n", h=2, c=2)
                        dst = Ob[:, qt, 256 * hc:256 * hc + 256].rearrange("p (h n) -> p h n", h=2)
                        link(v.tensor_tensor(out=dst, in0=t2[:, :, 0], in1=t2[:, :, 1], op=ALU.add), "outputs_scaled")
                    else:
                        dst = Oc[:, qt, 256 * hc:256 * hc + 256]
                        link(v.tensor_tensor(out=dst, in0=dst, in1=t4, op=ALU.add), "outputs_scaled")

            def attention(c0, c1):
                for c in range(c0, c1):
                    bias_scores(c)
                    if c > c0:
                        outputs(c - 1)
                outputs(c1 - 1)

            dve.wait_ge(sem("constants_ready"), 1)
            scale_rows(XN, src=X)
            flag("xn_ready")
            dve.wait_ge(pair_free[0], 1)
            scaled_T(("xt0", "xt1"), VT[:, 0:8], None, "xT_ready")

            def mod_added(n):
                i = mods_early[n]
                part, h = i // 2, i % 2
                c0 = 8 * (part if part < 2 else part - 1) + 4 * h
                products(f"md{i}")
                freed(v.tensor_tensor(out=modT[:, c0:c0 + 4], in0=pair(f"md{i}")[:, 0:4], in1=VT[:, 92 + c0:96 + c0],
                                      op=ALU.add), f"md{i}")

            def weighted_rows(j, acc, name):
                dve.wait_ge(slot_loaded[j % RING], uses_before(j))
                w = ring[:, (j % RING) * SLOT:(j % RING + 1) * SLOT].rearrange("p (k n) -> p k n", k=KD)
                link(v.tensor_scalar(acc, w[:, 0], VT2[:, 32:33], None, ALU.mult))
                for k in range(1, KD):
                    link(v.scalar_tensor_tensor(out=acc, in0=w[:, k], scalar=VT2[:, 32 + k:33 + k], in1=acc,
                                                op0=ALU.mult, op1=ALU.add), name if k == KD - 1 else "dve_step")

            def mod_sums(n):
                weighted_rows(item_at[f"mod{mods_early[n]}"], mod_sum[:, n % 2], "mod_summed")

            def mod_scale(c0, g0):
                link(v.scalar_tensor_tensor(out=modT[:, c0:c0 + 8], in0=modT[:, c0:c0 + 8], scalar=1.0,
                                            in1=VT[:, g0:g0 + 8], op0=ALU.add, op1=ALU.mult))

            for n in range(6):
                mod_sums(n)
                if n:
                    mod_added(n - 1)
            mod_added(5)
            mod_scale(8, 16)
            for h in range(3):
                dve.wait_ge(pair_free[steps[f"x{h}"] % 2], steps[f"x{h}"] // 2 + 1)
                for k in range(4):
                    for c in range(4 * h, 4 * h + 4):
                        tap = VT[:, 44 + 12 * k + c:45 + 12 * k + c]
                        if k == 0:
                            ins = v.tensor_scalar(cvT[:, c], xbcP[:, c, 0:T], tap, VT[:, 32 + c:33 + c], ALU.mult, ALU.add)
                        else:
                            ins = v.scalar_tensor_tensor(out=cvT[:, c], in0=xbcP[:, c, k:k + T], scalar=tap,
                                                         in1=cvT[:, c], op0=ALU.mult, op1=ALU.add)
                    link(ins)
            flag("conv_done")
            dve.wait_ge(sem("small_loaded"), 16 * n_small)
            dr, dabs, dtt, dA, ncs = [ssd_small[:, 32 * k:32 * k + 32] for k in range(5)]
            products("dt")
            freed(v.tensor_tensor(out=dr.rearrange("p (t h) -> p t h", t=2),
                                  in0=pair("dt").rearrange("p (t n) -> p t n", t=2)[:, :, 0:16],
                                  in1=dtb.unsqueeze(1).broadcast_to([P, 2, 16]), op=ALU.add), "dt")
            flag("dt_raw")
            dve.wait_ge(sem("dt_logs"), 1)
            link(v.scalar_tensor_tensor(out=dtt, in0=dr, scalar=0.0, in1=dabs, op0=ALU.max, op1=ALU.add))
            d3 = [x.rearrange("p (t h) -> p t h", t=2) for x in (dr, dtt, ncs)]
            link(v.scalar_tensor_tensor(out=d3[0], in0=d3[1], scalar=-1.0,
                                        in1=dA[:, 0:16].unsqueeze(1).broadcast_to([P, 2, 16]),
                                        op0=ALU.mult, op1=ALU.mult), "da_ready")
            link(v.tensor_scalar(nsnk, snk, -1.0, None, ALU.mult))
            attention(0, n_att1)
            products("G")
            freed(v.tensor_copy(GT, pair("G").rearrange("p (g s t) -> p g s t", g=2, s=2)), "G")
            for k in range(4):
                products(f"xsT{k}")
                freed(v.tensor_copy(xs[:, :, 256 * k:256 * k + 256],
                                    pair(f"xsT{k}")[:, 0:512].rearrange("p (t n) -> p t n", t=2)), f"xsT{k}")
            link(v.tensor_tensor(out=xdt.rearrange("p t (h n) -> p t h n", n=64),
                                 in0=xs.rearrange("p t (h n) -> p t h n", n=64),
                                 in1=d3[1].unsqueeze(3).broadcast_to([P, 2, 16, 64]), op=ALU.mult), "xdt_ready")
            products("cs")
            freed(v.tensor_scalar(ncs, pair("cs")[:, 0:32], -1.0, None, ALU.mult), "cs")
            def decay(g):
                b = g % 2
                products(f"cb{g}")
                if g >= 2:
                    dve.wait_ge(sem("ssd_heads_done"), g - 1)
                S4 = pair(f"cb{g}").rearrange("p (h t) -> p h t", h=4)
                for h in range(4):
                    hh = 4 * g + h
                    link(v.scalar_tensor_tensor(out=Mt[:, b, h, 0:256], in0=S4[:, h], scalar=ncs[:, hh:hh + 1],
                                                in1=MK[:, 0], op0=ALU.add, op1=ALU.add))
                    ins = v.scalar_tensor_tensor(out=Mt[:, b, h, 256:384], in0=S4[:, h, 128:256],
                                                 scalar=ncs[:, 16 + hh:17 + hh], in1=MK[:, 1, 128:256],
                                                 op0=ALU.add, op1=ALU.add)
                    if h < 3:
                        link(ins)
                freed(ins, f"cb{g}")
                flag("decay_biased")

            def times_g(g):
                b = g % 2
                gg = g // 2
                dve.wait_ge(sem("decay_exp"), g + 1)
                link(v.tensor_tensor(out=Mt[:, b, :, 0:256], in0=Mt[:, b, :, 0:256],
                                     in1=GT[:, gg, 0:1].broadcast_to([P, 4, 256]), op=ALU.mult))
                link(v.tensor_tensor(out=Mt[:, b, :, 256:384], in0=Mt[:, b, :, 256:384],
                                     in1=GT[:, gg, 1:2, 128:256].broadcast_to([P, 4, 128]), op=ALU.mult), "decay_ready")

            for g in range(4):
                decay(g)
                if g:
                    times_g(g - 1)
            times_g(3)
            dve.wait_ge(sem("ssd_heads_done"), 4)
            link(v.tensor_tensor(out=Y.rearrange("p t (h n) -> p t h n", n=64),
                                 in0=xs.rearrange("p t (h n) -> p t h n", n=64),
                                 in1=dsk.unsqueeze(1).unsqueeze(3).broadcast_to([P, 2, 16, 64]), op=ALU.mult))
            for t in range(2):
                link(v.tensor_tensor(out=Y[:, t], in0=Y[:, t], in1=ps[2 + t], op=ALU.add))
            link(v.tensor_tensor(out=Y, in0=Y, in1=silz, op=ALU.mult), "ssd_gated")
            products("ot1")
            freed(v.tensor_copy(OT, pair("ot1")), "ot1")

            def halves(dst, h):
                return dst[:, :, 512 * h:512 * h + 512]

            def two(name):
                return pair(name).rearrange("p (t n) -> p t n", t=2)

            for h in range(2):
                products(f"a{h}")
                products(f"ga{h}")
                dve.wait_ge(pair_free[steps[f"ga{h}"] % 2], steps[f"ga{h}"] // 2 + 1)
                freed(v.tensor_tensor(out=halves(MRG, h), in0=two(f"a{h}"), in1=sg, op=ALU.mult), f"a{h}")
                flag("merged")
            scale_rows(Y, nseg=2, width=512, src=Y)
            link(v.tensor_tensor(out=Y, in0=Y, in1=growA.unsqueeze(1).broadcast_to([P, 2, D]), op=ALU.mult), "y_ready")
            for h in range(2):
                products(f"yt{h}")
                freed(v.tensor_copy(AT[:, 4 * h:4 * h + 4], pair(f"yt{h}")), f"yt{h}")
            mod_sums(6)
            mod_sums(7)
            for h in range(2):
                products(f"b{h}")
                dve.wait_ge(pair_free[steps[f"gb{h}"] % 2], steps[f"gb{h}"] // 2 + 1)
                freed(v.tensor_tensor(out=sg, in0=two(f"b{h}"), in1=sg, op=ALU.mult), f"b{h}")
                link(v.tensor_tensor(out=halves(MRG, h), in0=halves(MRG, h), in1=sg, op=ALU.add), "merged")
                if h == 0:
                    mod_added(6)
                    mod_added(7)
                    mod_scale(24, 24)
            for h in range(2):
                products(f"wo{h}")
                freed(v.tensor_tensor(out=halves(X, h), in0=two(f"wo{h}"), in1=halves(X, h), op=ALU.add), f"wo{h}")
            flag("resid_ready")
            scale_rows(XN, src=X)
            flag("h2n_ready")
            scaled_T(("ht0", "ht1"), VT[:, 8:16], None, "h2_ready")

            def route_parts(t):
                o = 64 * t
                return rt_s[:, o:o + 8], rt_s[:, o + 12:o + 16], rt_s[:, o + 16:o + 32], rt_s[:, o + 32:o + 36]

            products("rt1")
            lg = rt_s[:, 128:168].rearrange("p (t n) -> p t n", t=2)
            freed(v.tensor_tensor(out=lg, in0=pair("rt1").rearrange("p (t n) -> p t n", t=2)[:, :, 0:20],
                                  in1=rb1.unsqueeze(1).broadcast_to([P, 2, 20]), op=ALU.add), "rt1")
            for t in range(2):
                e_, oh, ev, w_ = route_parts(t)
                link(v.tensor_copy(g8[:, 0:4], lg[:, t, 0:4]))
                link(v.max(out=m8, in_=g8))
                link(v.max_index(out=i8, in_max=m8, in_values=g8))
                link(v.tensor_copy(f8, i8))
                link(v.tensor_scalar(oh, io32[:, 0:4], f8[:, 0:1], None, ALU.is_equal))
                link(v.tensor_scalar(e_[:, 0:4], lg[:, t, 0:4], m8[:, 0:1], None, ALU.subtract))
                link(v.tensor_scalar(oh, oh, -1.0, BIG, ALU.add, ALU.mult))
                link(v.tensor_tensor(out=ev.rearrange("p (g e) -> p g e", g=4),
                                     in0=lg[:, t, 4:20].rearrange("p (g e) -> p g e", g=4),
                                     in1=oh.unsqueeze(2).broadcast_to([P, 4, 4]), op=ALU.add))
                link(v.max(out=m8, in_=ev))
                link(v.max_index(out=i8, in_max=m8, in_values=ev))
                link(v.tensor_copy(f8, i8))
                link(v.tensor_tensor(out=e_[:, 4:5], in0=m8[:, 1:2], in1=m8[:, 0:1], op=ALU.subtract))
                link(v.tensor_copy(w_[:, 0:2], f8[:, 0:2]))
            flag("route_exp")
            dve.wait_ge(sem("route_exped"), 2)
            for t in range(2):
                e_, oh, ev, w_ = route_parts(t)
                link(v.tensor_reduce(out=w_[:, 2:3], in_=e_[:, 0:4], axis=AX.X, op=ALU.add))
                link(v.tensor_scalar(w_[:, 3:4], e_[:, 4:5], 1.0, None, ALU.add))
                link(v.tensor_tensor(out=w_[:, 2:3], in0=w_[:, 2:3], in1=w_[:, 3:4], op=ALU.mult))
                link(v.reciprocal(w_[:, 2:3], w_[:, 2:3]))
                link(v.tensor_tensor(out=w_[:, 3:4], in0=w_[:, 2:3], in1=e_[:, 4:5], op=ALU.mult))
                link(v.tensor_scalar(comb[:, t, 0:16], io32[:, 0:16], w_[:, 0:1], w_[:, 2:3], ALU.is_equal, ALU.mult))
                link(v.tensor_scalar(ev, io32[:, 0:16], w_[:, 1:2], w_[:, 3:4], ALU.is_equal, ALU.mult))
                link(v.tensor_tensor(out=comb[:, t, 0:16], in0=comb[:, t, 0:16], in1=ev, op=ALU.add))


            def ranks(n, step_name):
                sel = rt_s[:, 0:64].rearrange("p (t e) -> p t e", t=NT)
                link(v.tensor_scalar(sel[:, :, 0:n], comb[:, :, 0:n], 0.0, None, ALU.is_gt))
                link(v.tensor_scalar(tri, DM, 0.5 * BIG, None, ALU.is_lt), "tri_ready")
                products(step_name)
                cum = pair(step_name)[:, 0:2 * n].rearrange("p (t e) -> p t e", t=NT)
                link(v.memset(rank[:, :, 32:33], -1.0))
                link(v.memset(rank[:, :, n:n + 1], -1.0))
                link(v.memset(comb0[:, :, 0:1], 0.0))
                big = rt_s[0:1, 64:64 + n]
                size = rt_s[0:1, 96:96 + n]
                link(v.tensor_scalar(big, cum[0:1, 0], float(P), None, ALU.is_gt))
                link(v.tensor_scalar(size, cum[0:1, 0], float(P // 2), None, ALU.is_gt))
                link(v.memset(sizes[0:1, :], 0))
                link(v.tensor_tensor(out=sizes[0:1, 1:n + 1], in0=big, in1=size, op=ALU.add))
                link(v.tensor_tensor(out=rank[:, :, 0:n], in0=cum, in1=sel[:, :, 0:n], op=ALU.mult))
                freed(v.tensor_scalar(rank[:, :, 0:n], rank[:, :, 0:n], -1.0, None, ALU.add), step_name)

            def picks(b, e, buf):
                for t in range(NT):
                    ins = v.tensor_scalar(pick[:, buf, t], iota, rank[:, t, bass.ds(e, 1)], None, ALU.is_equal)
                ins.then_inc(sem(f"picked{b}"), 1)

            def start_experts(b):
                link(v.memset(YS, 0.0))
                link(v.memset(pickT, 0.0))
                dve.sem_inc(sem(f"ys_ready{b}"), 1)
                dve.sem_inc(sem(f"pickT_ready{b}"), 1)
                picks(b, 0, 0)

            def add_outputs(b, e, dst):
                dve.wait_ge(sem(f"scattered{b}"), e + 1)
                for t in range(NT):
                    for h in range(2):
                        ins = v.scalar_tensor_tensor(out=dst[:, t, 512 * h:512 * h + 512],
                                                     in0=ps[2 + t][:, 512 * h:512 * h + 512],
                                                     scalar=comb0[:, t, bass.ds(e, 1)],
                                                     in1=dst[:, t, 512 * h:512 * h + 512], op0=ALU.mult, op1=ALU.add)
                ins.then_inc(sem(f"outputs_added{b}"), 1)
                dve.wait_ge(sem(f"outputs_added{b}"), e + 1)

            ranks(n1_exp, "rk1")
            start_experts(1)
            dve.sem_inc(sem("sg_free"), 1)
            with dve.Fori(0, n1_exp // 2) as i:
                for k in range(2):
                    e = 2 * i + k
                    dve.wait_ge(PD, 3 * e + (n_s1 + 1))
                    picks(1, e + 1, 1 - k)
                    dve.wait_ge(PD, 3 * e + (n_s1 + 2))
                    dve.wait_ge(gate_free, e + 1)

                    def body(w):
                        n = 4 * w
                        v.tensor_tensor(out=HID[:, 0, 0:n], in0=ps[1][:, 0:n], in1=SG[:, 0:n], op=ALU.mult)\
                            .then_inc(sem("hidden_ready1"), 1)

                    by_size(dve, size_of(dve, e), body)
                    dve.wait_ge(sem("hidden_ready1"), e + 1)
                    dve.sem_inc(sem("sg_free"), 1)
                    add_outputs(1, e, X)
            add_outputs(1, n1_exp, X)
            flag("moe1_added")
            for h in range(2):
                products(f"pp{h}")
                dve.wait_ge(pair_free[steps[f"pg{h}"] % 2], steps[f"pg{h}"] // 2 + 1)
                freed(v.tensor_tensor(out=sg, in0=two(f"pp{h}"), in1=sg, op=ALU.mult), f"pp{h}")
                link(v.tensor_tensor(out=halves(X, h), in0=halves(X, h), in1=sg, op=ALU.add), "ple_added")
                if h == 0:
                    for n in range(2):
                        weighted_rows(base_mid + after1[f"mod{4 + n}"], gate_sum[:, n], "gate_summed")
            dve.wait_ge(sem("p_loaded"), 16 * n_p)
            scale_rows(X, src=X)
            link(v.tensor_tensor(out=X, in0=X, in1=growB.unsqueeze(1).broadcast_to([P, 2, D]), op=ALU.mult), "x2_ready")
            scale_rows(XN, src=X)
            flag("xn2_ready")
            for i in mods_late:
                products(f"md{i}")
                part, h = i // 2, i % 2
                dst = G12[:, part // 3, 512 * h:512 * h + 512]
                freed(v.tensor_tensor(out=dst, in0=pair(f"md{i}")[:, 0:512], in1=dst, op=ALU.add), f"md{i}")
            scaled_T(("nt0", "nt1"), modT[:, 8:16], modT[:, 0:8], "xT2_ready")
            l4 = lamv.rearrange("p (a b d) -> p a b d", a=2, b=2)
            link(v.tensor_tensor(out=l4[:, :, 0], in0=l4[:, :, 0], in1=l4[:, :, 1], op=ALU.mult))
            link(v.tensor_reduce(out=lam_s[:, 0:2], in_=l4[:, :, 0], axis=AX.X, op=ALU.add), "lambda_sums")
            dve.wait_ge(pair_free[steps["kc"] % 2], steps["kc"] // 2 + 1)
            for j in range(2):
                for h in range(2):
                    for r in range(2):
                        src = kraw[64 * h:64 * h + 64, j]
                        pos = VT2[64 * r:64 * r + 64, 16 * j:16 * j + 16]
                        for half in range(2):
                            win = src[:, 16 * half:16 * half + 240].rearrange("p (c m r) -> p m c r", m=8, r=2)[:, :, :, r]
                            dst = kexp[64 * r:64 * r + 64, j, 8 * half:8 * half + 8, h, :]
                            link(v.tensor_copy(dst, win))
                            link(v.tensor_tensor(out=dst, in0=dst,
                                                 in1=pos[:, 8 * half:8 * half + 8].unsqueeze(2).broadcast_to([64, 8, 15]),
                                                 op=ALU.add))
            flag("windows_ready")
            products("cc")
            link(v.tensor_scalar(kcmp, pair("cc")[:, 0:30], cb2T, None, ALU.add))
            freed(v.tensor_tensor(out=vcmp[0:15, :, :], in0=pair("cc")[0:15, 512:640].rearrange("p (h n) -> p h n", h=2),
                                  in1=cb2[0:15, :].unsqueeze(1).broadcast_to([15, 2, 64]), op=ALU.add), "cc")
            dve.wait_ge(sem("lambda_exp"), 1)
            link(v.tensor_tensor(out=lam_s[:, 4:5], in0=lam_s[:, 1:2], in1=lam_s[:, 0:1], op=ALU.subtract))
            link(v.tensor_scalar(lam_s[:, 4:5], lam_s[:, 4:5], -0.2, None, ALU.add))
            attention(n_att1, len(chunks))
            o8 = Ob.rearrange("p t (h n) -> p (t h) n", n=P)
            sq = MRG.rearrange("p t n -> p (t n)")[:, 0:1024].rearrange("p (t n) -> p t n", n=P)
            link(v.tensor_tensor(out=sq, in0=o8, in1=o8, op=ALU.mult))
            link(v.tensor_reduce(out=ss_s[:, 0:8], in_=sq, axis=AX.X, op=ALU.add), "diff_squares")
            dve.wait_ge(sem("diff_rms"), 1)
            link(v.reciprocal(ss_s[:, 0:8], ss_s[:, 0:8]))
            link(v.tensor_scalar(ss_s[:, 0:8], ss_s[:, 0:8], 0.8, None, ALU.mult))
            link(v.tensor_tensor(out=o8, in0=o8, in1=ss_s[:, 0:8].unsqueeze(2).broadcast_to([P, 8, P]), op=ALU.mult))
            link(v.tensor_tensor(out=o8, in0=o8, in1=sub_g.unsqueeze(1).broadcast_to([P, 8, P]), op=ALU.mult),
                 "branches_ready")
            for b in range(3):
                products(f"bt{b}")
                freed(v.tensor_copy(hT3[b], pair(f"bt{b}")), f"bt{b}")
                for h in range(2):
                    products(f"y{b}{h}")
                    dve.wait_ge(pair_free[steps[f"g{b}{h}"] % 2], steps[f"g{b}{h}"] // 2 + 1)
                    if b == 0:
                        freed(v.tensor_tensor(out=halves(MRG, h), in0=two(f"y{b}{h}"), in1=sg2, op=ALU.mult), f"y{b}{h}")
                        flag("merged2")
                    else:
                        freed(v.tensor_tensor(out=sg2, in0=two(f"y{b}{h}"), in1=sg2, op=ALU.mult), f"y{b}{h}")
                        link(v.tensor_tensor(out=halves(MRG, h), in0=halves(MRG, h), in1=sg2, op=ALU.add), "merged2")
            for h in range(2):
                products(f"no{h}")
                g1 = G12[:, 0, 512 * h:512 * h + 512].unsqueeze(1).broadcast_to([P, 2, 512])
                freed(v.tensor_tensor(out=halves(MRG, h), in0=two(f"no{h}"), in1=g1, op=ALU.mult), f"no{h}")
                link(v.tensor_tensor(out=halves(X, h), in0=halves(X, h), in1=halves(MRG, h), op=ALU.add))
            flag("resid2_ready")
            scale_rows(XN, src=X)
            flag("h3n_ready")
            scaled_T(("h20", "h21"), modT[:, 24:32], modT[:, 16:24], "h3_ready")
            products("rt2")
            lg2 = rt_s[:, 128:192].rearrange("p (t n) -> p t n", t=2)
            freed(v.tensor_tensor(out=lg2, in0=pair("rt2").rearrange("p (t n) -> p t n", t=2)[:, :, 0:32],
                                  in1=rb2.unsqueeze(1).broadcast_to([P, 2, 32]), op=ALU.add), "rt2")
            for t in range(2):
                link(v.max(out=m8, in_=lg2[:, t]))
                link(v.max_index(out=i8, in_max=m8, in_values=lg2[:, t]))
                link(v.tensor_copy(f8, i8))
                link(v.tensor_scalar(w8[:, 4 * t:4 * t + 4], m8[:, 0:4], m8[:, 0:1], None, ALU.subtract), "route2_exp")
                dve.wait_ge(sem("route2_exped"), t + 1)
                link(v.reciprocal(rt_s[:, 224 + t:225 + t], rt_s[:, 224 + t:225 + t]))
                link(v.tensor_scalar(w8[:, 4 * t:4 * t + 4], w8[:, 4 * t:4 * t + 4], rt_s[:, 224 + t:225 + t], None, ALU.mult))
                for q in range(4):
                    dst = comb[:, t, :] if q == 0 else rt_s[:, 192:224]
                    link(v.tensor_scalar(dst, io32, f8[:, q:q + 1], w8[:, 4 * t + q:4 * t + q + 1], ALU.is_equal,
                                         ALU.mult))
                    if q:
                        link(v.tensor_tensor(out=comb[:, t, :], in0=comb[:, t, :], in1=dst, op=ALU.add))
            ranks(NE2, "rk2")
            products("ct")
            freed(v.tensor_copy(combT[0:32, :], pair("ct")[0:32, 0:256]), "ct")
            products("cb")
            for t in range(2):
                link(v.tensor_copy(ACC[:, t], ps[2 + t]))
            flag("acc_ready")
            dve.wait_ge(PD, done_value("cb"))
            dve.sem_inc(pair_free[steps["cb"] % 2], 1)

            start_experts(2)

            def hidden2(e, half, w):
                n = 2 * e + half
                pd = 6 * e + (base_pd2 + 2 * half + 1)
                c = slice(0, 4 * w)
                dve.wait_ge(PD, pd)
                v.tensor_scalar(GS[:, c], ps[0][:, c], 7.0, None, ALU.min).then_inc(sem("gate_limited"), 1)
                dve.wait_ge(PD, pd + 1)
                v.tensor_scalar(US[:, c], ps[1][:, c], 7.0, -7.0, ALU.min, ALU.max).then_inc(up_free, 1)
                dve.wait_ge(sem("gate_limited"), n + 1)
                dve.wait_ge(up_free, n + 1)
                v.scalar_tensor_tensor(out=US[:, c], in0=US[:, c], scalar=1.0, in1=GS[:, c], op0=ALU.add,
                                       op1=ALU.mult).then_inc(sem("up_times_gate"), 1)
                dve.wait_ge(sem("up_times_gate"), n + 1)
                dve.wait_ge(sem("sig_ready"), n + 1)
                v.tensor_tensor(out=HID[:, half, c], in0=US[:, c], in1=SG[:, c], op=ALU.mult)\
                    .then_inc(sem("hidden_ready2"), 1)

            with dve.Fori(0, NE2 // 2) as i:
                for k in range(2):
                    e = 2 * i + k
                    dve.wait_ge(PD, 6 * e + (base_pd2 + 1))
                    picks(2, e + 1, 1 - k)

                    def body(w):
                        hidden2(e, 0, w)
                        dve.wait_ge(sem("hidden_ready2"), 2 * e + 1)
                        add_outputs(2, e, ACC)
                        hidden2(e, 1, w)

                    by_size(dve, size_of(dve, e), body)
                    dve.wait_ge(sem("hidden_ready2"), 2 * e + 2)
            add_outputs(2, NE2, ACC)
            link(v.tensor_tensor(out=ACC, in0=ACC, in1=G12[:, 1].unsqueeze(1).broadcast_to([P, 2, D]), op=ALU.mult))
            link(v.tensor_tensor(out=X, in0=X, in1=ACC, op=ALU.add), "moe2_added")
            dve.wait_ge(sem("last_gain_loaded"), 16)
            scale_rows(X, src=X)
            for t in range(NT):
                link(v.tensor_tensor(out=X[:, t], in0=X[:, t], in1=growF, op=ALU.mult), "out_ready")

        @block.tensor
        def _(pe):
            mm = nc.tensor.matmul

            def begin(name):
                m = steps[name]
                if m >= 2:
                    pe.wait_ge(pair_free[m % 2], m // 2)
                return ps[m % 2]

            def slot(j, nk, n=None):
                pe.wait_ge(slot_loaded[j % RING], uses_before(j))
                n = n or SLOT // nk
                return ring[:, (j % RING) * SLOT:(j % RING) * SLOT + nk * n].rearrange("p (t n) -> p t n", t=nk)

            def all_free(name):
                for q in range(2):
                    pe.wait_ge(pair_free[q], (steps[name] - q) // 2 + 1)

            def lin_T(name, w, xT, nct, nk=KD, c0=0, bias=None):
                out = begin(name).rearrange("p (c t) -> p c t", t=T)
                for ct in range(nct):
                    for k in range(nk):
                        ins = mm(out[:, ct], w[:, k, c0 + P * ct:c0 + P * ct + P], xT[:, k], start=(k == 0),
                                 stop=(k == nk - 1 and bias is None))
                    if bias is not None:
                        r, bc = bias
                        ins = mm(out[:, ct], brow[r:r + 1, bc + P * ct:bc + P * ct + P], ones[r:r + 1, 0:T],
                                 start=False, stop=True)
                ins.then_inc(PD, 1)

            def lin_N(name, w, xT, n, nk=KD, c0=0, bias=None):
                out = begin(name).rearrange("p (t n) -> p t n", t=NT)
                for t in range(NT):
                    for k in range(nk):
                        ins = mm(out[:, t, 0:n], xT[:, k, P * t:P * t + P], w[:, k, c0:c0 + n], start=(k == 0),
                                 stop=(k == nk - 1 and bias is None))
                    if bias is not None:
                        r, bc = bias
                        ins = mm(out[:, t, 0:n], ones[r:r + 1, 0:P], brow[r:r + 1, bc:bc + n], start=False, stop=True)
                ins.then_inc(PD, 1)

            def transposes(name, src, k0, n=4):
                out = begin(name).rearrange("p (c t) -> p c t", t=T)
                for k in range(n):
                    for t in range(NT):
                        ins = nc.tensor.transpose(out[:, k, P * t:P * t + P], src[:, t, P * (k0 + k):P * (k0 + k) + P],
                                                  ident)
                ins.then_inc(PD, 1)

            def attention(c0, c1):
                def scores(c):
                    kind, _, qt, hc, w = chunks[c]
                    nk = 15 if kind == "cmp" else P * (qt + 1)
                    if c >= c0 + 2:
                        pe.wait_ge(sem("scores_biased"), c - 1)
                    for h in range(4):
                        q, k = map_operands(kind, 4 * hc + h)
                        ins = mm(ps[c % 2][:, score_col(h):score_col(h) + nk], q[:, P * qt:P * qt + P], k[:, 0:nk], start=True,
                                 stop=True)
                    ins.then_inc(sem("scores_done"), 1)

                scores(c0)
                for c in range(c0, c1):
                    if c + 1 < c1:
                        scores(c + 1)
                    kind, _, qt, hc, w = chunks[c]
                    cmp = kind == "cmp"
                    nt = 1 if cmp else qt + 1
                    rows = 15 if cmp else P
                    pe.wait_ge(sem("probs_ready"), c + 1)
                    if c:
                        pe.wait_ge(sem("probsT_ready"), c)
                    for m in range(4 * nt):
                        h, kt = m // nt, m % nt
                        ins = nc.tensor.transpose(ps[2][0:rows, P * m:P * m + P],
                                                  SC[:, c % 2, h, P * kt:P * kt + rows], ident)
                    ins.then_inc(sem("probs_transposed"), 1)
                    pe.wait_ge(sem("probsT_ready"), c + 1)
                    if c >= 2:
                        pe.wait_ge(sem("outputs_scaled"), c - 1)
                    for h in range(4):
                        for kt in range(nt):
                            ins = mm(ps[3][:, 512 * (c % 2) + w * h:512 * (c % 2) + w * h + w],
                                     PT[0:rows, c % 2, h * nt + kt], map_values(kind, 4 * hc + h, kt),
                                     start=(kt == 0), stop=(kt == nt - 1))
                    ins.then_inc(sem("outputs_done"), 1)

            pe.wait_ge(sem("constants_ready"), 1)
            pe.wait_ge(sem("vectors_loaded"), 16 * n_vec)
            vr = XT.rearrange("p k t -> p (k t)")
            begin("vec")
            nc.tensor.transpose(ps[0][:, 0:P], vr[:, 0:P], ident)
            nc.tensor.transpose(ps[0][:, P:P + 40], vr[0:40, P:2 * P], ident[0:40, 0:40]).then_inc(PD, 1)
            pe.wait_ge(sem("xn_ready"), 1)
            transposes("xt0", XN, 0)
            transposes("xt1", XN, 4)
            pe.wait_ge(sem("xT_ready"), 1)
            I = item_at

            def mod_T(n):
                o = begin(f"md{mods_early[n]}")
                pe.wait_ge(sem("mod_summed"), n + 1)
                for ct in range(4):
                    ins = mm(o[:, ct:ct + 1], mod_sum[:, n % 2, P * ct:P * ct + P], ones[:, 0:1], start=True, stop=True)
                ins.then_inc(PD, 1)

            lin_T("q", slot(I["q"], KD), XT, 4)
            lin_T("k", slot(I["k"], KD), XT, 4)
            mod_T(0)
            lin_N("v", slot(I["v"], KD), XT, 512)
            mod_T(1)
            for h in range(2):
                lin_N(f"z{h}", slot(I[f"z{h}"], KD), XT, 512)
                mod_T(2 + h)
            for h in range(3):
                lin_T(f"x{h}", slot(I[f"x{h}"], KD), XT, 4)
                if h < 2:
                    mod_T(4 + h)
            pe.wait_ge(sem("small_loaded"), 16 * n_small)
            lin_N("dt", wdt, XT, 16)
            all_free("dt")
            attention(0, n_att1)
            pe.wait_ge(sem("conv_ready"), 1)
            o = begin("G").rearrange("p (g s t) -> p g s t", g=2, s=2)
            for g in range(2):
                for s_ in range(2):
                    ins = mm(o[:, g, s_], cvT[:, 8 + g, P * s_:P * s_ + P], cvT[:, 10 + g], start=True, stop=True)
            ins.then_inc(PD, 1)
            for k in range(4):
                o = begin(f"xsT{k}")[:, 0:512].rearrange("p (t n) -> p t n", t=2)
                for t in range(2):
                    for c in range(2):
                        ins = nc.tensor.transpose(o[:, t, P * c:P * c + P], cvT[:, 2 * k + c, P * t:P * t + P], ident)
                ins.then_inc(PD, 1)
            pe.wait_ge(sem("da_ready"), 1)
            da = ssd_small[:, 0:32]
            o = begin("cs")
            mm(o[:, 0:16], U[:, 0, 0:P], da[:, 0:16], start=True, stop=True)
            mm(o[:, 16:32], U[:, 0, P:T], da[:, 0:16], start=True, stop=False)
            mm(o[:, 16:32], U[:, 1, P:T], da[:, 16:32], start=False, stop=True).then_inc(PD, 1)

            def cum_rows(g):
                o = begin(f"cb{g}")
                for h in range(4):
                    for kt in range(2):
                        col = 16 * kt + 4 * g + h
                        ins = mm(o[:, 256 * h:256 * h + 256], da[:, col:col + 1].broadcast_to([P, P]), U[:, kt],
                                 start=(kt == 0), stop=(kt == 1))
                ins.then_inc(PD, 1)

            def ssd_heads(g):
                pe.wait_ge(sem("decay_ready"), g + 1)
                for h in range(4):
                    hh = 4 * g + h
                    c = slice(64 * hh, 64 * hh + 64)
                    m = Mt[:, g % 2, h]
                    mm(ps[2][:, c], m[:, 0:P], xdt[:, 0, c], start=True, stop=True)
                    mm(ps[3][:, c], m[:, P:T], xdt[:, 0, c], start=True, stop=False)
                    ins = mm(ps[3][:, c], m[:, T:T + P], xdt[:, 1, c], start=False, stop=True)
                ins.then_inc(sem("ssd_heads_done"), 1)

            pe.wait_ge(sem("xdt_ready"), 1)
            pe.wait_ge(sem("outputs_scaled"), n_att1)
            for g in range(4):
                cum_rows(g)
                if g:
                    ssd_heads(g - 1)
            ssd_heads(3)
            transposes("ot1", O1, 0)
            pe.wait_ge(pair_free[steps["ot1"] % 2], steps["ot1"] // 2 + 1)
            for h in range(2):
                lin_N(f"a{h}", slot(I["woa"], 4), OT, 512, nk=4, c0=512 * h)
                lin_N(f"ga{h}", slot(I[f"ga{h}"], KD), XT, 512)
            pe.wait_ge(sem("y_ready"), 1)
            transposes("yt0", Y, 0)
            transposes("yt1", Y, 4)
            pe.wait_ge(pair_free[steps["yt0"] % 2], steps["yt0"] // 2 + 1)
            pe.wait_ge(pair_free[steps["yt1"] % 2], steps["yt1"] // 2 + 1)
            for h in range(2):
                lin_N(f"b{h}", slot(I[f"wob{h}"], KD), AT, 512)
                lin_N(f"gb{h}", slot(I[f"gb{h}"], KD), XT, 512)
                if h == 0:
                    mod_T(6)
                    mod_T(7)
            pe.wait_ge(sem("merged"), 4)
            for h in range(2):
                transposes(f"mt{h}", MRG, 4 * h)
            for h in range(2):
                pe.wait_ge(pair_free[steps[f"mt{h}"] % 2], steps[f"mt{h}"] // 2 + 1)
            for h in range(2):
                lin_N(f"wo{h}", slot(I[f"wo{h}"], KD), AT, 512)
            pe.wait_ge(sem("h2n_ready"), 1)
            transposes("ht0", XN, 0)
            transposes("ht1", XN, 4)
            pe.wait_ge(sem("h2_ready"), 1)
            lin_N("rt1", wr1, XT, 20)

            def rows_back(names):
                for t in range(NT):
                    o = begin(names[t])
                    for k in range(KD):
                        ins = nc.tensor.transpose(o[:, P * k:P * k + P], XT[:, k, P * t:P * t + P], ident)
                    ins.then_inc(PD, 1)

            def ranks(n, step_name, turn):
                pe.wait_ge(sem("tri_ready"), turn)
                sel = rt_s[:, 0:64].rearrange("p (t e) -> p t e", t=NT)
                o = begin(step_name)
                mm(o[:, 0:n], tri[:, 0, 0:P], sel[:, 0, 0:n], start=True, stop=False)
                mm(o[:, 0:n], tri[:, 1, 0:P], sel[:, 1, 0:n], start=False, stop=True)
                mm(o[:, n:2 * n], tri[:, 1, P:T], sel[:, 1, 0:n], start=True, stop=True).then_inc(PD, 1)

            rows_back(("hb0", "hb1"))
            ranks(n1_exp, "rk1", 1)
            all_free("rk1")

            def half_up(j, load_value, dst, w, bias=None):
                pe.wait_ge(slot_loaded[j % RING], load_value)
                w_ = ring[:, (j % RING) * SLOT:(j % RING + 1) * SLOT].rearrange("p (t n) -> p t n", t=KD)
                if w == H2:
                    parts = [(dst[H2 * h:H2 * h + H2, 0:256], lambda k: XG[:, k, 0:H2], 256 * h, 256, H2)
                             for h in range(2)]
                elif w == P:
                    parts = [(dst[:, 0:512], lambda k: XG[:, k], 0, 512, P)]
                else:
                    parts = [(dst[:, 512 * t:512 * t + 512], lambda k, t=t: XT[:, k, P * t:P * t + P], 0, 512, P)
                             for t in range(NT)]
                for k in range(KD):
                    for out, stat, c0, n, rows in parts:
                        ins = mm(out, stat(k), w_[:, k, c0:c0 + n], start=(k == 0),
                                 stop=(bias is None and k == KD - 1))
                if bias is not None:
                    q, buf = bias
                    for out, stat, c0, n, rows in parts:
                        ins = mm(out, ones[32 * q:32 * q + 1, 0:rows], b1q[32 * q:32 * q + 1, buf, c0:c0 + n],
                                 start=False, stop=True)
                ins.then_inc(PD, 1)

            def turn_hidden(b, half, w):
                o = ps[2 - b]
                src = HID[:, half]
                for c in range(4 * w // P):
                    ins = nc.tensor.transpose(o[:, P * c:P * c + P], src[:, P * c:P * c + P], ident)
                ins.then_inc(sem(f"hidden_turned{b}"), 1)

            def half_down(j, load_value, hT, w, first, last):
                pe.wait_ge(slot_loaded[j % RING], load_value)
                w_ = ring[:, (j % RING) * SLOT:(j % RING + 1) * SLOT].rearrange("p (t n) -> p t n", t=4)
                for f in range(4):
                    beg, end = first and f == 0, last and f == 3
                    for h in range(2):
                        cols = w_[:, f, 512 * h:512 * h + 512]
                        if w == H2:
                            at = P * (f % 2) + H2 * (f // 2)
                            ins = mm(ps[2][H2 * h:H2 * h + H2, 0:512], hT[:, at:at + H2], cols, start=beg, stop=end)
                        else:
                            for t in range(w // P):
                                ins = mm(ps[2 + t][:, 512 * h:512 * h + 512], hT[:, 512 * t + P * f:512 * t + P * f + P],
                                         cols, start=beg, stop=end)
                ins.then_inc(PD, 1)

            def gather(b, e, buf, size):
                pe.wait_ge(sem(f"picked{b}"), e + 1)

                def body(w):
                    if w == T:
                        pe.drain().then_inc(sem(f"gathered{b}"), 1)
                        return
                    for k in range(KD):
                        for t in range(NT):
                            ins = mm(ps[b - 1][:, P * k:P * k + w], HT[:, t, P * k:P * k + P], pick[:, buf, t, 0:w],
                                     start=(t == 0), stop=(t == NT - 1))
                    ins.then_inc(sem(f"gathered{b}"), 1)

                by_size(pe, size, body)

            def scatter(b, e, size):
                pe.wait_ge(sem(f"ys_ready{b}"), e + 1)

                def body(w):
                    if w == T:
                        pe.drain().then_inc(sem(f"scattered{b}"), 1)
                        return
                    for t in range(NT):
                        for h in range(2):
                            r = slice(H2 * h, H2 * h + H2) if w == H2 else slice(0, P)
                            y = YS[r, 0:512] if w == H2 else YS[:, 512 * h:512 * h + 512]
                            ins = mm(ps[2 + t][:, 512 * h:512 * h + 512], pickT[r, P * t:P * t + P], y, start=True,
                                     stop=True)
                    ins.then_inc(sem(f"scattered{b}"), 1)

                by_size(pe, size, body)

            def turn_picks(b, buf, w):
                for t in range(NT):
                    o = ps[1][:, P * t:P * t + P]
                    if w == H2:
                        for h in range(2):
                            ins = mm(o[H2 * h:H2 * h + H2, :], pick[:, buf, t, 0:H2], ident, start=True, stop=True)
                    else:
                        ins = nc.tensor.transpose(o, pick[:, buf, t], ident)
                ins.then_inc(sem(f"pick_turned{b}"), 1)

            def experts(b, j0, n):
                nh = b
                nk = 3 * nh
                hidden = sem(f"hidden_ready{b}")
                hiddenT = sem(f"hiddenT_ready{b}")

                def expert(i, par, w, size_before, size_next):
                    e = 2 * i + par
                    j = j0 + nk * par

                    def value(jj):
                        return 16 * (2 * nk // RING) * i + uses_before(jj)

                    if b == 2:
                        pe.wait_ge(sem(f"b1_loaded{par}"), 16 * i + 16)
                    for half in range(nh):
                        if half:
                            pe.wait_ge(sem("gate_limited"), 2 * e + 1)
                        else:
                            pe.wait_ge(sem(f"xg_ready{b}"), e + 1)
                        half_up(j, value(j), ps[0], w, (half, par) if b == 2 else None)
                        if half:
                            pe.wait_ge(up_free, 2 * e + 1)
                        else:
                            pe.wait_ge(sem(f"pickT_ready{b}"), e + 1)
                        half_up(j + 1, value(j + 1), ps[1], w, (2 + half, par) if b == 2 else None)
                        j += 2
                        if half == 0:
                            scatter(b, e, size_before)
                    if b == 1:
                        pe.wait_ge(hidden, e + 1)
                        turn_hidden(b, 0, w)
                        gather(b, e + 1, 1 - par, size_next)
                    else:
                        pe.wait_ge(hidden, 2 * e + 1)
                        pe.wait_ge(sem("gate_limited"), 2 * e + 2)
                        turn_hidden(b, 0, w)
                        pe.wait_ge(up_free, 2 * e + 2)
                        gather(b, e + 1, 1 - par, size_next)
                        pe.wait_ge(hidden, 2 * e + 2)
                        pe.wait_ge(hiddenT, 2 * e + 1)
                        turn_hidden(b, 1, w)
                    pe.wait_ge(sem(f"outputs_added{b}"), e + 1)
                    for half in range(nh):
                        pe.wait_ge(hiddenT, nh * e + (half + 1))
                        half_down(j, value(j), HIDT[:, half], w, half == 0, half == nh - 1)
                        j += 1
                    if b == 2:
                        pe.wait_ge(sem(f"xg_ready{b}"), e + 2)
                    turn_picks(b, par, w)

                gather(b, 0, 0, size_of(pe, 0))
                with pe.Fori(0, n // 2) as i:
                    for par in range(2):
                        e = 2 * i + par
                        size_before, size, size_next = size_of(pe, e - 1), size_of(pe, e), size_of(pe, e + 1)
                        by_size(pe, size, lambda w: expert(i, par, w, size_before, size_next))
                pe.wait_ge(sem(f"pickT_ready{b}"), n + 1)
                scatter(b, n, size_of(pe, n - 1))

            experts(1, n_front1, n1_exp)
            J = {k: base_mid + n for k, n in after1.items()}
            pe.wait_ge(sem("moe1_added"), 1)
            transposes("p0", X, 0)
            transposes("p1", X, 4)
            pe.wait_ge(sem("p_loaded"), 16 * n_p)
            transposes("ptr", pin, 0, n=2)
            for nm in ("p0", "p1", "ptr"):
                pe.wait_ge(pair_free[steps[nm] % 2], steps[nm] // 2 + 1)
            for h in range(2):
                lin_N(f"pg{h}", slot(J[f"pg{h}"], KD), XT, 512)
                lin_N(f"pp{h}", slot(J["pp"], 2, 1024), pT, 512, nk=2, c0=512 * h)
            for i in mods_late:
                if i < 6:
                    o = begin(f"md{i}")
                    pe.wait_ge(sem("gate_summed"), i - 3)
                    ins = mm(o[:, 0:512], ones[:, 0:P], gate_sum[:, i - 4], start=True, stop=True)
                else:
                    w = slot(J[f"mod{i}"], KD)
                    o = begin(f"md{i}")
                    for k in range(KD):
                        ins = mm(o[:, 0:512], VT2[:, 32 + k:33 + k].broadcast_to([P, P]), w[:, k], start=(k == 0),
                                 stop=(k == KD - 1))
                ins.then_inc(PD, 1)
            pe.wait_ge(sem("xn2_ready"), 1)
            transposes("nt0", XN, 0)
            transposes("nt1", XN, 4)
            pe.wait_ge(sem("xT2_ready"), 1)

            def seg(s_, off=0):
                return 32 * (s_ % 4), 512 * (s_ // 4) + off

            lin_T("qa", slot(J["qa"], KD), XT, 4, bias=seg(0))
            wk = slot(J["kva"], KD, 256)
            lin_T("ka", wk, XT, 1, bias=seg(1))
            lin_N("va", wk, XT, 128, c0=128, bias=seg(1, 128))
            lin_T("qb", slot(J["qb"], KD), XT, 4, bias=seg(2))
            lin_T("kb", slot(J["kb"], KD), XT, 4, bias=seg(3))
            lin_N("vb", slot(J["vb"], KD), XT, 512, bias=seg(4))
            lin_T("qc", slot(J["qc"], KD), XT, 4, bias=seg(5))
            wk = slot(J["kvc"], KD)
            lin_T("kc", wk, XT, 2, bias=seg(6))
            lin_T("ksl", wk, XT, 1, c0=256, bias=seg(6, 256))
            lin_N("vsl", wk, XT, 128, c0=384, bias=seg(6, 384))
            wk = slot(J["kvw"], KD, 256)
            lin_T("kwn", wk, XT, 1, bias=seg(7))
            lin_N("vwn", wk, XT, 128, c0=128, bias=seg(7, 128))
            lin_N("gn", wgn, XT, 24, bias=seg(8))
            pe.wait_ge(sem("windows_ready"), 1)
            for j in range(2):
                w = slot(J[f"cw{j}"], 16)
                o = begin(f"c{j}")
                for m in range(2):
                    for l in range(16):
                        ins = mm(o[:, 30 * m:30 * m + 30], w[:, l, P * m:P * m + P],
                                 kexp[:, j, l].rearrange("p h c -> p (h c)"), start=(l == 0), stop=(l == 15))
                ins.then_inc(PD, 1)
            for j in range(2):
                pe.wait_ge(pair_free[steps[f"c{j}"] % 2], steps[f"c{j}"] // 2 + 1)
            o = begin("cc")
            for half in range(2):
                for m in range(2):
                    mm(o[64 * half:64 * half + 64, 0:30], cw2[:, 0, m], hid[:, 0, m], start=(m == 0), stop=(m == 1))
            for h in range(2):
                for m in range(2):
                    ins = mm(o[0:15, 512 + 64 * h:576 + 64 * h], hid[:, 1, m, 15 * h:15 * h + 15], cw2[:, 1, m],
                             start=(m == 0), stop=(m == 1))
            ins.then_inc(PD, 1)
            all_free("cc")
            attention(n_att1, len(chunks))
            pe.wait_ge(sem("branches_ready"), 1)
            for b, o_ in enumerate((Oa, Ob, Oc)):
                transposes(f"bt{b}", o_, 0)
                pe.wait_ge(pair_free[steps[f"bt{b}"] % 2], steps[f"bt{b}"] // 2 + 1)
                for h in range(2):
                    lin_N(f"y{b}{h}", slot(J[f"wb{b}"], 4), hT3[b], 512, nk=4, c0=512 * h)
                    lin_N(f"g{b}{h}", slot(J[f"gm{b}{h}"], KD), XT, 512, bias=seg(9 + 2 * b + h))
            pe.wait_ge(sem("merged2"), 6)
            for h in range(2):
                transposes(f"nt{h + 2}", MRG, 4 * h)
            for h in range(2):
                pe.wait_ge(pair_free[steps[f"nt{h + 2}"] % 2], steps[f"nt{h + 2}"] // 2 + 1)
            for h in range(2):
                lin_N(f"no{h}", slot(J[f"w2o{h}"], KD), AT, 512)
            pe.wait_ge(sem("h3n_ready"), 1)
            transposes("h20", XN, 0)
            transposes("h21", XN, 4)
            pe.wait_ge(sem("h3_ready"), 1)
            lin_N("rt2", wr2, XT, 32)
            rows_back(("hb2", "hb3"))
            ranks(NE2, "rk2", 2)
            o = begin("ct")
            for t in range(2):
                ins = nc.tensor.transpose(o[0:32, P * t:P * t + P], comb[:, t], ident)
            ins.then_inc(PD, 1)
            pe.wait_ge(pair_free[steps["ct"] % 2], steps["ct"] // 2 + 1)
            pe.wait_ge(sem("b2_loaded"), 16)
            begin("cb")
            for t in range(2):
                for h in range(2):
                    ins = mm(ps[2 + t][:, 512 * h:512 * h + 512], combT[0:32, P * t:P * t + P],
                             b2R[0:32, 512 * h:512 * h + 512], start=True, stop=True)
            ins.then_inc(PD, 1)
            pe.wait_ge(sem("acc_ready"), 1)
            all_free("cb")
            experts(2, base_exp2, NE2)


_OUT = (1, T, D)
_INPUTS = ["x", "p", "mix_norm_g", "w_in", "conv_w", "conv_b", "dt_bias", "a_log", "d_skip", "ssd_norm_g", "w_out_a",
           "w_out_b", "w_out", "ffn_norm_g", "w_rg", "b_rg", "w_re", "b_re", "w_gate", "w_up", "w_down", "w_ple_proj",
           "w_ple_gate", "final_norm_g", "c_2", "mod_w_2", "mod_b_2", "norm1_g_2", "norm2_g_2", "w_in_2", "b_in_2",
           "sinks_2", "diff_lambda_2", "diff_subln_g_2", "cmp_pos_2", "cmp_w1_2", "cmp_b1_2", "cmp_w2_2", "cmp_b2_2",
           "w_branch_2", "w_out_2", "router_w_2", "router_b_2", "exp_w1_2", "exp_b1_2", "exp_w2_2", "exp_b2_2",
           "final_g_2"]


def kernel(**inputs):
    import concourse.bacc as bacc
    from concourse import mybir
    from concourse.bass_utils import run_bass_kernel_spmd

    nc = bacc.Bacc("TRN2", target_bir_lowering=False, num_devices=1)
    arrays, aps = {}, {}
    for name in _INPUTS:
        arr = np.ascontiguousarray(inputs[name])
        arrays[name] = arr
        aps[name] = nc.dram_tensor(name, arr.shape, mybir.dt.from_np(arr.dtype), kind="ExternalInput").ap()
    aps["out"] = nc.dram_tensor("out", _OUT, mybir.dt.float32, kind="ExternalOutput").ap()
    build(nc, aps)
    r = run_bass_kernel_spmd(nc, [arrays], core_ids=[0])
    return r.results[0]["out"]
```
